# Optimizing a Trainium2 kernel written in Bass

```python
import jax, jax.numpy as jnp
from jax import lax
import numpy as np

D_MODEL = 1024
BATCH = 1
SEQ = 256
DEPTH = 1

N_Q_HEADS = 16
N_KV_HEADS = 4
HEAD_DIM = 64
WINDOW = 128
ATTN_BLOCK = 128
ROPE_THETA = 10000.0
LRU_WIDTH = D_MODEL
LRU_BLOCKS = 8
LRU_BLOCK_W = LRU_WIDTH // LRU_BLOCKS
CONV_WIDTH = 4
LRU_C = 8.0
LRU_MIN_RAD = 0.9
LRU_MAX_RAD = 0.999
N_EXPERTS = 32
TOP_K = 4
D_FF = D_MODEL
SWIGLU_LIMIT = 7.0
SWIGLU_ALPHA = 1.702
MOE_BLOCK = 256
EPS = 1e-6

Q_W = N_Q_HEADS * HEAD_DIM
KV_W = N_KV_HEADS * HEAD_DIM
IN_W = Q_W + 2 * KV_W + 2 * LRU_WIDTH + 2 * D_MODEL

kernel_name = "hybrid_swa_rglru_moe_block"

def rms_norm(x, g):
    xf = x.astype(jnp.float32)
    xf = xf * lax.rsqrt(jnp.mean(xf * xf, axis=-1, keepdims=True) + EPS)
    return (xf * g.astype(jnp.float32)).astype(x.dtype)

def rope(t, positions):
    inv_freq = ROPE_THETA ** (-jnp.arange(0, HEAD_DIM, 2, dtype=jnp.float32) / HEAD_DIM)
    ang = positions.astype(jnp.float32)[..., None] * inv_freq
    cos = jnp.cos(ang)[:, :, None, :]
    sin = jnp.sin(ang)[:, :, None, :]
    tf = t.astype(jnp.float32)
    t1, t2 = jnp.split(tf, 2, axis=-1)
    return jnp.concatenate([t1 * cos - t2 * sin, t2 * cos + t1 * sin], axis=-1).astype(t.dtype)

def banded_sink_attention(q, k, v, sinks):
    B, S = q.shape[0], q.shape[1]
    nb = S // ATTN_BLOCK
    G = N_Q_HEADS // N_KV_HEADS
    qb = q.reshape(B, nb, ATTN_BLOCK, N_KV_HEADS, G, HEAD_DIM)

    def windows(t):
        tp = jnp.pad(t, ((0, 0), (ATTN_BLOCK, 0), (0, 0), (0, 0)))
        prev = tp[:, :S].reshape(B, nb, ATTN_BLOCK, N_KV_HEADS, HEAD_DIM)
        cur = t.reshape(B, nb, ATTN_BLOCK, N_KV_HEADS, HEAD_DIM)
        return jnp.concatenate([prev, cur], axis=2)

    kw, vw = windows(k), windows(v)
    s = jnp.einsum("bnqhgd,bnkhd->bnhgqk", qb, kw).astype(jnp.float32) * (HEAD_DIM ** -0.5)
    blk = jnp.arange(nb)[:, None, None] * ATTN_BLOCK
    qpos = blk + jnp.arange(ATTN_BLOCK)[None, :, None]
    kpos = blk - ATTN_BLOCK + jnp.arange(2 * ATTN_BLOCK)[None, None, :]
    rel = qpos - kpos
    valid = (rel >= 0) & (rel < WINDOW) & (kpos >= 0)
    s = jnp.where(valid[None, :, None, None, :, :], s, -jnp.inf)
    sink = sinks.astype(jnp.float32).reshape(1, 1, N_KV_HEADS, G, 1, 1)
    m = jnp.maximum(jnp.max(s, axis=-1, keepdims=True), sink)
    p = jnp.exp(s - m)
    denom = jnp.sum(p, axis=-1, keepdims=True) + jnp.exp(sink - m)
    o = jnp.einsum("bnhgqk,bnkhd->bnqhgd", (p / denom).astype(v.dtype), vw)
    return o.reshape(B, S, Q_W)

def causal_depthwise_conv(x, w, b):
    S = x.shape[1]
    xp = jnp.pad(x, ((0, 0), (CONV_WIDTH - 1, 0), (0, 0)))
    out = b
    for tap in range(CONV_WIDTH):
        out = out + xp[:, tap:tap + S] * w[tap]
    return out

def rg_lru(x, w_rg, b_rg, w_ig, b_ig, lru_a):
    B, S = x.shape[0], x.shape[1]
    xb = x.reshape(B, S, LRU_BLOCKS, LRU_BLOCK_W)
    r = jax.nn.sigmoid(jnp.einsum("bsnd,nde->bsne", xb, w_rg).reshape(B, S, LRU_WIDTH) + b_rg)
    i = jax.nn.sigmoid(jnp.einsum("bsnd,nde->bsne", xb, w_ig).reshape(B, S, LRU_WIDTH) + b_ig)
    log_a = -LRU_C * r.astype(jnp.float32) * jax.nn.softplus(lru_a.astype(jnp.float32))
    a = jnp.exp(log_a)
    mult = jnp.sqrt(-jnp.expm1(2.0 * log_a))
    u = mult * (i * x).astype(jnp.float32)

    def combine(left, right):
        a1, b1 = left
        a2, b2 = right
        return a1 * a2, a2 * b1 + b2

    _, h = lax.associative_scan(combine, (a, u), axis=1)
    return h.astype(x.dtype)

def hybrid_mixer(h, positions, w_in, b_in, sinks, conv_w, conv_b, w_rg, b_rg, w_ig, b_ig, lru_a, w_out, b_out):
    B, S = h.shape[0], h.shape[1]
    proj = h @ w_in + b_in
    o1 = Q_W
    o2 = o1 + KV_W
    o3 = o2 + KV_W
    o4 = o3 + LRU_WIDTH
    o5 = o4 + LRU_WIDTH
    o6 = o5 + D_MODEL
    q, k, v, lx, ly, ga, gl = jnp.split(proj, [o1, o2, o3, o4, o5, o6], axis=-1)
    q = rope(q.reshape(B, S, N_Q_HEADS, HEAD_DIM), positions)
    k = rope(k.reshape(B, S, N_KV_HEADS, HEAD_DIM), positions)
    v = v.reshape(B, S, N_KV_HEADS, HEAD_DIM)
    attn = banded_sink_attention(q, k, v, sinks)
    lx = causal_depthwise_conv(lx, conv_w, conv_b)
    lru = rg_lru(lx, w_rg, b_rg, w_ig, b_ig, lru_a) * jax.nn.gelu(ly, approximate=True)
    merged = jax.nn.sigmoid(ga) * attn + jax.nn.sigmoid(gl) * lru
    return merged @ w_out + b_out

def moe_ffn(h, w_router, b_router, w_e1, b_e1, w_e2, b_e2):
    T, D = h.shape
    logits = h.astype(jnp.float32) @ w_router.astype(jnp.float32) + b_router.astype(jnp.float32)
    top_v, top_i = lax.top_k(logits, TOP_K)
    top_w = jax.nn.softmax(top_v, axis=-1)
    N = T * TOP_K
    flat_e = top_i.reshape(-1)
    flat_w = top_w.reshape(-1)
    flat_tok = jnp.arange(N, dtype=jnp.int32) // TOP_K
    order = jnp.argsort(flat_e, stable=True)
    se = flat_e[order]
    counts = jnp.bincount(flat_e, length=N_EXPERTS)
    starts = jnp.cumsum(counts) - counts
    pcounts = (counts + MOE_BLOCK - 1) // MOE_BLOCK * MOE_BLOCK
    pends = jnp.cumsum(pcounts)
    pstarts = pends - pcounts
    dest = pstarts[se] + (jnp.arange(N) - starts[se])
    n_blocks = N // MOE_BLOCK + N_EXPERTS
    n_slots = n_blocks * MOE_BLOCK
    blk_expert = jnp.minimum(jnp.searchsorted(pends, jnp.arange(n_blocks) * MOE_BLOCK, side="right"), N_EXPERTS - 1)
    src_tok = jnp.full((n_slots,), T, jnp.int32).at[dest].set(flat_tok[order])
    slot_w = jnp.zeros((n_slots,), jnp.float32).at[dest].set(flat_w[order])
    h_pad = jnp.concatenate([h, jnp.zeros((1, D), h.dtype)], axis=0)

    def expert_block(args):
        idx, wts, e = args
        xb = h_pad[idx]
        gu = xb @ w_e1[e] + b_e1[e]
        g, u = jnp.split(gu, 2, axis=-1)
        g = jnp.minimum(g, SWIGLU_LIMIT)
        u = jnp.clip(u, -SWIGLU_LIMIT, SWIGLU_LIMIT)
        act = g * jax.nn.sigmoid(SWIGLU_ALPHA * g) * (u + 1.0)
        out = act @ w_e2[e] + b_e2[e]
        return out * wts.astype(out.dtype)[:, None]

    yp = lax.map(expert_block, (src_tok.reshape(n_blocks, MOE_BLOCK), slot_w.reshape(n_blocks, MOE_BLOCK), blk_expert))
    y = jnp.zeros((T + 1, D), yp.dtype).at[src_tok].add(yp.reshape(n_slots, D))
    return y[:T]

def setup_inputs(seed: int = 0) -> dict:
    key = jax.random.key(seed)
    ks = jax.random.split(key, 32)
    f32 = jnp.float32
    nrm = lambda k, shape, scale: jax.random.normal(k, shape, f32) * scale
    x = nrm(ks[0], (BATCH, SEQ, D_MODEL), 1.0)
    c = nrm(ks[1], (BATCH, D_MODEL), 1.0)
    offs = jax.random.randint(ks[2], (BATCH, 1), 0, SEQ, dtype=jnp.int32)
    positions = (jnp.arange(SEQ, dtype=jnp.int32)[None, :] + offs).astype(jnp.int32)
    u = jax.random.uniform(ks[3], (DEPTH, LRU_WIDTH), f32, LRU_MIN_RAD ** 2, LRU_MAX_RAD ** 2)
    lru_a = jnp.log(jnp.expm1(-0.5 * jnp.log(u)))
    return {
        "x": x,
        "c": c,
        "positions": positions,
        "w_ada": nrm(ks[4], (DEPTH, D_MODEL, 6 * D_MODEL), 0.5 * D_MODEL ** -0.5),
        "b_ada": nrm(ks[5], (DEPTH, 6 * D_MODEL), 0.01),
        "g_pre_mix": 1.0 + nrm(ks[6], (DEPTH, D_MODEL), 0.01),
        "g_post_mix": 1.0 + nrm(ks[7], (DEPTH, D_MODEL), 0.01),
        "w_in": nrm(ks[8], (DEPTH, D_MODEL, IN_W), D_MODEL ** -0.5),
        "b_in": nrm(ks[9], (DEPTH, IN_W), 0.01),
        "sinks": nrm(ks[10], (DEPTH, N_Q_HEADS), 0.5),
        "conv_w": nrm(ks[11], (DEPTH, CONV_WIDTH, LRU_WIDTH), CONV_WIDTH ** -0.5),
        "conv_b": nrm(ks[12], (DEPTH, LRU_WIDTH), 0.01),
        "w_rg": nrm(ks[13], (DEPTH, LRU_BLOCKS, LRU_BLOCK_W, LRU_BLOCK_W), LRU_BLOCK_W ** -0.5),
        "b_rg": nrm(ks[14], (DEPTH, LRU_WIDTH), 0.01),
        "w_ig": nrm(ks[15], (DEPTH, LRU_BLOCKS, LRU_BLOCK_W, LRU_BLOCK_W), LRU_BLOCK_W ** -0.5),
        "b_ig": nrm(ks[16], (DEPTH, LRU_WIDTH), 0.01),
        "lru_a": lru_a,
        "w_out": nrm(ks[17], (DEPTH, D_MODEL, D_MODEL), D_MODEL ** -0.5),
        "b_out": nrm(ks[18], (DEPTH, D_MODEL), 0.01),
        "g_pre_ffn": 1.0 + nrm(ks[19], (DEPTH, D_MODEL), 0.01),
        "g_post_ffn": 1.0 + nrm(ks[20], (DEPTH, D_MODEL), 0.01),
        "w_router": nrm(ks[21], (DEPTH, D_MODEL, N_EXPERTS), D_MODEL ** -0.5),
        "b_router": nrm(ks[22], (DEPTH, N_EXPERTS), 0.01),
        "w_e1": nrm(ks[23], (DEPTH, N_EXPERTS, D_MODEL, 2 * D_FF), D_MODEL ** -0.5),
        "b_e1": nrm(ks[24], (DEPTH, N_EXPERTS, 2 * D_FF), 0.01),
        "w_e2": nrm(ks[25], (DEPTH, N_EXPERTS, D_FF, D_MODEL), D_FF ** -0.5),
        "b_e2": nrm(ks[26], (DEPTH, N_EXPERTS, D_MODEL), 0.01),
    }

def reference(x, c, positions, w_ada, b_ada, g_pre_mix, g_post_mix, w_in, b_in, sinks, conv_w, conv_b,
              w_rg, b_rg, w_ig, b_ig, lru_a, w_out, b_out, g_pre_ffn, g_post_ffn, w_router, b_router,
              w_e1, b_e1, w_e2, b_e2):
    B, S, D = x.shape
    for l in range(DEPTH):
        mod = (jax.nn.silu(c) @ w_ada[l] + b_ada[l])[:, None, :]
        sh1, sc1, gt1, sh2, sc2, gt2 = jnp.split(mod, 6, axis=-1)
        h = rms_norm(x, g_pre_mix[l]) * (1.0 + sc1) + sh1
        y = hybrid_mixer(h, positions, w_in[l], b_in[l], sinks[l], conv_w[l], conv_b[l], w_rg[l], b_rg[l],
                         w_ig[l], b_ig[l], lru_a[l], w_out[l], b_out[l])
        x = x + gt1 * rms_norm(y, g_post_mix[l])
        h = rms_norm(x, g_pre_ffn[l]) * (1.0 + sc2) + sh2
        y = moe_ffn(h.reshape(B * S, D), w_router[l], b_router[l], w_e1[l], b_e1[l], w_e2[l], b_e2[l]).reshape(B, S, D)
        x = x + gt2 * rms_norm(y, g_post_ffn[l])
    return x


_drawn_inputs = setup_inputs


def setup_inputs(seed=0):
    import zlib

    import numpy as np

    out = dict(_drawn_inputs(seed))
    spreads = {}
    factors = {'g_pre_mix': 4.502,
     'g_post_mix': 6.891,
     'b_in': 3.548,
     'sinks': 8.0,
     'conv_b': 2.795,
     'b_rg': 8.0,
     'b_ig': 8.0,
     'b_out': 7.851,
     'g_pre_ffn': 3.276,
     'g_post_ffn': 62.499,
     'b_router': 3.177,
     'b_e1': 8.0,
     'b_e2': 62.021}
    for name, (base, spread) in spreads.items():
        noise = np.random.default_rng([zlib.crc32(name.encode()), seed]).standard_normal(out[name].shape)
        drawn = base * np.exp(spread * noise) if base else spread * noise
        out[name] = __import__('jax').numpy.asarray(drawn.astype(out[name].dtype))
    for name, factor in factors.items():
        out[name] = (out[name] * factor).astype(out[name].dtype)
    return out
```

```python
from contextlib import ExitStack

import numpy as np

import concourse.bass as bass
import concourse.mybir as mybir

F32 = mybir.dt.float32
BF16 = mybir.dt.bfloat16
I32 = mybir.dt.int32
U32 = mybir.dt.uint32
ALU = mybir.AluOpType
ACT = mybir.ActivationFunctionType
AX = mybir.AxisListType

P = 128
D = 1024
T = 256
TT = T // P
KT = D // P
HEADS, KV_HEADS, HEAD_DIM = 16, 4, 64
HALF = HEAD_DIM // 2
GROUP = HEADS // KV_HEADS
CONV = 4
EXPERTS, TOP_K = 32, 4
LIMIT, ALPHA = 7.0, 1.702
LRU_C = 8.0
EPS = 1e-6
ROPE_THETA = 10000.0
NEG = -1.0e30
GELU_A = 0.044715
GELU_B = 2.0 * float(np.sqrt(2.0 / np.pi))
BLOCK = 64
PASSES = T // BLOCK

Q0, K0, V0 = 0, HEADS * HEAD_DIM, HEADS * HEAD_DIM + KV_HEADS * HEAD_DIM
LX0 = V0 + KV_HEADS * HEAD_DIM
LY0, GA0, GL0 = LX0 + D, LX0 + 2 * D, LX0 + 3 * D

RING = 16
SLOT = 2048
PROJ_W = 256
N_ADA_A = KT
LX = [N_ADA_A + i for i in range(4)]
QC = [LX[-1] + 1 + i for i in range(4)]
KC = QC[-1] + 1
VC = KC + 1
GATES_A = VC + 1
LY_A = [GATES_A + 1, GATES_A + 2]
GATES_B = LY_A[-1] + 1
LY = [*LY_A, GATES_B + 1, GATES_B + 2]
GATES = (GATES_A, GATES_B)
GL = [LY[-1] + 1 + i for i in range(4)]
GA = [GL[-1] + 1 + i for i in range(4)]
ADA_B = [GA[-1] + 1 + i for i in range(2 * KT)]
WO = [ADA_B[-1] + 1 + i for i in range(4)]
MIXER_CHUNKS = WO[-1] + 1
E1_CHUNKS, E2_CHUNKS = KT, KT // 2
EXPERT_CHUNKS = E1_CHUNKS + E2_CHUNKS
UNROLL = 4
assert UNROLL * EXPERT_CHUNKS % RING == 0
TURNS = UNROLL * EXPERT_CHUNKS // RING
PROJ = [*LX, *QC, KC, VC, *LY, *GL, *GA]

R_C, R_GPRE, R_BADA, R_BIN, R_CONVW, R_CONVB, R_BRG, R_BIG, R_LRUA = 0, 8, 16, 32, 64, 96, 104, 112, 120


def layer(nc, a, out):
    with ExitStack() as ctx:
        def sb(name, shape, dt=F32):
            return ctx.enter_context(nc.sbuf_tensor(name, shape, dt))

        def sem(name):
            return ctx.enter_context(nc.semaphore(name))

        ps = ctx.enter_context(nc.psum_tensor("ps", [P, 8, 512], F32))

        ring = sb("ring", [P, RING, SLOT])
        ident = sb("ident", [P, P])
        ones = sb("ones", [P, P])
        before = sb("before", [P, P], BF16)
        ones_b = sb("ones_b", [P, P], BF16)
        mask = sb("mask", [P, 2, P])
        slot_no = sb("slot_no", [P, 2, BLOCK])
        expert_no = sb("expert_no", [P, EXPERTS])
        rows = sb("rows", [P, P])
        rows_qk = sb("rows_qk", [10, P])
        cols = sb("cols", [P, P])
        cols_qk = sb("cols_qk", [P, 10])
        freq = sb("freq", [P, 1])
        silu_c = sb("silu_c", [P, KT])
        mod_a = sb("mod_a", [P, 2 * KT])
        decay = sb("decay", [P, 2, KT])
        stats = sb("stats", [P, 16])
        sinks = sb("sinks", [P, HEADS])
        neg_sinks = sb("neg_sinks", [P, HEADS])
        smax = sb("smax", [P, GROUP, 2])
        ssum = sb("ssum", [P, GROUP, 2])
        snk = sb("snk", [P, GROUP, 2])
        b_v = sb("b_v", [P, KV_HEADS * HEAD_DIM])
        w_rt = sb("w_rt", [P, KT, EXPERTS])
        b_rt = sb("b_rt", [P, EXPERTS])
        plus1 = sb("plus1", [P, 1])
        eps = sb("eps", [P, 1])
        logits = sb("logits", [P, TT, EXPERTS])
        top8 = sb("top8", [P, TT, 8])
        top_i = sb("top_i", [P, TT, 8], U32)
        top_f = sb("top_f", [P, TT, 8])
        top_w = sb("top_w", [P, TT, 8])
        hit = sb("hit", [P, TT, EXPERTS])
        hit_b = sb("hit_b", [P, TT, EXPERTS], BF16)
        route_w = sb("route_w", [P, TT, EXPERTS])
        route_t = sb("route_t", [P, 2, EXPERTS])
        rank = sb("rank", [P, TT, EXPERTS])
        passes_f = sb("passes_f", [P, 4])
        more_i = sb("more_i", [P, 1], I32)

        z_h = sb("z_h", [P, 2048])
        z_attn = sb("z_attn", [P, KT * (T + CONV - 1)])
        z_lru = sb("z_lru", [P, 2048])
        z_gate = sb("z_gate", [P, 3072])
        z_q = sb("z_q", [P, 2048])
        z_k = sb("z_k", [P, 2048])
        z_p = sb("z_p", [P, GROUP * 3 * P])
        z_t = sb("z_t", [P, 1536])
        z_c = sb("z_c", [P, 1536])

        def v3(t, at, a_, b_):
            return t[:, at:at + a_ * b_].rearrange("p (a b) -> p a b", a=a_)

        def v4(t, at, a_, b_, c_):
            return t[:, at:at + a_ * b_ * c_].rearrange("p (a b c) -> p a b c", a=a_, b=b_)

        x_in = v3(z_attn, 0, TT, D)
        x_n = v3(z_gate, 0, TT, D)
        h_t = v3(z_h, 0, KT, T)
        lx = v3(z_attn, 0, KT, T + CONV - 1)
        xc = v3(z_lru, 0, KT, T)
        g_r, g_i, g_a = (v3(z_gate, 1024 * i, 4, T) for i in range(3))
        q_r = v3(z_q, 0, KT, T)
        k_rep = v3(z_k, 0, KV_HEADS, T)
        qk_raw = v4(z_t, 0, 2, 2, T)
        swap = v3(z_t, 1024, 2, T)
        k_r = v3(z_p, 0, 2, T)
        prob = v3(z_p, 0, GROUP, 3 * P)
        cos_t, sin_t, tmp_a, tmp_b = (z_c[:, T * i:T * (i + 1)] for i in range(4))
        v_sb = v3(z_c, 1024, TT, KV_HEADS * HEAD_DIM)
        lru_tmp = v3(z_c, 0, 2, T)
        gate = v3(z_c, 512, 2, T)
        attn = v3(z_attn, 0, KT, T)
        ly = v3(z_t, 0, 2, T)
        ly2 = v3(z_t, 512, 2, T)
        sg = v3(z_t, 1024, 2, T)
        x1 = v3(z_gate, 0, TT, D)
        b_out = z_gate[:, 2048:3072]
        g1_bc, sh2_bc = z_q[:, 0:1024], z_q[:, 1024:2048]
        a2_bc, g2_bc = z_k[:, 0:1024], z_k[:, 1024:2048]
        mod_row = v3(z_p, 0, 2, 512)
        bada_row = v3(z_t, 0, 2, 512)
        gain_row = v3(z_q, 0, 2, 512)
        y_sb = v3(z_lru, 0, TT, D)
        h2 = v3(z_h, 0, TT, D)
        h2_t = v3(z_attn, 0, KT, T)
        b_e1 = z_lru[:, 0:2048]
        hsel = v3(z_attn, 0, KT, BLOCK)
        g_c, u_c, s_g = (z_attn[:, 512 * i:512 * (i + 1)] for i in (1, 2, 3))
        act_t = v4(z_q, 0, 4, 2, BLOCK)
        g_u = z_q[:, 512:1024]
        o_sb = z_q[:, 1024:1536]
        scat_t = v3(z_q, 1536, TT, P)
        scat = v4(z_q, 1792, TT, 2, BLOCK)
        b_e2 = z_p[0:EXPERTS, 0:1024]
        route_wt = z_p[0:EXPERTS, 1024:1280]
        pick = v3(z_t, 0, TT, BLOCK)
        bias_pick = z_t[0:EXPERTS, 256:256 + BLOCK]
        fin = v3(z_lru, 0, TT, D)
        junk = z_attn[:, 0:1024]

        landed = [sem(f"landed{i}") for i in range(RING)]
        chunk_used = sem("chunk_used")
        x_loaded, rows_loaded, small_loaded, x_again = sem("x_loaded"), sem("rows_loaded"), sem("small_loaded"), sem("x_again")
        late_loaded, moe_loaded, pad_set = sem("late_loaded"), sem("moe_loaded"), sem("pad_set")
        out_stored = sem("out_stored")
        pool_set, pool_step = sem("pool_set"), sem("pool_step")
        dve_step, act_step = sem("dve_step"), sem("act_step")
        eps_set = sem("eps_set")
        x_sq, xn_done, xn_t, rows_t, cols_done, c_sig, silu_done = (sem(n) for n in (
            "x_sq", "xn_done", "xn_t", "rows_t", "cols_done", "c_sig", "silu_done"))
        mod_done, h_dve, h_act = sem("mod_done"), sem("h_dve"), sem("h_act")
        proj_read, v_done = sem("proj_read"), sem("v_done")
        pos_f, angle_done, sin_done, rope_done = sem("pos_f"), sem("angle_done"), sem("sin_done"), sem("rope_done")
        swapped, times_sin, rope_q, k_rep_done = sem("swapped"), sem("times_sin"), sem("rope_q"), sem("k_rep_done")
        conv_done, gates_ps, gates_read = sem("conv_done"), sem("gates_ps"), sem("gates_read")
        decay_done, sp_done = sem("decay_done"), sem("sp_done")
        a_done, th_done, m2_done, mult_done, ix_done, u_done, state_done = (sem(n) for n in (
            "a_done", "th_done", "m2_done", "mult_done", "ix_done", "u_done", "state_done"))
        scores_ps, smax_done, exp_done, prob_done = sem("scores_ps"), sem("smax_done"), sem("exp_done"), sem("prob_done")
        prob_t_ps, prob_t_done, pv_ps, attn_done = sem("prob_t_ps"), sem("prob_t_done"), sem("pv_ps"), sem("attn_done")
        ly_in, gelu_done, z_done, zsig_done, lg_done = (sem(n) for n in ("ly_in", "gelu_done", "z_done", "zsig_done", "lg_done"))
        gate_in, gate_used, merged = sem("gate_in"), sem("gate_used"), sem("merged")
        late_set, mod_row_done, bc_ps, bc_done = sem("late_set"), sem("mod_row_done"), sem("bc_ps"), sem("bc_done")
        y_done, y_sq, x1_done, x1_sq, h2_done, h2_t_ps, h2_t_act, h2_t_dve = (sem(n) for n in (
            "y_done", "y_sq", "x1_done", "x1_sq", "h2_done", "h2_t_ps", "h2_t_act", "h2_t_dve"))
        logits_ps, top_done, topexp_done, route_done, rank_ps, rank_done = (sem(n) for n in (
            "logits_ps", "top_done", "topexp_done", "route_done", "rank_ps", "rank_done"))
        route_t_ps, route_t_done = sem("route_t_ps"), sem("route_t_done")
        picked, gathered, hsel_done = sem("picked"), sem("gathered"), sem("hsel_done")
        g_done, sig_done, act_done = sem("g_done"), sem("sig_done"), sem("act_done")
        act_t_ps, act_t_a, act_t_d, scat_t_done = sem("act_t_ps"), sem("act_t_a"), sem("act_t_d"), sem("scat_t_done")
        o_done, combined = sem("o_done"), sem("combined")
        y2_sq, fin_done = sem("y2_sq"), sem("fin_done")

        def loads(n):
            return n // RING + 1 + sum(g <= n and g % RING == n % RING for g in GATES)

        def wait_chunk(eng, n):
            eng.wait_ge(landed[n % RING], 16 * loads(n))

        def wait_expert_chunk(eng, r, m, turn):
            n = MIXER_CHUNKS + r * EXPERT_CHUNKS + m
            eng.wait_ge(landed[n % RING], turn * (16 * TURNS) + 16 * loads(n))

        def expert_slot(r, m):
            return (MIXER_CHUNKS + r * EXPERT_CHUNKS + m) % RING

        def all_experts(eng, body, pool=None):
            groups = EXPERTS // UNROLL
            with eng.Fori(0, groups) as q:
                body(q, q, None)
            eng.wait_ge(rank_done, 1)
            more = eng.value_load(more_i[0:1, 0:1], min_val=0, max_val=PASSES - 1)
            with eng.If(more > 0):
                with eng.Fori(0, more) as p:
                    if pool is not None:
                        pool(p)
                    with eng.Fori(0, groups) as q:
                        body(p * groups + q + groups, q, p)
            return more

        block = ctx.enter_context(nc.Block())

        @block.sync
        def _(sp):
            def load(n, dst, src):
                if n >= RING:
                    sp.wait_ge(chunk_used, n - RING + 1)
                sp.dma_start(dst, src).then_inc(landed[n % RING], 16)

            w_ada = a["w_ada"][0].rearrange("(k p) n -> k p n", p=P)
            for k in range(KT):
                load(k, ring[:, k % RING, :], w_ada[k, :, 0:2 * D])
            w_in = a["w_in"][0].rearrange("(k p) n -> p k n", p=P)
            starts = {**{n: LX0 + PROJ_W * i for i, n in enumerate(LX)},
                      **{n: Q0 + PROJ_W * i for i, n in enumerate(QC)}, KC: K0, VC: V0,
                      **{n: LY0 + PROJ_W * i for i, n in enumerate(LY)},
                      **{n: GA0 + PROJ_W * i for i, n in enumerate(GA)},
                      **{n: GL0 + PROJ_W * i for i, n in enumerate(GL)}}
            for n in range(LX[0], GA[-1] + 1):
                slot = ring[:, n % RING, :]
                if n in GATES:
                    half = GATES.index(n)
                    w = slot[:, 0:1024].rearrange("p (g n e) -> p g n e", g=2, n=4)
                    load(n, w[:, 0], a["w_rg"][0, 4 * half:4 * half + 4].rearrange("n d e -> d n e"))
                    load(n, w[:, 1], a["w_ig"][0, 4 * half:4 * half + 4].rearrange("n d e -> d n e"))
                else:
                    c = starts[n]
                    load(n, slot.rearrange("p (k n) -> p k n", k=KT), w_in[:, :, c:c + PROJ_W])
            for i, n in enumerate(ADA_B):
                half, k = divmod(i, KT)
                load(n, ring[:, n % RING, :], w_ada[k, :, 2 * D * (1 + half):2 * D * (2 + half)])
            w_out = a["w_out"][0].rearrange("(c k p) n -> c p k n", k=2, p=P)
            for i, n in enumerate(WO):
                load(n, ring[:, n % RING, :].rearrange("p (k n) -> p k n", k=2), w_out[i])

            w_e1 = a["w_e1"][0].rearrange("e (k p) n -> e k p n", p=P)
            w_e2 = a["w_e2"][0].rearrange("e (c k p) n -> e c p k n", k=2, p=P)

            def experts(turn, q, p):
                for r in range(UNROLL):
                    for m in range(EXPERT_CHUNKS):
                        n = MIXER_CHUNKS + r * EXPERT_CHUNKS + m
                        sp.wait_ge(chunk_used, turn * (UNROLL * EXPERT_CHUNKS) + (n - RING + 1))
                        slot = ring[:, n % RING, :]
                        if m < E1_CHUNKS:
                            src = w_e1[bass.ds(q * UNROLL + r, 1), m].rearrange("e p n -> (e p) n")
                        else:
                            slot = slot.rearrange("p (k n) -> p k n", k=2)
                            src = w_e2[bass.ds(q * UNROLL + r, 1), m - E1_CHUNKS].rearrange("e p k n -> (e p) k n")
                        sp.dma_start(slot, src).then_inc(landed[n % RING], 16)

            all_experts(sp, experts)

        @block.tensor
        def _(pe):
            pe.wait_ge(pool_set, 4)
            pe.wait_ge(rows_loaded, 16 * 11)
            pe.transpose(ps[:, 1, 0:P], rows[:, :], ident[:, :])
            pe.transpose(ps[:, 1, P:P + 10], rows_qk[:, :], ident[0:10, 0:10]).then_inc(rows_t, 1)

            pe.wait_ge(silu_done, 1)
            for k in range(N_ADA_A):
                wait_chunk(pe, k)
                for n in range(2 * KT):
                    mm = pe.matmul(ps[:, 0, n:n + 1], ring[:, k % RING, n * P:(n + 1) * P], silu_c[:, k:k + 1],
                                   start=(k == 0 and n == 0), stop=(k == KT - 1), skip_group_check=True)
                mm.then_inc(chunk_used, 1)
                if k in (1, 3):
                    t = k // 2
                    pe.wait_ge(xn_done, t + 1)
                    for f in range(KT):
                        mm = pe.transpose(ps[:, 4 + f // 2, (f % 2) * T + t * P:(f % 2) * T + (t + 1) * P],
                                          x_n[:, t, f * P:(f + 1) * P], ident[:, :])
                    mm.then_inc(xn_t, 1)

            def proj_bank_free(j):
                if j == 0:
                    pe.wait_ge(mod_done, 1)
                elif j == 1:
                    pe.wait_ge(cols_done, 2)
                elif PROJ[j - 2] == VC:
                    pe.wait_ge(v_done, 1)
                elif PROJ[j - 2] in LY:
                    pe.wait_ge(ly_in, 2 * LY.index(PROJ[j - 2]) + 2)
                elif PROJ[j - 2] in GL + GA:
                    pe.wait_ge(gate_in, 2 * (GL + GA).index(PROJ[j - 2]) + 2)
                else:
                    pe.wait_ge(proj_read, j - 1)

            def project_tile(j, i):
                n = PROJ[j]
                w = ring[:, n % RING, :].rearrange("p (k n) -> p k n", k=KT)
                dst = ps[:, j % 2, i * T:(i + 1) * T]
                if i == 0:
                    proj_bank_free(j)
                    wait_chunk(pe, n)
                for k in range(KT):
                    if j == 0 and i == 0:
                        pe.wait_ge(h_dve if k < KT // 2 else h_act, k % (KT // 2) + 1)
                    if n == VC:
                        mm = pe.matmul(dst, h_t[:, k, i * P:(i + 1) * P], w[:, k, :], start=(k == 0), stop=(k == KT - 1))
                    else:
                        mm = pe.matmul(dst, w[:, k, i * P:(i + 1) * P], h_t[:, k, :], start=(k == 0), stop=(k == KT - 1))
                if i == 1:
                    mm.then_inc(chunk_used, 1)

            def gates(half):
                wait_chunk(pe, GATES[half])
                w = ring[:, GATES[half] % RING, 0:1024].rearrange("p (g n e) -> p g n e", g=2, n=4)
                for n in range(4 * half, 4 * half + 4):
                    pe.wait_ge(conv_done, n + 1)
                    if n >= 2:
                        pe.wait_ge(gates_read, n - 1)
                    for g in range(2):
                        mm = pe.matmul(ps[:, 2 + n % 2, g * T:(g + 1) * T], w[:, g, n % 4, :], xc[:, n, :],
                                       start=True, stop=True)
                    if n % 4 == 3:
                        mm.then_inc(chunk_used, 1)
                    else:
                        mm.then_inc(gates_ps, 1)

            for j in range(len(LX) + len(QC) + 2):
                project_tile(j, 0)
                project_tile(j, 1)
            gates(0)
            def scores(g):
                pe.wait_ge(rope_q, 5)
                pe.wait_ge(k_rep_done, 1)
                if g:
                    pe.wait_ge(prob_t_done, GROUP * g)
                for blk in range(2):
                    for h in range(GROUP):
                        half = slice(h % 2 * HEAD_DIM, (h % 2 + 1) * HEAD_DIM)
                        dst = ps[:, 4 + h, 0:P] if blk == 0 else ps[:, 4 + h, P:3 * P]
                        mm = pe.matmul(dst, q_r[half, 2 * g + h // 2, blk * P:(blk + 1) * P],
                                       k_rep[half, g, 0:(blk + 1) * P], start=True, stop=True,
                                       tile_position=(h % 2 * HEAD_DIM, 0))
                mm.then_inc(scores_ps, 1)

            def transposes(g):
                for h in range(GROUP):
                    pe.wait_ge(prob_done, GROUP * g + h + 1)
                    for b in range(3):
                        mm = pe.transpose(ps[:, 4 + h, b * P:(b + 1) * P], prob[:, h, b * P:(b + 1) * P], ident[:, :])
                    mm.then_inc(prob_t_ps, 1)

            def weighted_values(g):
                for h in range(GROUP):
                    tile_no = 2 * g + h // 2
                    pe.wait_ge(prob_t_done, GROUP * g + h + 1)
                    if h == 0:
                        pe.wait_ge(v_done, 1)
                        if g == 0:
                            pe.wait_ge(gates_read, KT)
                        else:
                            pe.wait_ge(attn_done, 2 * g)
                    at = (h % 2) * HEAD_DIM
                    v = v_sb[:, :, g * HEAD_DIM:(g + 1) * HEAD_DIM]
                    dst = ps[at:at + HEAD_DIM, 2 + tile_no % 2, :]
                    pe.matmul(dst[:, 0:P], v[:, 0], prob[:, h, 0:P], start=True, stop=True)
                    pe.matmul(dst[:, P:2 * P], v[:, 0], prob[:, h, P:2 * P], start=True, stop=False)
                    mm = pe.matmul(dst[:, P:2 * P], v[:, 1], prob[:, h, 2 * P:3 * P], start=False, stop=True)
                    mm.then_inc(pv_ps, 1)

            for u in range(len(LY) + len(GL) + len(GA)):
                if u == 2:
                    gates(1)
                if u % 2 and 3 <= u <= 9:
                    weighted_values((u - 3) // 2)
                if u % 2 and u <= 7:
                    scores((u - 1) // 2)
                project_tile(10 + u, 0)
                if u % 2 == 0 and 2 <= u <= 8:
                    transposes((u - 2) // 2)
                project_tile(10 + u, 1)

            for i, n in enumerate(ADA_B):
                half, k = divmod(i, KT)
                wait_chunk(pe, n)
                if i == 0:
                    pe.wait_ge(prob_t_done, HEADS)
                for c in range(4):
                    mm = pe.matmul(ps[32 * c:32 * (c + 1), 4 + half, :], silu_c[:, k:k + 1].broadcast_to([P, 32]),
                                   ring[:, n % RING, 512 * c:512 * (c + 1)], start=(k == 0), stop=(k == KT - 1),
                                   tile_position=(0, 32 * c))
                mm.then_inc(chunk_used, 1)

            pe.wait_ge(gate_in, 2 * KT)
            pe.wait_ge(attn_done, KT)
            for i, n in enumerate(WO):
                wait_chunk(pe, n)
                w = ring[:, n % RING, :].rearrange("p (k n) -> p k n", k=2)
                for k in (2 * i, 2 * i + 1):
                    pe.wait_ge(merged, k + 1)
                    for t in range(TT):
                        for c in range(2):
                            mm = pe.matmul(ps[:, 2 * t + c, :], attn[:, k, t * P:(t + 1) * P],
                                           w[:, k % 2, 512 * c:512 * (c + 1)], start=(k == 0), stop=(k == KT - 1))
                mm.then_inc(chunk_used, 1)
                pe.wait_ge(mod_row_done, 1)
                for b in (2 * i, 2 * i + 1):
                    half, quad = divmod(b, 4)
                    if b >= 2:
                        pe.wait_ge(bc_done, b - 1)
                    pe.matmul(ps[:, 6 + b % 2, :], ones[32 * quad:32 * quad + 1, :],
                              mod_row[32 * quad:32 * quad + 1, half, :], start=True, stop=True,
                              tile_position=(32 * quad, 0)).then_inc(bc_ps, 1)

            for t in range(TT):
                pe.wait_ge(h2_done, t + 1)
                if t == 0:
                    pe.wait_ge(bc_done, 8)
                for f in range(KT):
                    mm = pe.transpose(ps[:, 4 + f // 2, (f % 2) * T + t * P:(f % 2) * T + (t + 1) * P],
                                      h2[:, t, f * P:(f + 1) * P], ident[:, :])
                mm.then_inc(h2_t_ps, 1)
            pe.wait_ge(h2_t_act, 2)
            pe.wait_ge(h2_t_dve, 2)
            pe.wait_ge(y_done, TT)
            for t in range(TT):
                for k in range(KT):
                    mm = pe.matmul(ps[:, t, 0:EXPERTS], h2_t[:, k, t * P:(t + 1) * P], w_rt[:, k, :],
                                   start=(k == 0), stop=(k == KT - 1))
                mm.then_inc(logits_ps, 1)
            pe.wait_ge(route_done, TT)
            pe.matmul(ps[:, 2, 0:EXPERTS], before[:, :], hit_b[:, 0, :], start=True, stop=True)
            pe.matmul(ps[:, 2, EXPERTS:2 * EXPERTS], ones_b[:, :], hit_b[:, 0, :], start=True, stop=False)
            pe.matmul(ps[:, 2, EXPERTS:2 * EXPERTS], before[:, :], hit_b[:, 1, :], start=False, stop=True)
            pe.matmul(ps[:, 2, 2 * EXPERTS:3 * EXPERTS], ones_b[:, :], hit_b[:, 0, :], start=True, stop=False)
            pe.matmul(ps[:, 2, 2 * EXPERTS:3 * EXPERTS], ones_b[:, :], hit_b[:, 1, :], start=False,
                      stop=True).then_inc(rank_ps, 1)
            for t in range(TT):
                mm = pe.transpose(ps[0:EXPERTS, 4, t * P:(t + 1) * P], route_w[:, t, :], ident[:, :])
            mm.then_inc(route_t_ps, 1)
            pe.wait_ge(route_t_done, 1)
            pe.wait_ge(rank_done, 1)
            pe.wait_ge(moe_loaded, 32)
            for t in range(TT):
                for c in range(2):
                    mm = pe.matmul(ps[:, 2 * t + c, :], route_wt[:, t * P:(t + 1) * P], b_e2[:, 512 * c:512 * (c + 1)],
                                   start=True, stop=False, skip_group_check=True)
            mm.then_inc(combined, 1)
            pe.wait_ge(combined, 1)

            def experts(turn, q, p):
                for r in range(UNROLL):
                    done = turn * UNROLL + r
                    pe.wait_ge(picked, done + 1)
                    for k in range(KT):
                        for t in range(TT):
                            mm = pe.matmul(ps[:, 7, k * BLOCK:(k + 1) * BLOCK], h2[:, t, k * P:(k + 1) * P], pick[:, t, :],
                                           start=(t == 0), stop=(t == TT - 1))
                    mm.then_inc(gathered, 1)
                    for b in range(2):
                        for c in range(2):
                            pe.matmul(ps[64 * c:64 * (c + 1), 4 + b, :], bias_pick[:, :],
                                      b_e1[0:EXPERTS, b * D + 512 * c:b * D + 512 * (c + 1)], start=True, stop=False,
                                      tile_position=(0, 64 * c))
                    for k in range(KT):
                        if k == 0:
                            pe.wait_ge(hsel_done, done + 1)
                        wait_expert_chunk(pe, r, k, turn)
                        w = ring[:, expert_slot(r, k), :]
                        for b in range(2):
                            for c in range(2):
                                mm = pe.matmul(ps[64 * c:64 * (c + 1), 4 + b, :], hsel[:, k, :],
                                               w[:, b * D + 512 * c:b * D + 512 * (c + 1)], start=False, stop=(k == KT - 1),
                                               tile_position=(0, 64 * c))
                        mm.then_inc(chunk_used, 1)
                    pe.wait_ge(act_done, done + 1)
                    for c in range(4):
                        mm = pe.transpose(ps[:, 6 + c // 2, c % 2 * P:(c % 2 + 1) * P], g_u[:, c * P:(c + 1) * P], ident[:, :])
                    mm.then_inc(act_t_ps, 1)
                    for t in range(TT):
                        mm = pe.transpose(ps[:, 4, t * P:(t + 1) * P], scat[:, t].rearrange("p a s -> p (a s)"), ident[:, :])
                    mm.then_inc(act_t_ps, 1)
                    pe.wait_ge(act_t_a, done + 1)
                    pe.wait_ge(act_t_d, done + 1)
                    for k in range(KT):
                        if k % 2 == 0:
                            wait_expert_chunk(pe, r, E1_CHUNKS + k // 2, turn)
                        w = ring[:, expert_slot(r, E1_CHUNKS + k // 2), :]
                        for c in range(2):
                            mm = pe.matmul(ps[64 * c:64 * (c + 1), 6, :], act_t[:, k % 4, k // 4, :],
                                           w[:, (k % 2) * D + 512 * c:(k % 2) * D + 512 * (c + 1)],
                                           start=(k == 0), stop=(k == KT - 1), tile_position=(0, 64 * c))
                        if k % 2:
                            mm.then_inc(chunk_used, 1)
                    pe.wait_ge(scat_t_done, done + 1)
                    pe.wait_ge(o_done, done + 1)
                    for t in range(TT):
                        for c in range(2):
                            mm = pe.matmul(ps[:, 2 * t + c, :], scat_t[64 * c:64 * (c + 1), t, :], o_sb[64 * c:64 * (c + 1), :],
                                           start=False, stop=False, skip_group_check=True, tile_position=(64 * c, 0))
                    mm.then_inc(combined, 1)

            all_experts(pe, experts)

        @block.vector
        def _(dve):
            steps = [0]

            def step(ins):
                ins.then_inc(dve_step, 1)
                steps[0] += 1
                return steps[0]

            def then(n=None):
                dve.wait_ge(dve_step, steps[0] if n is None else n)

            dve.memset(eps[:, :], EPS).then_inc(eps_set, 1)
            step(dve.memset(plus1[:, :], 0.0))
            then()
            dve.memset(plus1[0:64, :], 1.0)
            dve.wait_ge(x_sq, 1)
            step(dve.reciprocal(stats[:, 2:4], stats[:, 0:2]))
            then()
            for t in range(TT):
                dve.tensor_scalar(x_n[:, t, :], x_in[:, t, :], stats[:, 2 + t:3 + t], None, ALU.mult).then_inc(xn_done, 1)
            dve.wait_ge(rows_t, 1)
            dve.tensor_copy(cols_qk[:, :], ps[:, 1, P:P + 10]).then_inc(cols_done, 1)
            dve.tensor_copy(cols[:, :], ps[:, 1, 0:P]).then_inc(cols_done, 1)
            dve.wait_ge(cols_done, 2)
            dve.wait_ge(c_sig, 1)
            dve.tensor_tensor(silu_c[:, :], cols[:, R_C:R_C + KT], silu_c[:, :], ALU.mult).then_inc(silu_done, 1)
            ang, turns_, red = tmp_a, sin_t, cos_t
            dve.wait_ge(small_loaded, 16 * 5)
            step(dve.tensor_copy(ang, tmp_b.bitcast(I32)))
            step(dve.tensor_scalar(neg_sinks[:, :], sinks[:, :], -1.0, None, ALU.mult))
            then()
            step(dve.tensor_scalar(ang, ang, freq[:, 0:1], None, ALU.mult))
            then()
            step(dve.tensor_scalar(turns_, ang, 1.0 / (2.0 * np.pi), 12582912.0, ALU.mult, ALU.add))
            then()
            step(dve.tensor_scalar(turns_, turns_, 12582912.0, None, ALU.subtract))
            two_pi = 2.0 * np.pi
            hi = 6.28125
            mid = float(np.float32(np.round((two_pi - hi) * 2 ** 20) / 2 ** 20))
            lo = float(np.float32(two_pi - hi - mid))
            src = ang
            for part in (hi, mid, lo):
                then()
                step(dve.scalar_tensor_tensor(red, turns_, -part, src, ALU.mult, ALU.add))
                src = red
            then()
            dve.tensor_scalar(red, red, 3.1415925, -3.1415925, ALU.min, ALU.max).then_inc(angle_done, 1)
            dve.wait_ge(chunk_used, N_ADA_A)
            step(dve.tensor_tensor(mod_a[:, :], ps[:, 0, 0:2 * KT], cols[:, R_BADA:R_BADA + 2 * KT], ALU.add))
            then()
            dve.scalar_tensor_tensor(mod_a[:, KT:], mod_a[:, KT:], 1.0, cols[:, R_GPRE:R_GPRE + KT], ALU.add,
                                     ALU.mult).then_inc(mod_done, 1)
            dve.wait_ge(mod_done, 1)
            dve.wait_ge(xn_t, TT)
            for k in range(KT // 2):
                dve.tensor_scalar(h_t[:, k, :], ps[:, 4 + k // 2, (k % 2) * T:(k % 2 + 1) * T], mod_a[:, KT + k:KT + k + 1], mod_a[:, k:k + 1],
                                  ALU.mult, ALU.add).then_inc(h_dve, 1)
            dve.wait_ge(sin_done, 2)
            step(dve.tensor_tensor(tmp_a, tmp_a, tmp_a, ALU.mult))
            for quad in (0, 2):
                step(dve.tensor_scalar(sin_t[32 * quad:32 * (quad + 1), :], sin_t[32 * quad:32 * (quad + 1), :], -1.0, None,
                                       ALU.mult))
            then()
            dve.tensor_scalar(cos_t, tmp_a, -2.0, 1.0, ALU.mult, ALU.add).then_inc(rope_done, 1)

            dve.wait_ge(sp_done, 1)
            for i, f in enumerate((-LRU_C, LRU_C)):
                ins = dve.tensor_scalar(decay[:, i, :], stats[:, 4:12], f, None, ALU.mult)
            ins.then_inc(decay_done, 1)

            def conv(c):
                dve.wait_ge(proj_read, c + 1)
                for tap in range(CONV - 1, -1, -1):
                    if tap < CONV - 1:
                        then()
                    for n in (2 * c, 2 * c + 1):
                        w = cols[:, R_CONVW + KT * tap + n:R_CONVW + KT * tap + n + 1]
                        if tap == CONV - 1:
                            ins = dve.tensor_scalar(xc[:, n, :], lx[:, n, tap:tap + T], w,
                                                    cols[:, R_CONVB + n:R_CONVB + n + 1], ALU.mult, ALU.add)
                        else:
                            ins = dve.scalar_tensor_tensor(xc[:, n, :], lx[:, n, tap:tap + T], w, xc[:, n, :], ALU.mult, ALU.add)
                        if tap:
                            step(ins)
                        else:
                            ins.then_inc(conv_done, 1)

            def rope(c):
                raw = qk_raw[:, c % 2]
                dst = q_r[:, 2 * c:2 * c + 2, :] if c < 4 else k_r
                dve.wait_ge(proj_read, len(LX) + c + 1)
                dve.wait_ge(rope_done, 1)
                if c:
                    dve.wait_ge(rope_q, c)
                for quad in range(4):
                    other = quad ^ 1
                    ins = dve.tensor_copy(swap[32 * quad:32 * (quad + 1)], raw[32 * other:32 * (other + 1)])
                ins.then_inc(swapped, 1)
                step(dve.tensor_tensor(dst, raw, cos_t[:, None, :].broadcast_to([P, 2, T]), ALU.mult))
                dve.wait_ge(times_sin, c + 1)
                then()
                dve.tensor_tensor(dst, dst, swap, ALU.add).then_inc(rope_q, 1)

            for c in range(4):
                conv(c)
            for c in range(5):
                rope(c)
            dve.wait_ge(rope_q, 5)
            for g in range(KV_HEADS):
                for half in range(2):
                    ins = dve.tensor_copy(k_rep[64 * half:64 * (half + 1), g, :], k_r[64 * (g % 2):64 * (g % 2 + 1), g // 2, :])
            ins.then_inc(k_rep_done, 1)
            dve.wait_ge(chunk_used, VC + 1)
            dve.tensor_tensor(v_sb[:, :, :], ps[:, 1, :].rearrange("p (t n) -> p t n", t=TT),
                              b_v[:, None, :].broadcast_to([P, TT, PROJ_W]), ALU.add).then_inc(v_done, 1)

            def lru_squares(b):
                for n in range(4):
                    dve.wait_ge(th_done, 4 * b + n + 1)
                    step(dve.tensor_tensor(lru_tmp[:, n % 2, :], g_a[:, n, :], g_a[:, n, :], ALU.mult))
                    then()
                    dve.scalar_tensor_tensor(g_r[:, n, :], lru_tmp[:, n % 2, :], 1.0, g_r[:, n, :], ALU.add,
                                             ALU.mult).then_inc(m2_done, 1)

            def lru_states(b):
                for n in range(4):
                    dve.wait_ge(mult_done, b + 1)
                    dve.wait_ge(ix_done, 4 * b + n + 1)
                    dve.tensor_tensor(g_i[:, n, :], g_i[:, n, :], g_r[:, n, :], ALU.mult).then_inc(u_done, 1)
                for n in range(4):
                    dve.wait_ge(u_done, 4 * b + n + 1)
                    dve.tensor_tensor_scan(xc[:, 4 * b + n, :], g_a[:, n, :], g_i[:, n, :], 0.0, ALU.mult,
                                           ALU.add).then_inc(state_done, 1)

            def softmax_max(g):
                dve.wait_ge(scores_ps, g + 1)
                if g:
                    dve.wait_ge(pv_ps, GROUP * g)
                for h in range(GROUP):
                    dve.tensor_tensor_reduce(prob[:, h, 0:P], ps[:, 4 + h, 0:P], mask[:, 1, :], 1.0, NEG, ALU.add, ALU.max,
                                             smax[:, h, 0:1])
                    ins = dve.tensor_tensor_reduce(prob[:, h, P:3 * P], ps[:, 4 + h, P:3 * P],
                                                   mask[:, :, :].rearrange("p a b -> p (a b)"), 1.0, NEG,
                                                   ALU.add, ALU.max, smax[:, h, 1:2])
                step(ins)
                then()
                step(dve.tensor_scalar(smax[:, :, :], smax[:, :, :], -HEAD_DIM ** -0.5, None, ALU.mult))
                then()
                sink = sinks[:, GROUP * g:GROUP * (g + 1), None].broadcast_to([P, GROUP, 2])
                nsink = neg_sinks[:, GROUP * g:GROUP * (g + 1), None].broadcast_to([P, GROUP, 2])
                step(dve.tensor_tensor(smax[:, :, :], smax[:, :, :], nsink, ALU.min))
                then()
                dve.tensor_tensor(snk[:, :, :], smax[:, :, :], sink, ALU.add).then_inc(smax_done, 1)

            def softmax_scale(g):
                dve.wait_ge(exp_done, g + 1)
                step(dve.tensor_tensor(ssum[:, :, :], ssum[:, :, :], snk[:, :, :], ALU.add))
                then()
                step(dve.reciprocal(ssum[:, :, :], ssum[:, :, :]))
                then()
                for h in range(GROUP):
                    dve.tensor_scalar(prob[:, h, 0:P], prob[:, h, 0:P], ssum[:, h, 0:1], None, ALU.mult)
                    dve.tensor_scalar(prob[:, h, P:3 * P], prob[:, h, P:3 * P], ssum[:, h, 1:2], None,
                                      ALU.mult).then_inc(prob_done, 1)

            def attn_out(g):
                for m in range(2 * g, 2 * g + 2):
                    dve.wait_ge(pv_ps, 2 * m + 2)
                    dve.wait_ge(lg_done, m + 1)
                    dve.tensor_copy(attn[:, m, :], ps[:, 2 + m % 2, 0:T]).then_inc(attn_done, 1)

            def gelu_in(n):
                i = n % 2
                dve.wait_ge(ly_in, n + 1)
                step(dve.tensor_scalar(ly2[:, i, :], ly2[:, i, :], GELU_A, 1.0, ALU.mult, ALU.add))
                then()
                dve.tensor_tensor(ly2[:, i, :], ly2[:, i, :], ly[:, i, :], ALU.mult).then_inc(z_done, 1)

            def gelu_out(n):
                dve.wait_ge(zsig_done, n + 1)
                dve.tensor_tensor(attn[:, n, :], ly[:, n % 2, :], sg[:, n % 2, :], ALU.mult).then_inc(gelu_done, 1)

            def state_gelu(n):
                dve.wait_ge(state_done, n + 1)
                dve.wait_ge(gelu_done, n + 1)
                dve.tensor_tensor(xc[:, n, :], xc[:, n, :], attn[:, n, :], ALU.mult).then_inc(lg_done, 1)

            def gate_lru(n):
                dve.wait_ge(gate_in, n + 1)
                dve.wait_ge(lg_done, n + 1)
                dve.tensor_tensor(xc[:, n, :], gate[:, n % 2, :], xc[:, n, :], ALU.mult).then_inc(gate_used, 1)

            def gate_attn(n):
                dve.wait_ge(gate_in, KT + n + 1)
                dve.wait_ge(attn_done, n + 1)
                dve.tensor_tensor(attn[:, n, :], gate[:, n % 2, :], attn[:, n, :], ALU.mult).then_inc(gate_used, 1)
                dve.wait_ge(gate_used, KT + n + 1)
                dve.tensor_tensor(attn[:, n, :], attn[:, n, :], xc[:, n, :], ALU.add).then_inc(merged, 1)

            lru_squares(0)
            gelu_in(0)
            lru_states(0)
            gelu_out(0)
            gelu_in(1)
            gelu_out(1)
            state_gelu(0)
            state_gelu(1)
            softmax_max(0)
            softmax_scale(0)
            for n in (2, 3):
                gelu_in(n)
                gelu_out(n)
                state_gelu(n)
            gelu_in(4)
            gelu_out(4)
            lru_squares(1)
            gelu_in(5)
            gelu_out(5)
            attn_out(0)
            softmax_max(1)
            lru_states(1)
            softmax_scale(1)
            for n in (6, 7):
                gelu_in(n)
                gelu_out(n)
            for n in range(4, 8):
                state_gelu(n)
            gate_lru(0)
            gate_lru(1)
            for g in (2, 3):
                attn_out(g - 1)
                softmax_max(g)
                softmax_scale(g)
                for n in range(4 * g - 6, 4 * g - 2):
                    if n < KT:
                        gate_lru(n)
            gate_attn(0)
            gate_attn(1)
            attn_out(3)
            for n in range(2, KT):
                gate_attn(n)

            dve.wait_ge(late_loaded, 16 * 11)
            for half in range(2):
                dve.wait_ge(chunk_used, ADA_B[KT * half + KT - 1] + 1)
                step(dve.tensor_tensor(mod_row[:, half, :], ps[:, 4 + half, :], bada_row[:, half, :], ALU.add))
                then()
                if half:
                    step(dve.tensor_scalar(mod_row[:, half, :], mod_row[:, half, :], plus1[:, 0:1], None, ALU.add))
                    then()
                ins = dve.tensor_tensor(mod_row[:, half, :], mod_row[:, half, :], gain_row[:, half, :], ALU.mult)
            ins.then_inc(mod_row_done, 1)
            bc = [g1_bc, sh2_bc, a2_bc, g2_bc]
            for b in range(8):
                dve.wait_ge(bc_ps, b + 1)
                dve.tensor_copy(bc[b // 2][:, (b % 2) * 512:(b % 2 + 1) * 512], ps[:, 6 + b % 2, :]).then_inc(bc_done, 1)

            dve.wait_ge(chunk_used, WO[-1] + 1)
            for t in range(TT):
                dve.tensor_tensor(y_sb[:, t, :], ps[:, 2 * t:2 * t + 2, :].rearrange("p a b -> p (a b)"), b_out,
                                  ALU.add).then_inc(y_done, 1)
            dve.wait_ge(x_again, 16)
            dve.wait_ge(bc_done, 8)
            for t in range(TT):
                dve.wait_ge(y_sq, t + 1)
                step(dve.reciprocal(stats[:, 2 + t:3 + t], stats[:, t:t + 1]))
                then()
                step(dve.scalar_tensor_tensor(y_sb[:, t, :], y_sb[:, t, :], stats[:, 2 + t:3 + t], g1_bc, ALU.mult, ALU.mult))
                then()
                dve.tensor_tensor(x1[:, t, :], x1[:, t, :], y_sb[:, t, :], ALU.add).then_inc(x1_done, 1)
            for t in range(TT):
                dve.wait_ge(x1_sq, t + 1)
                step(dve.reciprocal(stats[:, 6 + t:7 + t], stats[:, 4 + t:5 + t]))
                then()
                step(dve.scalar_tensor_tensor(h2[:, t, :], x1[:, t, :], stats[:, 6 + t:7 + t], a2_bc, ALU.mult, ALU.mult))
                then()
                dve.tensor_tensor(h2[:, t, :], h2[:, t, :], sh2_bc, ALU.add).then_inc(h2_done, 1)
            dve.wait_ge(h2_t_ps, TT)
            for b in range(2):
                dve.tensor_copy(h2_t[:, 2 * b:2 * b + 2, :], ps[:, 4 + b, :].rearrange("p (k t) -> p k t", k=2)).then_inc(h2_t_dve, 1)

            for t in range(TT):
                dve.wait_ge(logits_ps, t + 1)
                step(dve.tensor_tensor(logits[:, t, :], ps[:, t, 0:EXPERTS], b_rt[:, :], ALU.add))
                then()
                step(dve.max(top8[:, t, :], logits[:, t, :]))
                then()
                dve.tensor_scalar(top_w[:, t, 4:5], top8[:, t, 0:1], -1.0, None, ALU.mult).then_inc(top_done, 1)
                step(dve.max_index(top_i[:, t, :], top8[:, t, :], logits[:, t, :]))
                then()
                step(dve.tensor_copy(top_f[:, t, :], top_i[:, t, :]))
                then()
            for t in range(TT):
                dve.wait_ge(topexp_done, t + 1)
                step(dve.reciprocal(top_w[:, t, 5:6], top_w[:, t, 6:7]))
                then()
                step(dve.tensor_scalar(top_w[:, t, 0:4], top_w[:, t, 0:4], top_w[:, t, 5:6], None, ALU.mult))
                then()
                for k in range(TOP_K):
                    w = top_w[:, t, k:k + 1]
                    i = top_f[:, t, k:k + 1]
                    if k == 0:
                        step(dve.tensor_scalar(route_w[:, t, :], expert_no[:, :], i, w, ALU.is_equal, ALU.mult))
                        step(dve.tensor_scalar(hit[:, t, :], expert_no[:, :], i, None, ALU.is_equal))
                    else:
                        step(dve.tensor_scalar(route_t[:, 0, :], expert_no[:, :], i, w, ALU.is_equal, ALU.mult))
                        step(dve.scalar_tensor_tensor(hit[:, t, :], expert_no[:, :], i, hit[:, t, :], ALU.is_equal, ALU.add))
                        then()
                        step(dve.tensor_tensor(route_w[:, t, :], route_w[:, t, :], route_t[:, 0, :], ALU.add))
                    then()
                dve.tensor_copy(hit_b[:, t, :], hit[:, t, :]).then_inc(route_done, 1)
            dve.wait_ge(rank_ps, 1)
            step(dve.reduce_max(passes_f[:, 0:1], ps[:, 2, 2 * EXPERTS:3 * EXPERTS], axis=AX.X))
            step(dve.scalar_tensor_tensor(rank[:, :, :], ps[:, 2, 0:2 * EXPERTS].rearrange("p (t e) -> p t e", t=TT), 1.0,
                                          hit[:, :, :], ALU.add, ALU.mult))
            then()
            step(dve.tensor_scalar(rank[:, :, :], rank[:, :, :], 1.0, None, ALU.subtract))
            for i in range(1, PASSES):
                step(dve.tensor_scalar(passes_f[:, i:i + 1], passes_f[:, 0:1], float(i * BLOCK), None, ALU.is_gt))
            then()
            step(dve.tensor_tensor(passes_f[:, 1:2], passes_f[:, 1:2], passes_f[:, 2:3], ALU.add))
            then()
            dve.wait_ge(route_t_ps, 1)
            dve.tensor_copy(route_wt[:, :], ps[0:EXPERTS, 4, 0:T]).then_inc(route_t_done, 1)
            dve.tensor_tensor(more_i[:, :], passes_f[:, 1:2], passes_f[:, 3:4], ALU.add).then_inc(rank_done, 1)

            def experts(turn, q, p):
                for r in range(UNROLL):
                    done = turn * UNROLL + r
                    e = q * UNROLL + r
                    dve.wait_ge(chunk_used, turn * (UNROLL * EXPERT_CHUNKS) + (MIXER_CHUNKS + r * EXPERT_CHUNKS - E2_CHUNKS + 1))
                    if p is not None and r == 0:
                        dve.wait_ge(rank_done, p + 2)
                    for t in range(TT):
                        dve.tensor_scalar(pick[:, t, :], slot_no[:, 0, :], rank[:, t, bass.ds(e, 1)], None, ALU.is_equal)
                        dve.tensor_scalar(scat[:, t].rearrange("p a s -> p (a s)"), slot_no[:, :, :].rearrange("p a s -> p (a s)"),
                                          rank[:, t, bass.ds(e, 1)], route_w[:, t, bass.ds(e, 1)], ALU.is_equal, ALU.mult)
                    dve.tensor_scalar(bias_pick[:, :], ones[0:EXPERTS, 0:BLOCK], ident[0:EXPERTS, bass.ds(e, 1)], None,
                                      ALU.mult).then_inc(picked, 1)
                    dve.wait_ge(gathered, done + 1)
                    dve.tensor_copy(hsel[:, :, :], ps[:, 7, :].rearrange("p (k s) -> p k s", k=KT)).then_inc(hsel_done, 1)
                    dve.wait_ge(chunk_used, turn * (UNROLL * EXPERT_CHUNKS) + MIXER_CHUNKS + r * EXPERT_CHUNKS + E1_CHUNKS)
                    dve.tensor_scalar(g_c, ps[:, 4, :], LIMIT, None, ALU.min).then_inc(g_done, 1)
                    dve.tensor_scalar(u_c, ps[:, 5, :], LIMIT, -LIMIT, ALU.min, ALU.max).then_inc(g_done, 1)
                    dve.wait_ge(g_done, done * 3 + 2)
                    dve.scalar_tensor_tensor(u_c, u_c, 1.0, g_c, ALU.add, ALU.mult).then_inc(g_done, 1)
                    dve.wait_ge(sig_done, done + 1)
                    dve.wait_ge(g_done, done * 3 + 3)
                    dve.tensor_tensor(g_u, u_c, s_g, ALU.mult).then_inc(act_done, 1)
                    dve.wait_ge(act_t_ps, done * 2 + 1)
                    dve.tensor_copy(act_t[:, 0:2].rearrange("p a b c -> p (a b c)"), ps[:, 6, 0:T]).then_inc(act_t_d, 1)
                    dve.wait_ge(chunk_used, turn * (UNROLL * EXPERT_CHUNKS) + MIXER_CHUNKS + (r + 1) * EXPERT_CHUNKS)
                    dve.tensor_copy(o_sb, ps[:, 6, :]).then_inc(o_done, 1)

            def next_pass(p):
                dve.wait_ge(picked, (p + 1) * EXPERTS)
                dve.tensor_scalar(rank[:, :, :], rank[:, :, :], float(BLOCK), None, ALU.subtract).then_inc(rank_done, 1)

            more = all_experts(dve, experts, next_pass)

            dve.wait_ge(combined, more * EXPERTS + (EXPERTS + 1))
            for t in range(TT):
                dve.wait_ge(y2_sq, t + 1)
                step(dve.reciprocal(stats[:, 10 + t:11 + t], stats[:, 8 + t:9 + t]))
                then()
                step(dve.scalar_tensor_tensor(fin[:, t, :], ps[:, 2 * t:2 * t + 2, :].rearrange("p a b -> p (a b)"),
                                              stats[:, 10 + t:11 + t], g2_bc, ALU.mult, ALU.mult))
                then()
                dve.tensor_tensor(fin[:, t, :], fin[:, t, :], x1[:, t, :], ALU.add).then_inc(fin_done, 1)

        @block.scalar
        def _(act):
            def load(dst, src, s):
                act.dma_start(dst, src).then_inc(s, 16)

            def rows_of(name):
                return a[name].rearrange("l (r p) -> (l r) p", p=P)

            load(rows[R_C:R_C + KT, :], a["c"].rearrange("l (r p) -> (l r) p", p=P), rows_loaded)
            load(x_in, a["x"][0].rearrange("(t p) d -> p t d", p=P), x_loaded)
            load(rows[R_GPRE:R_GPRE + KT, :], rows_of("g_pre_mix"), rows_loaded)
            load(rows[R_BADA:R_BADA + 2 * KT, :], rows_of("b_ada")[0:2 * KT], rows_loaded)
            load(rows[R_BIN:R_BIN + 4 * KT, :], rows_of("b_in")[LX0 // P:LX0 // P + 4 * KT], rows_loaded)
            load(rows[R_CONVW:R_CONVW + CONV * KT, :], a["conv_w"][0].rearrange("t (r p) -> (t r) p", p=P), rows_loaded)
            load(rows[R_CONVB:R_CONVB + KT, :], rows_of("conv_b"), rows_loaded)
            load(rows[R_BRG:R_BRG + KT, :], rows_of("b_rg"), rows_loaded)
            load(rows[R_BIG:R_BIG + KT, :], rows_of("b_ig"), rows_loaded)
            load(rows[R_LRUA:R_LRUA + KT, :], rows_of("lru_a"), rows_loaded)
            load(rows_qk[:, :], rows_of("b_in")[0:10], rows_loaded)
            load(freq[:, :], a["inv_freq"], rows_loaded)
            load(tmp_b.bitcast(I32), a["positions"][0:1, :].broadcast_to([P, T]), small_loaded)
            load(sinks[:, :], a["sinks"][0:1, :].broadcast_to([P, HEADS]), small_loaded)
            load(b_v[:, :], a["b_in"][0:1, V0:V0 + PROJ_W].broadcast_to([P, PROJ_W]), small_loaded)
            load(b_rt[:, :], a["b_router"][0:1, :].broadcast_to([P, EXPERTS]), small_loaded)
            load(w_rt[:, :, :], a["w_router"][0].rearrange("(k p) e -> p k e", p=P), small_loaded)

            act.wait_ge(eps_set, 1)
            act.wait_ge(x_loaded, 16)
            for t in range(TT):
                ins = act.activation(x_n[:, t, :], x_in[:, t, :], ACT.Square, accum_out=stats[:, t:t + 1])
            ins.then_inc(act_step, 1)
            act.wait_ge(act_step, 1)
            act.activation(stats[:, 0:2], stats[:, 0:2], ACT.Sqrt, bias=eps[:, 0:1], scale=1.0 / D).then_inc(x_sq, 1)
            act.wait_ge(cols_done, 2)
            act.activation(silu_c[:, :], cols[:, R_C:R_C + KT], ACT.Sigmoid).then_inc(c_sig, 1)
            act.activation(stats[:, 4:12], cols[:, R_LRUA:R_LRUA + KT], ACT.Exp).then_inc(act_step, 1)
            act.wait_ge(act_step, 2)
            act.activation(stats[:, 4:12], stats[:, 4:12], ACT.Ln, bias=1.0).then_inc(sp_done, 1)
            act.wait_ge(angle_done, 1)
            act.activation(sin_t, cos_t, ACT.Sin).then_inc(sin_done, 1)
            act.activation(tmp_a, cos_t, ACT.Sin, scale=0.5).then_inc(sin_done, 1)
            act.wait_ge(mod_done, 1)
            act.wait_ge(xn_t, TT)
            for k in range(KT // 2, KT):
                act.activation(h_t[:, k, :], ps[:, 4 + k // 2, (k % 2) * T:(k % 2 + 1) * T], ACT.Identity, bias=mod_a[:, k:k + 1],
                               scale=mod_a[:, KT + k:KT + k + 1]).then_inc(h_act, 1)

            act.wait_ge(pad_set, 1)
            def bias_in(base, n):
                at = R_BIN + (base - LX0) // P + n
                return cols[:, at:at + 1]

            for c in range(4):
                act.wait_ge(chunk_used, LX[c] + 1)
                for i in range(2):
                    ins = act.activation(lx[:, 2 * c + i, CONV - 1:], ps[:, c % 2, i * T:(i + 1) * T], ACT.Identity,
                                         bias=bias_in(LX0, 2 * c + i))
                ins.then_inc(proj_read, 1)
            for c in range(5):
                act.wait_ge(chunk_used, (QC[c] if c < 4 else KC) + 1)
                if c >= 2:
                    act.wait_ge(rope_q, c - 1)
                for i in range(2):
                    ins = act.activation(qk_raw[:, c % 2, i, :], ps[:, c % 2, i * T:(i + 1) * T], ACT.Identity,
                                         bias=cols_qk[:, 2 * c + i:2 * c + i + 1])
                ins.then_inc(proj_read, 1)

            def gate_sigmoids(b):
                for n in range(4 * b, 4 * b + 4):
                    if n % 4 == 3:
                        act.wait_ge(chunk_used, GATES[b] + 1)
                    else:
                        act.wait_ge(gates_ps, 3 * b + n % 4 + 1)
                    if n == 4:
                        act.wait_ge(state_done, 4)
                    act.activation(g_r[:, n % 4, :], ps[:, 2 + n % 2, 0:T], ACT.Sigmoid, bias=cols[:, R_BRG + n:R_BRG + n + 1])
                    act.activation(g_i[:, n % 4, :], ps[:, 2 + n % 2, T:2 * T], ACT.Sigmoid,
                                   bias=cols[:, R_BIG + n:R_BIG + n + 1]).then_inc(gates_read, 1)

            def gate_powers(b):
                act.wait_ge(decay_done, 1)
                for n in range(4 * b, 4 * b + 4):
                    act.wait_ge(gates_read, n + 1)
                    act.activation(g_a[:, n % 4, :], g_r[:, n % 4, :], ACT.Exp, scale=decay[:, 0, n:n + 1]).then_inc(a_done, 1)
                for n in range(4 * b, 4 * b + 4):
                    act.wait_ge(a_done, n + 1)
                    act.activation(g_r[:, n % 4, :], g_r[:, n % 4, :], ACT.Tanh, scale=decay[:, 1, n:n + 1]).then_inc(th_done, 1)

            def gate_roots(b):
                act.wait_ge(m2_done, 4 * b + 4)
                act.activation(z_gate[:, 0:1024], z_gate[:, 0:1024], ACT.Sqrt).then_inc(mult_done, 1)

            def exps(g):
                act.wait_ge(smax_done, g + 1)
                for h in range(GROUP):
                    for b, sl in ((0, slice(0, P)), (1, slice(P, 3 * P))):
                        act.activation(prob[:, h, sl], prob[:, h, sl], ACT.Exp, bias=smax[:, h, b:b + 1],
                                       scale=HEAD_DIM ** -0.5, accum_out=ssum[:, h, b:b + 1])
                act.activation(snk[:, :, :], snk[:, :, :], ACT.Exp).then_inc(exp_done, 1)

            def prob_t(g):
                for h in range(GROUP):
                    act.wait_ge(prob_t_ps, GROUP * g + h + 1)
                    act.activation(prob[:, h, :], ps[:, 4 + h, 0:3 * P], ACT.Copy).then_inc(prob_t_done, 1)

            def read_ly(n):
                i = n % 2
                j = PROJ.index(LY[n // 2])
                if i == 0:
                    act.wait_ge(chunk_used, LY[n // 2] + 1)
                if n == 0:
                    act.wait_ge(rope_q, 5)
                if n >= 2:
                    act.wait_ge(gelu_done, n - 1)
                src = ps[:, j % 2, i * T:(i + 1) * T]
                act.activation(ly[:, i, :], src, ACT.Identity, bias=bias_in(LY0, n))
                act.activation(ly2[:, i, :], src, ACT.Square, bias=bias_in(LY0, n)).then_inc(ly_in, 1)

            def gelu_sig(n):
                act.wait_ge(z_done, n + 1)
                act.activation(sg[:, n % 2, :], ly2[:, n % 2, :], ACT.Sigmoid, scale=GELU_B).then_inc(zsig_done, 1)

            def read_gate(n):
                base, m = (GL0, n) if n < KT else (GA0, n - KT)
                chunk = (GL if n < KT else GA)[m // 2]
                i = n % 2
                if i == 0:
                    act.wait_ge(chunk_used, chunk + 1)
                if n >= 2:
                    act.wait_ge(gate_used, n - 1)
                act.activation(gate[:, i, :], ps[:, PROJ.index(chunk) % 2, i * T:(i + 1) * T], ACT.Sigmoid,
                               bias=bias_in(base, m)).then_inc(gate_in, 1)

            gate_sigmoids(0)
            gate_powers(0)
            read_ly(0)
            gate_roots(0)
            gelu_sig(0)
            read_ly(1)
            gelu_sig(1)
            exps(0)
            for n in (2, 3):
                read_ly(n)
                gelu_sig(n)
            gate_sigmoids(1)
            prob_t(0)
            read_ly(4)
            gelu_sig(4)
            gate_powers(1)
            read_ly(5)
            gelu_sig(5)
            gate_roots(1)
            exps(1)
            for n in (6, 7):
                read_ly(n)
                gelu_sig(n)
            prob_t(1)
            read_gate(0)
            read_gate(1)
            exps(2)
            act.wait_ge(state_done, KT)
            load(x1, a["x"][0].rearrange("(t p) d -> p t d", p=P), x_again)
            load(b_out, a["b_out"][0:1, :].broadcast_to([P, D]), late_loaded)
            act.wait_ge(gelu_done, KT)
            for quad in range(4):
                src = a["b_ada"][0:1, 2 * D:6 * D].rearrange("l (h c n) -> l h c n", h=2, c=4)[:, :, quad, :]
                load(bada_row[32 * quad:32 * quad + 1, :, :], src, late_loaded)
            read_gate(2)
            read_gate(3)
            prob_t(2)
            read_gate(4)
            read_gate(5)
            exps(3)
            read_gate(6)
            read_gate(7)
            prob_t(3)
            for n in range(8, 2 * KT):
                read_gate(n)
            act.wait_ge(late_set, 1)
            for half, quad, name, part in ((0, 0, "g_post_mix", 0), (0, 1, "g_post_mix", 1), (1, 0, "g_pre_ffn", 0),
                                           (1, 1, "g_pre_ffn", 1), (1, 2, "g_post_ffn", 0), (1, 3, "g_post_ffn", 1)):
                load(gain_row[32 * quad:32 * quad + 1, half, :], a[name][0:1, 512 * part:512 * (part + 1)], late_loaded)

            for t in range(TT):
                act.wait_ge(y_done, t + 1)
                act.activation(junk, y_sb[:, t, :], ACT.Square, accum_out=stats[:, t:t + 1]).then_inc(act_step, 1)
                act.wait_ge(act_step, 3 + t)
                act.activation(stats[:, t:t + 1], stats[:, t:t + 1], ACT.Sqrt, bias=eps[:, 0:1], scale=1.0 / D).then_inc(y_sq, 1)
            for t in range(TT):
                act.wait_ge(x1_done, t + 1)
                act.activation(junk, x1[:, t, :], ACT.Square, accum_out=stats[:, 4 + t:5 + t]).then_inc(act_step, 1)
                act.wait_ge(act_step, 5 + t)
                act.activation(stats[:, 4 + t:5 + t], stats[:, 4 + t:5 + t], ACT.Sqrt, bias=eps[:, 0:1],
                               scale=1.0 / D).then_inc(x1_sq, 1)
            load(b_e1[0:EXPERTS, :], a["b_e1"][0], moe_loaded)
            act.wait_ge(bc_done, 8)
            load(b_e2[:, :], a["b_e2"][0], moe_loaded)
            act.wait_ge(h2_t_ps, TT)
            for b in range(2, 4):
                act.activation(h2_t[:, 2 * b:2 * b + 2, :], ps[:, 4 + b, :].rearrange("p (k t) -> p k t", k=2),
                               ACT.Copy).then_inc(h2_t_act, 1)
            for t in range(TT):
                act.wait_ge(top_done, t + 1)
                act.activation(top_w[:, t, 0:TOP_K], top8[:, t, 0:TOP_K], ACT.Exp, bias=top_w[:, t, 4:5],
                               accum_out=top_w[:, t, 6:7]).then_inc(topexp_done, 1)

            def experts(turn, q, p):
                for r in range(UNROLL):
                    done = turn * UNROLL + r
                    act.wait_ge(g_done, done * 3 + 1)
                    act.activation(s_g, g_c, ACT.Sigmoid, scale=ALPHA).then_inc(sig_done, 1)
                    act.wait_ge(act_t_ps, done * 2 + 1)
                    act.activation(act_t[:, 2:4].rearrange("p a b c -> p (a b c)"), ps[:, 7, 0:T], ACT.Copy).then_inc(act_t_a, 1)
                    act.wait_ge(act_t_ps, done * 2 + 2)
                    act.activation(scat_t[:, :, :], ps[:, 4, 0:T].rearrange("p (t s) -> p t s", t=TT), ACT.Copy).then_inc(scat_t_done, 1)

            more = all_experts(act, experts)

            act.wait_ge(combined, more * EXPERTS + (EXPERTS + 1))
            for t in range(TT):
                act.activation(junk, ps[:, 2 * t:2 * t + 2, :].rearrange("p a b -> p (a b)"), ACT.Square,
                               accum_out=stats[:, 8 + t:9 + t]).then_inc(act_step, 1)
                act.wait_ge(act_step, 7 + t)
                act.activation(stats[:, 8 + t:9 + t], stats[:, 8 + t:9 + t], ACT.Sqrt, bias=eps[:, 0:1],
                               scale=1.0 / D).then_inc(y2_sq, 1)
            for t in range(TT):
                act.wait_ge(fin_done, t + 1)
                act.dma_start(out[0, t * P:(t + 1) * P, :], fin[:, t, :]).then_inc(out_stored, 16)
            act.wait_ge(out_stored, 16 * TT)

        @block.gpsimd
        def _(pool):
            pool.memset(ones[:, :], 1.0).then_inc(pool_set, 1)
            pool.memset(ident[:, :], 0.0).then_inc(pool_set, 1)
            pool.memset(mask[:, :, :], 0.0).then_inc(pool_set, 1)
            pool.wait_ge(pool_set, 3)
            pool.affine_select(out=ident[:, :], in_=ident[:, :], compare_op=ALU.not_equal, fill=1.0, base=0,
                               pattern=[[-1, P]], channel_multiplier=1).then_inc(pool_set, 1)
            pool.affine_select(out=mask[:, 1, :], in_=mask[:, 1, :], compare_op=ALU.is_ge, fill=NEG, base=0,
                               pattern=[[-1, P]], channel_multiplier=1).then_inc(pool_set, 1)
            pool.affine_select(out=mask[:, 0, :], in_=mask[:, 0, :], compare_op=ALU.is_gt, fill=NEG, base=0,
                               pattern=[[1, P]], channel_multiplier=-1).then_inc(pool_set, 1)
            pool.memset(ones_b[:, :], 1.0).then_inc(pool_set, 1)
            pool.wait_ge(pool_set, 7)
            pool.affine_select(out=before[:, :], in_=ones_b[:, :], compare_op=ALU.is_gt, fill=0.0, base=0,
                               pattern=[[1, P]], channel_multiplier=-1).then_inc(pool_set, 1)
            pool.iota(slot_no[:, :, :], pattern=[[0, 2], [1, BLOCK]], base=0, channel_multiplier=0,
                      allow_small_or_imprecise_dtypes=True).then_inc(pool_set, 1)
            pool.iota(expert_no[:, :], pattern=[[1, EXPERTS]], base=0, channel_multiplier=0,
                      allow_small_or_imprecise_dtypes=True).then_inc(pool_set, 1)
            pool.wait_ge(xn_done, TT)
            pool.memset(lx[:, :, 0:CONV - 1], 0.0).then_inc(pad_set, 1)
            for c in range(5):
                pool.wait_ge(swapped, c + 1)
                pool.tensor_tensor(swap, swap, sin_t[:, None, :].broadcast_to([P, 2, T]), ALU.mult).then_inc(times_sin, 1)
            for n in range(KT):
                pool.wait_ge(gates_read, n + 1)
                pool.tensor_tensor(g_i[:, n % 4, :], g_i[:, n % 4, :], xc[:, n, :], ALU.mult).then_inc(ix_done, 1)
            pool.wait_ge(scores_ps, KV_HEADS)
            pool.memset(gain_row[:, :, :], 1.0).then_inc(late_set, 1)


_INS = ["x", "c", "positions", "w_ada", "b_ada", "g_pre_mix", "g_post_mix", "w_in", "b_in", "sinks", "conv_w", "conv_b",
        "w_rg", "b_rg", "w_ig", "b_ig", "lru_a", "w_out", "b_out", "g_pre_ffn", "g_post_ffn", "w_router", "b_router",
        "w_e1", "b_e1", "w_e2", "b_e2"]


def kernel(**inputs):
    import concourse.bacc as _bacc
    from concourse.bass_utils import run_bass_kernel_spmd as _run

    nc = _bacc.Bacc("TRN2", target_bir_lowering=False, num_devices=1)
    arrays, aps = {}, {}
    for name in _INS:
        arrays[f"in_{name}"] = np.ascontiguousarray(inputs[name])
    freqs = np.float32(ROPE_THETA) ** (-np.arange(0, HEAD_DIM, 2, dtype=np.float32) / np.float32(HEAD_DIM))
    arrays["in_inv_freq"] = np.tile(freqs.astype(np.float32), P // HALF).reshape(P, 1)
    for name, v in arrays.items():
        aps[name[3:]] = nc.dram_tensor(name, v.shape, mybir.dt.from_np(v.dtype), kind="ExternalInput").ap()
    out = nc.dram_tensor("out_0", (1, T, D), F32, kind="ExternalOutput").ap()
    layer(nc, aps, out)
    r = _run(nc, [arrays], core_ids=[0])
    return r.results[0]["out_0"]
```

```python
from contextlib import ExitStack

import numpy as np

import concourse.bass as bass
import concourse.mybir as mybir

F32 = mybir.dt.float32
BF16 = mybir.dt.bfloat16
I32 = mybir.dt.int32
U32 = mybir.dt.uint32
ALU = mybir.AluOpType
ACT = mybir.ActivationFunctionType
AX = mybir.AxisListType

P = 128
D = 1024
T = 256
TT = T // P
KT = D // P
HEADS, KV_HEADS, HEAD_DIM = 16, 4, 64
HALF = HEAD_DIM // 2
GROUP = HEADS // KV_HEADS
CONV = 4
EXPERTS, TOP_K = 32, 4
LIMIT, ALPHA = 7.0, 1.702
LRU_C = 8.0
EPS = 1e-6
ROPE_THETA = 10000.0
NEG = -1.0e30
GELU_A = 0.044715
GELU_B = 2.0 * float(np.sqrt(2.0 / np.pi))
BLOCK = 64
PASSES = T // BLOCK

Q0, K0, V0 = 0, HEADS * HEAD_DIM, HEADS * HEAD_DIM + KV_HEADS * HEAD_DIM
LX0 = V0 + KV_HEADS * HEAD_DIM
LY0, GA0, GL0 = LX0 + D, LX0 + 2 * D, LX0 + 3 * D

RING = 16
SLOT = 2048
PROJ_W = 256
N_ADA_A = KT
LX = [N_ADA_A + i for i in range(4)]
QC = [LX[-1] + 1 + i for i in range(4)]
KC = QC[-1] + 1
VC = KC + 1
GATES_A = VC + 1
LY_A = [GATES_A + 1, GATES_A + 2]
GATES_B = LY_A[-1] + 1
LY = [*LY_A, GATES_B + 1, GATES_B + 2]
GATES = (GATES_A, GATES_B)
GL = [LY[-1] + 1 + i for i in range(4)]
GA = [GL[-1] + 1 + i for i in range(4)]
SH2, G1, SC2, GT2 = range(4)
VECTOR_AT = (3, 2, 4, 5)
ADA_B = [[GA[-1] + 1 + 4 * v + (4 if v >= SC2 else 0) + i for i in range(4)] for v in range(4)]
WO = [ADA_B[G1][-1] + 1 + i for i in range(4)]
MIXER_CHUNKS = ADA_B[GT2][-1] + 1
E1_CHUNKS, E2_CHUNKS = KT, KT // 2
EXPERT_CHUNKS = E1_CHUNKS + E2_CHUNKS
UNROLL = 4
assert UNROLL * EXPERT_CHUNKS % RING == 0
TURNS = UNROLL * EXPERT_CHUNKS // RING
PROJ = [*LX, *QC, KC, VC, *LY, *GL, *GA]

ROW_BANK = (4, 4, 5, 4)
ROW_AT = (0, 256, 0, 0)

R_C, R_GPRE, R_BADA, R_BIN, R_CONVW, R_CONVB, R_BRG, R_BIG, R_LRUA = 0, 8, 16, 32, 64, 96, 104, 112, 120


def layer(nc, a, out):
    with ExitStack() as ctx:
        def sb(name, shape, dt=F32):
            return ctx.enter_context(nc.sbuf_tensor(name, shape, dt))

        def sem(name):
            return ctx.enter_context(nc.semaphore(name))

        ps = ctx.enter_context(nc.psum_tensor("ps", [P, 8, 512], F32))

        ring = sb("ring", [P, RING, SLOT])
        ident = sb("ident", [P, P])
        ones = sb("ones", [P, P])
        before = sb("before", [P, P], BF16)
        ones_b = sb("ones_b", [P, P], BF16)
        mask = sb("mask", [P, 2, P])
        slot_no = sb("slot_no", [P, 2, BLOCK])
        expert_no = sb("expert_no", [P, EXPERTS])
        rows = sb("rows", [P, P])
        rows_qk = sb("rows_qk", [10, P])
        cols = sb("cols", [P, P])
        cols_qk = sb("cols_qk", [P, 10])
        freq = sb("freq", [P, 1])
        silu_c = sb("silu_c", [P, KT])
        mod_a = sb("mod_a", [P, 2 * KT])
        decay = sb("decay", [P, 2, KT])
        stats = sb("stats", [P, 16])
        sinks = sb("sinks", [P, HEADS])
        neg_sinks = sb("neg_sinks", [P, HEADS])
        smax = sb("smax", [P, GROUP, 2])
        ssum = sb("ssum", [P, GROUP, 2])
        snk = sb("snk", [P, GROUP, 2])
        b_v = sb("b_v", [P, KV_HEADS * HEAD_DIM])
        w_rt = sb("w_rt", [P, KT, EXPERTS])
        b_rt = sb("b_rt", [P, EXPERTS])
        fold = sb("fold", [P, EXPERTS])
        expert_hot = sb("expert_hot", [EXPERTS, EXPERTS + 1])
        eps = sb("eps", [P, 1])
        logits = sb("logits", [P, TT, EXPERTS])
        top8 = sb("top8", [P, TT, 8])
        top_i = sb("top_i", [P, TT, 8], U32)
        top_f = sb("top_f", [P, TT, 8])
        neg_max = sb("neg_max", [P, TT, 1])
        sums = sb("sums", [P, TT, 1])
        hit = sb("hit", [P, TT, EXPERTS])
        hit_b = sb("hit_b", [P, TT, EXPERTS], BF16)
        route_w = sb("route_w", [P, TT, EXPERTS])
        rank = sb("rank", [P, TT, EXPERTS + 1])
        passes_f = sb("passes_f", [P, 4])
        more_i = sb("more_i", [P, 1], I32)

        z_h = sb("z_h", [P, 2048])
        z_attn = sb("z_attn", [P, KT * (T + CONV - 1)])
        z_lru = sb("z_lru", [P, 2048])
        z_gate = sb("z_gate", [P, 3072])
        z_q = sb("z_q", [P, 2048])
        z_k = sb("z_k", [P, 2048])
        z_p = sb("z_p", [P, GROUP * 3 * P])
        z_t = sb("z_t", [P, 1536])
        z_c = sb("z_c", [P, 1536])

        def v3(t, at, a_, b_):
            return t[:, at:at + a_ * b_].rearrange("p (a b) -> p a b", a=a_)

        def v4(t, at, a_, b_, c_):
            return t[:, at:at + a_ * b_ * c_].rearrange("p (a b c) -> p a b c", a=a_, b=b_)

        x_in = v3(z_attn, 0, TT, D)
        x_n = v3(z_gate, 0, TT, D)
        mod_a_rows = z_t[:, 0:512]
        h_t = v3(z_h, 0, KT, T)
        lx = v3(z_attn, 0, KT, T + CONV - 1)
        xc = v3(z_lru, 0, KT, T)
        g_r, g_i, g_a = (v3(z_gate, 1024 * i, 4, T) for i in range(3))
        q_r = v3(z_q, 0, KT, T)
        k_rep = v3(z_k, 0, KV_HEADS, T)
        qk_raw = v4(z_t, 0, 2, 2, T)
        swap = v3(z_t, 1024, 2, T)
        k_r = v3(z_p, 0, 2, T)
        prob = v3(z_p, 0, GROUP, 3 * P)
        cos_t, sin_t, tmp_a, tmp_b = (z_c[:, T * i:T * (i + 1)] for i in range(4))
        v_sb = v3(z_c, 1024, TT, KV_HEADS * HEAD_DIM)
        lru_tmp = v3(z_c, 0, 2, T)
        gate = v3(z_c, 512, 2, T)
        attn = v3(z_attn, 0, KT, T)
        ly = v3(z_t, 0, 2, T)
        ly2 = v3(z_t, 512, 2, T)
        sg = v3(z_t, 1024, 2, T)
        x1 = v3(z_gate, 0, TT, D)
        b_out = z_gate[:, 2048:2560]
        g1_bc = z_q[:, 0:1024]
        sh2_bc = z_q[:, 1024:2048]
        g2_bc = z_k[:, 0:1024]
        gain_row = v3(z_k, 1024, 4, 256)
        mod_row = v3(z_p, 0, 4, 256)
        bada_row = v3(z_t, 0, 4, 256)
        y_g = v3(z_attn, 0, TT, D)
        logit_part = z_p[:, 1280:1536]
        soft = v3(z_c, 512, TT, EXPERTS)
        match = v4(z_c, 0, TT, TOP_K, EXPERTS)
        h2 = v3(z_h, 0, TT, D)
        h2_t = v3(z_attn, 0, KT, T)
        b_e1 = z_lru[:, 0:2048]
        hsel = v3(z_attn, 0, KT, BLOCK)
        g_c, u_c, s_g = (z_attn[:, 512 * i:512 * (i + 1)] for i in (1, 2, 3))
        act_t = v4(z_q, 0, 4, 2, BLOCK)
        g_u = z_q[:, 512:1024]
        o_sb = z_q[:, 1024:1536]
        scat_t = v3(z_q, 1536, TT, P)
        scat = v4(z_q, 1792, TT, 2, BLOCK)
        b_e2 = z_gate[0:EXPERTS, 2048:3072]
        route_wt = z_p[0:EXPERTS, 1024:1280]
        pick = v3(z_t, 0, TT, BLOCK)
        bias_pick = z_t[0:EXPERTS, 256:256 + BLOCK]
        fin = v3(z_lru, 0, TT, D)
        junk = z_c[:, 0:1024]

        landed = [sem(f"landed{i}") for i in range(RING)]
        chunk_used = sem("chunk_used")
        x_loaded, rows_loaded, small_loaded, x_again = sem("x_loaded"), sem("rows_loaded"), sem("small_loaded"), sem("x_again")
        late_loaded, moe_loaded, pad_set = sem("late_loaded"), sem("moe_loaded"), sem("pad_set")
        out_stored = sem("out_stored")
        pool_set, pool_step = sem("pool_set"), sem("pool_step")
        dve_step, act_step = sem("dve_step"), sem("act_step")
        eps_set = sem("eps_set")
        x_sq, xn_done, xn_t, rows_t, cols_done, c_sig, silu_done = (sem(n) for n in (
            "x_sq", "xn_done", "xn_t", "rows_t", "cols_done", "c_sig", "silu_done"))
        mod_rows, mod_cols, mod_done = sem("mod_rows"), sem("mod_cols"), sem("mod_done")
        h_dve, h_act = sem("h_dve"), sem("h_act")
        proj_read, v_done = sem("proj_read"), sem("v_done")
        pos_f, angle_done, sin_done, rope_done = sem("pos_f"), sem("angle_done"), sem("sin_done"), sem("rope_done")
        swapped, times_sin, rope_q, k_rep_done = sem("swapped"), sem("times_sin"), sem("rope_q"), sem("k_rep_done")
        conv_done, gates_ps, gates_read = sem("conv_done"), sem("gates_ps"), sem("gates_read")
        decay_done, sp_done = sem("decay_done"), sem("sp_done")
        a_done, th_done, m2_done, mult_done, ix_done, u_done, state_done = (sem(n) for n in (
            "a_done", "th_done", "m2_done", "mult_done", "ix_done", "u_done", "state_done"))
        scores_ps, smax_done, exp_done, prob_done = sem("scores_ps"), sem("smax_done"), sem("exp_done"), sem("prob_done")
        prob_t_ps, prob_t_done, pv_ps, attn_done = sem("prob_t_ps"), sem("prob_t_done"), sem("pv_ps"), sem("attn_done")
        ly_in, gelu_done, z_done, zsig_done, lg_done = (sem(n) for n in ("ly_in", "gelu_done", "z_done", "zsig_done", "lg_done"))
        gate_in, gate_used, merged = sem("gate_in"), sem("gate_used"), sem("merged")
        mod_row_done, bc_ps, bc_done = sem("mod_row_done"), sem("bc_ps"), sem("bc_done")
        part_ps, part_done = sem("part_ps"), sem("part_done")
        y_sq, x1_done, x1_sq, h2_done, h2_t_ps, h2_t_act, h2_t_dve = (sem(n) for n in (
            "y_sq", "x1_done", "x1_sq", "h2_done", "h2_t_ps", "h2_t_act", "h2_t_dve"))
        logits_ps, top_done, topexp_done, route_done, rank_ps, rank_done = (sem(n) for n in (
            "logits_ps", "top_done", "topexp_done", "route_done", "rank_ps", "rank_done"))
        route_t_ps, route_t_done = sem("route_t_ps"), sem("route_t_done")
        picked, gathered, hsel_done = sem("picked"), sem("gathered"), sem("hsel_done")
        g_done, sig_done, act_done = sem("g_done"), sem("sig_done"), sem("act_done")
        act_t_ps, act_t_a, act_t_d, scat_t_done = sem("act_t_ps"), sem("act_t_a"), sem("act_t_d"), sem("scat_t_done")
        o_done, combined = sem("o_done"), sem("combined")
        y2_sq, fin_done = sem("y2_sq"), sem("fin_done")

        def loads(n):
            return n // RING + 1 + sum(g <= n and g % RING == n % RING for g in GATES)

        def wait_chunk(eng, n):
            eng.wait_ge(landed[n % RING], 16 * loads(n))

        def wait_expert_chunk(eng, r, m, turn):
            n = MIXER_CHUNKS + r * EXPERT_CHUNKS + m
            eng.wait_ge(landed[n % RING], turn * (16 * TURNS) + 16 * loads(n))

        def expert_slot(r, m):
            return (MIXER_CHUNKS + r * EXPERT_CHUNKS + m) % RING

        def all_experts(eng, body, pool=None):
            groups = EXPERTS // UNROLL
            with eng.Fori(0, groups) as q:
                body(q, q, None)
            eng.wait_ge(rank_done, 1)
            more = eng.value_load(more_i[0:1, 0:1], min_val=0, max_val=PASSES - 1)
            with eng.If(more > 0):
                with eng.Fori(0, more) as p:
                    if pool is not None:
                        pool(p)
                    with eng.Fori(0, groups) as q:
                        body(p * groups + q + groups, q, p)
            return more

        block = ctx.enter_context(nc.Block())

        @block.sync
        def _(sp):
            def load(n, dst, src):
                if n >= RING:
                    sp.wait_ge(chunk_used, n - RING + 1)
                sp.dma_start(dst, src).then_inc(landed[n % RING], 16)

            def load_rows(at, src):
                sp.dma_start(rows[at:at + src.shape[0], :], src).then_inc(rows_loaded, 16)

            def rows_of(name):
                return a[name].rearrange("l (r p) -> (l r) p", p=P)

            load_rows(R_C, rows_of("c"))
            load_rows(R_GPRE, rows_of("g_pre_mix"))
            load_rows(R_BADA, rows_of("b_ada")[0:2 * KT])
            load_rows(R_BIN, rows_of("b_in")[LX0 // P:LX0 // P + 4 * KT])
            load_rows(R_CONVW, a["conv_w"][0].rearrange("t (r p) -> (t r) p", p=P))
            load_rows(R_CONVB, rows_of("conv_b"))
            load_rows(R_BRG, rows_of("b_rg"))
            load_rows(R_BIG, rows_of("b_ig"))
            load_rows(R_LRUA, rows_of("lru_a"))
            sp.dma_start(rows_qk[:, :], rows_of("b_in")[0:10]).then_inc(rows_loaded, 16)
            sp.dma_start(freq[:, :], a["inv_freq"]).then_inc(rows_loaded, 16)

            w_ada = a["w_ada"][0].rearrange("(k p) n -> k p n", p=P)
            for k in range(KT):
                load(k, ring[:, k % RING, :], w_ada[k, :, 0:2 * D])
            w_in = a["w_in"][0].rearrange("(k p) n -> p k n", p=P)
            starts = {**{n: LX0 + PROJ_W * i for i, n in enumerate(LX)},
                      **{n: Q0 + PROJ_W * i for i, n in enumerate(QC)}, KC: K0, VC: V0,
                      **{n: LY0 + PROJ_W * i for i, n in enumerate(LY)},
                      **{n: GA0 + PROJ_W * i for i, n in enumerate(GA)},
                      **{n: GL0 + PROJ_W * i for i, n in enumerate(GL)}}
            for n in range(LX[0], GA[-1] + 1):
                slot = ring[:, n % RING, :]
                if n in GATES:
                    half = GATES.index(n)
                    w = slot[:, 0:1024].rearrange("p (g n e) -> p g n e", g=2, n=4)
                    load(n, w[:, 0], a["w_rg"][0, 4 * half:4 * half + 4].rearrange("n d e -> d n e"))
                    load(n, w[:, 1], a["w_ig"][0, 4 * half:4 * half + 4].rearrange("n d e -> d n e"))
                else:
                    c = starts[n]
                    load(n, slot.rearrange("p (k n) -> p k n", k=KT), w_in[:, :, c:c + PROJ_W])
            w_ada2 = a["w_ada"][0].rearrange("(c k p) n -> c p k n", k=2, p=P)
            w_out = a["w_out"][0].rearrange("(c k p) n -> c p k n", k=2, p=P)

            def load_vector(v):
                for i, n in enumerate(ADA_B[v]):
                    at = D * VECTOR_AT[v]
                    load(n, ring[:, n % RING, :].rearrange("p (k n) -> p k n", k=2), w_ada2[i, :, :, at:at + D])

            load_vector(SH2)
            load_vector(G1)
            for i, n in enumerate(WO):
                load(n, ring[:, n % RING, :].rearrange("p (k n) -> p k n", k=2), w_out[i])
            load_vector(SC2)
            load_vector(GT2)

            w_e1 = a["w_e1"][0].rearrange("e (k p) n -> e k p n", p=P)
            w_e2 = a["w_e2"][0].rearrange("e (c k p) n -> e c p k n", k=2, p=P)

            def experts(turn, q, p):
                for r in range(UNROLL):
                    for m in range(EXPERT_CHUNKS):
                        n = MIXER_CHUNKS + r * EXPERT_CHUNKS + m
                        sp.wait_ge(chunk_used, turn * (UNROLL * EXPERT_CHUNKS) + (n - RING + 1))
                        slot = ring[:, n % RING, :]
                        if m < E1_CHUNKS:
                            src = w_e1[bass.ds(q * UNROLL + r, 1), m].rearrange("e p n -> (e p) n")
                        else:
                            slot = slot.rearrange("p (k n) -> p k n", k=2)
                            src = w_e2[bass.ds(q * UNROLL + r, 1), m - E1_CHUNKS].rearrange("e p k n -> (e p) k n")
                        sp.dma_start(slot, src).then_inc(landed[n % RING], 16)

            all_experts(sp, experts)

        @block.tensor
        def _(pe):
            pe.wait_ge(pool_set, 4)
            pe.wait_ge(rows_loaded, 16 * 11)
            pe.transpose(ps[:, 1, 0:P], rows[:, :], ident[:, :])
            pe.transpose(ps[:, 1, P:P + 10], rows_qk[:, :], ident[0:10, 0:10]).then_inc(rows_t, 1)

            pe.wait_ge(silu_done, 1)
            for k in range(N_ADA_A):
                wait_chunk(pe, k)
                for c in range(4):
                    mm = pe.matmul(ps[32 * c:32 * (c + 1), 0, :], silu_c[:, k:k + 1].broadcast_to([P, 32]),
                                   ring[:, k % RING, 512 * c:512 * (c + 1)], start=(k == 0), stop=(k == KT - 1),
                                   tile_position=(0, 32 * c))
                mm.then_inc(chunk_used, 1)
                if k in (1, 3):
                    t = k // 2
                    pe.wait_ge(xn_done, t + 1)
                    for f in range(KT):
                        mm = pe.transpose(ps[:, 4 + f // 2, (f % 2) * T + t * P:(f % 2) * T + (t + 1) * P],
                                          x_n[:, t, f * P:(f + 1) * P], ident[:, :])
                    mm.then_inc(xn_t, 1)
            pe.wait_ge(mod_rows, 1)
            for j in range(4):
                mm = pe.transpose(ps[:, 1, j * P:(j + 1) * P], mod_a_rows[:, j * P:(j + 1) * P], ident[:, :])
            mm.then_inc(mod_cols, 1)

            def proj_bank_free(j):
                if j == 0:
                    pe.wait_ge(mod_done, 1)
                elif j == 1:
                    pe.wait_ge(mod_done, 1)
                elif PROJ[j - 2] == VC:
                    pe.wait_ge(v_done, 1)
                elif PROJ[j - 2] in LY:
                    pe.wait_ge(ly_in, 2 * LY.index(PROJ[j - 2]) + 2)
                elif PROJ[j - 2] in GL + GA:
                    pe.wait_ge(gate_in, 2 * (GL + GA).index(PROJ[j - 2]) + 2)
                else:
                    pe.wait_ge(proj_read, j - 1)

            def project_tile(j, i):
                n = PROJ[j]
                w = ring[:, n % RING, :].rearrange("p (k n) -> p k n", k=KT)
                dst = ps[:, j % 2, i * T:(i + 1) * T]
                if i == 0:
                    proj_bank_free(j)
                    wait_chunk(pe, n)
                for k in range(KT):
                    if j == 0 and i == 0:
                        pe.wait_ge(h_dve if k < KT // 2 else h_act, k % (KT // 2) + 1)
                    if n == VC:
                        mm = pe.matmul(dst, h_t[:, k, i * P:(i + 1) * P], w[:, k, :], start=(k == 0), stop=(k == KT - 1))
                    else:
                        mm = pe.matmul(dst, w[:, k, i * P:(i + 1) * P], h_t[:, k, :], start=(k == 0), stop=(k == KT - 1))
                if i == 1:
                    mm.then_inc(chunk_used, 1)

            def gates(half):
                wait_chunk(pe, GATES[half])
                w = ring[:, GATES[half] % RING, 0:1024].rearrange("p (g n e) -> p g n e", g=2, n=4)
                for n in range(4 * half, 4 * half + 4):
                    pe.wait_ge(conv_done, n + 1)
                    if n >= 2:
                        pe.wait_ge(gates_read, n - 1)
                    for g in range(2):
                        mm = pe.matmul(ps[:, 2 + n % 2, g * T:(g + 1) * T], w[:, g, n % 4, :], xc[:, n, :],
                                       start=True, stop=True)
                    if n % 4 == 3:
                        mm.then_inc(chunk_used, 1)
                    else:
                        mm.then_inc(gates_ps, 1)

            for j in range(len(LX) + len(QC) + 2):
                project_tile(j, 0)
                project_tile(j, 1)
            gates(0)
            def scores(g):
                pe.wait_ge(rope_q, 5)
                pe.wait_ge(k_rep_done, 1)
                if g:
                    pe.wait_ge(prob_t_done, GROUP * g)
                for blk in range(2):
                    for h in range(GROUP):
                        half = slice(h % 2 * HEAD_DIM, (h % 2 + 1) * HEAD_DIM)
                        dst = ps[:, 4 + h, 0:P] if blk == 0 else ps[:, 4 + h, P:3 * P]
                        mm = pe.matmul(dst, q_r[half, 2 * g + h // 2, blk * P:(blk + 1) * P],
                                       k_rep[half, g, 0:(blk + 1) * P], start=True, stop=True,
                                       tile_position=(h % 2 * HEAD_DIM, 0))
                mm.then_inc(scores_ps, 1)

            def transposes(g):
                for h in range(GROUP):
                    pe.wait_ge(prob_done, GROUP * g + h + 1)
                    for b in range(3):
                        mm = pe.transpose(ps[:, 4 + h, b * P:(b + 1) * P], prob[:, h, b * P:(b + 1) * P], ident[:, :])
                    mm.then_inc(prob_t_ps, 1)

            def weighted_values(g):
                for h in range(GROUP):
                    tile_no = 2 * g + h // 2
                    pe.wait_ge(prob_t_done, GROUP * g + h + 1)
                    if h == 0:
                        pe.wait_ge(v_done, 1)
                        if g == 0:
                            pe.wait_ge(gates_read, KT)
                        else:
                            pe.wait_ge(attn_done, 2 * g)
                    at = (h % 2) * HEAD_DIM
                    v = v_sb[:, :, g * HEAD_DIM:(g + 1) * HEAD_DIM]
                    dst = ps[at:at + HEAD_DIM, 2 + tile_no % 2, :]
                    pe.matmul(dst[:, 0:P], v[:, 0], prob[:, h, 0:P], start=True, stop=True)
                    pe.matmul(dst[:, P:2 * P], v[:, 0], prob[:, h, P:2 * P], start=True, stop=False)
                    mm = pe.matmul(dst[:, P:2 * P], v[:, 1], prob[:, h, 2 * P:3 * P], start=False, stop=True)
                    mm.then_inc(pv_ps, 1)

            for u in range(len(LY) + len(GL) + len(GA)):
                if u == 2:
                    gates(1)
                if u % 2 and 3 <= u <= 9:
                    weighted_values((u - 3) // 2)
                if u % 2 and u <= 7:
                    scores((u - 1) // 2)
                project_tile(10 + u, 0)
                if u % 2 == 0 and 2 <= u <= 8:
                    transposes((u - 2) // 2)
                project_tile(10 + u, 1)

            def vector_rows(v, part):
                n = ADA_B[v][part]
                wait_chunk(pe, n)
                w = ring[:, n % RING, :].rearrange("p (k n) -> p k n", k=2)
                for k in range(2):
                    kt = 2 * part + k
                    for c in range(4):
                        mm = pe.matmul(ps[32 * c:32 * (c + 1), ROW_BANK[v], ROW_AT[v]:ROW_AT[v] + 256],
                                       silu_c[:, kt:kt + 1].broadcast_to([P, 32]), w[:, k, 256 * c:256 * (c + 1)],
                                       start=(kt == 0), stop=(kt == KT - 1), tile_position=(0, 32 * c))
                mm.then_inc(chunk_used, 1)

            def spread(v):
                for c in range(4):
                    mm = pe.matmul(ps[:, 6 + c // 2, 256 * (c % 2):256 * (c % 2 + 1)],
                                   ident[:, 32 * c:32 * c + 1].broadcast_to([P, P]), mod_row[:, v, :], start=True, stop=True)
                mm.then_inc(bc_ps, 1)

            pe.wait_ge(prob_t_done, HEADS)
            for v in (SH2, G1):
                for part in range(4):
                    vector_rows(v, part)

            pe.wait_ge(gate_in, 2 * KT)
            pe.wait_ge(attn_done, KT)
            pe.wait_ge(x_again, 16 * 5)
            for q in range(4):
                pe.matmul(ps[:, q, :], ones[32 * q:32 * q + 1, :], b_out[32 * q:32 * q + 1, :], start=True, stop=False,
                          tile_position=(32 * q, 0))
            for i, n in enumerate(WO):
                wait_chunk(pe, n)
                w = ring[:, n % RING, :].rearrange("p (k n) -> p k n", k=2)
                for k in (2 * i, 2 * i + 1):
                    pe.wait_ge(merged, k + 1)
                    for t in range(TT):
                        for c in range(2):
                            mm = pe.matmul(ps[:, 2 * t + c, :], attn[:, k, t * P:(t + 1) * P],
                                           w[:, k % 2, 512 * c:512 * (c + 1)], start=False, stop=(k == KT - 1))
                mm.then_inc(chunk_used, 1)
                if i == 0:
                    pe.wait_ge(mod_row_done, 1)
                    spread(SH2)
                if i == 1:
                    pe.wait_ge(bc_done, 1)
                    spread(G1)

            def turn_h2(t):
                pe.wait_ge(h2_done, t + 1)
                for f in range(KT):
                    mm = pe.transpose(ps[:, 2 * t + f // 4, (f % 4) * P:(f % 4 + 1) * P],
                                      h2[:, t, f * P:(f + 1) * P], ident[:, :])
                mm.then_inc(h2_t_ps, 1)

            for part in range(4):
                vector_rows(SC2, part)
            vector_rows(GT2, 0)
            pe.wait_ge(mod_row_done, 2)
            pe.wait_ge(bc_done, 2)
            spread(SC2)
            vector_rows(GT2, 1)
            turn_h2(0)
            vector_rows(GT2, 2)
            vector_rows(GT2, 3)
            turn_h2(1)
            pe.wait_ge(h2_t_act, 2)
            pe.wait_ge(h2_t_dve, 2)
            for k in range(KT):
                c = k % 4
                mm = pe.matmul(ps[32 * c:32 * (c + 1), 5, 0:T], w_rt[:, k, :], h2_t[:, k, :], start=(k < 4), stop=(k >= 4),
                               tile_position=(0, 32 * c))
            mm.then_inc(part_ps, 1)
            pe.wait_ge(part_done, 1)
            pe.wait_ge(mod_row_done, 3)
            for t in range(TT):
                mm = pe.matmul(ps[:, 4, t * EXPERTS:(t + 1) * EXPERTS], logit_part[:, t * P:(t + 1) * P], fold[:, :],
                               start=True, stop=True)
            mm.then_inc(logits_ps, 1)
            spread(GT2)
            pe.wait_ge(route_done, 1)
            pe.matmul(ps[:, 5, 0:EXPERTS], before[:, :], hit_b[:, 0, :], start=True, stop=True)
            pe.matmul(ps[:, 5, EXPERTS:2 * EXPERTS], ones_b[:, :], hit_b[:, 0, :], start=True, stop=False)
            pe.matmul(ps[:, 5, EXPERTS:2 * EXPERTS], before[:, :], hit_b[:, 1, :], start=False, stop=True)
            pe.matmul(ps[:, 5, 2 * EXPERTS:3 * EXPERTS], ones_b[:, :], hit_b[:, 0, :], start=True, stop=False)
            pe.matmul(ps[:, 5, 2 * EXPERTS:3 * EXPERTS], ones_b[:, :], hit_b[:, 1, :], start=False,
                      stop=True).then_inc(rank_ps, 1)
            pe.wait_ge(route_done, 2)
            for t in range(TT):
                mm = pe.transpose(ps[0:EXPERTS, 4, t * P:(t + 1) * P], route_w[:, t, :], ident[:, :])
            mm.then_inc(route_t_ps, 1)

            def gather(count):
                pe.wait_ge(picked, count)
                for k in range(KT):
                    for t in range(TT):
                        mm = pe.matmul(ps[:, 7, k * BLOCK:(k + 1) * BLOCK], h2[:, t, k * P:(k + 1) * P], pick[:, t, :],
                                       start=(t == 0), stop=(t == TT - 1))
                mm.then_inc(gathered, 1)

            def combine():
                for t in range(TT):
                    for c in range(2):
                        mm = pe.matmul(ps[:, 2 * t + c, :], scat_t[64 * c:64 * (c + 1), t, :], o_sb[64 * c:64 * (c + 1), :],
                                       start=False, stop=False, skip_group_check=True, tile_position=(64 * c, 0))
                mm.then_inc(combined, 1)

            pe.wait_ge(bc_done, 3)
            gather(1)
            pe.wait_ge(route_t_done, 1)
            pe.wait_ge(moe_loaded, 32)
            for t in range(TT):
                for c in range(2):
                    mm = pe.matmul(ps[:, 2 * t + c, :], route_wt[:, t * P:(t + 1) * P], b_e2[:, 512 * c:512 * (c + 1)],
                                   start=True, stop=False, skip_group_check=True)
            mm.then_inc(combined, 1)
            pe.wait_ge(combined, 1)
            pe.wait_ge(rank_done, 1)

            def experts(turn, q, p):
                for r in range(UNROLL):
                    done = turn * UNROLL + r
                    for b in range(2):
                        for c in range(2):
                            pe.matmul(ps[64 * c:64 * (c + 1), 4 + b, :], bias_pick[:, :],
                                      b_e1[0:EXPERTS, b * D + 512 * c:b * D + 512 * (c + 1)], start=True, stop=False,
                                      tile_position=(0, 64 * c))
                    for k in range(KT):
                        if k == 0:
                            pe.wait_ge(hsel_done, done + 1)
                        wait_expert_chunk(pe, r, k, turn)
                        w = ring[:, expert_slot(r, k), :]
                        for b in range(2):
                            for c in range(2):
                                mm = pe.matmul(ps[64 * c:64 * (c + 1), 4 + b, :], hsel[:, k, :],
                                               w[:, b * D + 512 * c:b * D + 512 * (c + 1)], start=False, stop=(k == KT - 1),
                                               tile_position=(0, 64 * c))
                        mm.then_inc(chunk_used, 1)
                    gather(done + 2)
                    pe.wait_ge(o_done, done + 1)
                    combine()
                    pe.wait_ge(act_done, done + 1)
                    for c in range(4):
                        mm = pe.transpose(ps[:, 6 - c // 2, c % 2 * P:(c % 2 + 1) * P], g_u[:, c * P:(c + 1) * P], ident[:, :])
                    mm.then_inc(act_t_ps, 1)
                    for t in range(TT):
                        mm = pe.transpose(ps[:, 4, t * P:(t + 1) * P], scat[:, t].rearrange("p a s -> p (a s)"), ident[:, :])
                    mm.then_inc(act_t_ps, 1)
                    pe.wait_ge(act_t_a, done + 1)
                    pe.wait_ge(act_t_d, done + 1)
                    for k in range(KT):
                        if k % 2 == 0:
                            wait_expert_chunk(pe, r, E1_CHUNKS + k // 2, turn)
                        w = ring[:, expert_slot(r, E1_CHUNKS + k // 2), :]
                        for c in range(2):
                            mm = pe.matmul(ps[64 * c:64 * (c + 1), 6, :], act_t[:, k % 4, k // 4, :],
                                           w[:, (k % 2) * D + 512 * c:(k % 2) * D + 512 * (c + 1)],
                                           start=(k == 0), stop=(k == KT - 1), tile_position=(0, 64 * c))
                        if k % 2:
                            mm.then_inc(chunk_used, 1)
                    pe.wait_ge(scat_t_done, done + 1)

            more = all_experts(pe, experts)
            pe.wait_ge(o_done, more * EXPERTS + (EXPERTS + 1))
            combine()

        @block.vector
        def _(dve):
            steps = [0]

            def step(ins):
                ins.then_inc(dve_step, 1)
                steps[0] += 1
                return steps[0]

            def then(n=None):
                dve.wait_ge(dve_step, steps[0] if n is None else n)

            dve.memset(eps[:, :], EPS).then_inc(eps_set, 1)
            dve.wait_ge(x_sq, 1)
            step(dve.reciprocal(stats[:, 2:4], stats[:, 0:2]))
            then()
            for t in range(TT):
                dve.tensor_scalar(x_n[:, t, :], x_in[:, t, :], stats[:, 2 + t:3 + t], None, ALU.mult).then_inc(xn_done, 1)
            dve.wait_ge(pool_set, 4)
            for q in range(4):
                dve.tensor_copy(fold[32 * q:32 * (q + 1), :], ident[32 * q:32 * (q + 1), 32 * q:32 * (q + 1)])
            dve.tensor_copy(expert_hot[:, 0:EXPERTS], ident[0:EXPERTS, 0:EXPERTS])
            step(dve.tensor_copy(expert_hot[:, EXPERTS:], ident[0:EXPERTS, 0:1]))
            dve.wait_ge(rows_t, 1)
            dve.tensor_copy(cols_qk[:, :], ps[:, 1, P:P + 10]).then_inc(cols_done, 1)
            dve.tensor_copy(cols[:, :], ps[:, 1, 0:P]).then_inc(cols_done, 1)
            dve.wait_ge(cols_done, 2)
            dve.wait_ge(c_sig, 1)
            dve.tensor_tensor(silu_c[:, :], cols[:, R_C:R_C + KT], silu_c[:, :], ALU.mult).then_inc(silu_done, 1)
            ang, turns_, red = tmp_a, sin_t, cos_t
            dve.wait_ge(small_loaded, 16 * 5)
            step(dve.tensor_copy(ang, tmp_b.bitcast(I32)))
            step(dve.tensor_scalar(neg_sinks[:, :], sinks[:, :], -1.0, None, ALU.mult))
            then()
            step(dve.tensor_scalar(ang, ang, freq[:, 0:1], None, ALU.mult))
            then()
            step(dve.tensor_scalar(turns_, ang, 1.0 / (2.0 * np.pi), 12582912.0, ALU.mult, ALU.add))
            then()
            step(dve.tensor_scalar(turns_, turns_, 12582912.0, None, ALU.subtract))
            two_pi = 2.0 * np.pi
            hi = 6.28125
            mid = float(np.float32(np.round((two_pi - hi) * 2 ** 20) / 2 ** 20))
            lo = float(np.float32(two_pi - hi - mid))
            src = ang
            for part in (hi, mid, lo):
                then()
                step(dve.scalar_tensor_tensor(red, turns_, -part, src, ALU.mult, ALU.add))
                src = red
            then()
            dve.tensor_scalar(red, red, 3.1415925, -3.1415925, ALU.min, ALU.max).then_inc(angle_done, 1)
            dve.wait_ge(chunk_used, N_ADA_A)
            dve.tensor_copy(mod_a_rows, ps[:, 0, :]).then_inc(mod_rows, 1)
            dve.wait_ge(mod_cols, 1)
            step(dve.tensor_tensor(mod_a[:, :].rearrange("p (c j) -> p c j", c=4),
                                   ps[:, 1, :].rearrange("p (j c x) -> p c j x", j=4, c=4)[:, :, :, 0],
                                   cols[:, R_BADA:R_BADA + 2 * KT].rearrange("p (c j) -> p c j", c=4), ALU.add))
            then()
            dve.scalar_tensor_tensor(mod_a[:, KT:], mod_a[:, KT:], 1.0, cols[:, R_GPRE:R_GPRE + KT], ALU.add,
                                     ALU.mult).then_inc(mod_done, 1)
            dve.wait_ge(mod_done, 1)
            dve.wait_ge(xn_t, TT)
            for k in range(KT // 2):
                dve.tensor_scalar(h_t[:, k, :], ps[:, 4 + k // 2, (k % 2) * T:(k % 2 + 1) * T], mod_a[:, KT + k:KT + k + 1], mod_a[:, k:k + 1],
                                  ALU.mult, ALU.add).then_inc(h_dve, 1)
            dve.wait_ge(sin_done, 2)
            step(dve.tensor_tensor(tmp_a, tmp_a, tmp_a, ALU.mult))
            for quad in (0, 2):
                step(dve.tensor_scalar(sin_t[32 * quad:32 * (quad + 1), :], sin_t[32 * quad:32 * (quad + 1), :], -1.0, None,
                                       ALU.mult))
            then()
            dve.tensor_scalar(cos_t, tmp_a, -2.0, 1.0, ALU.mult, ALU.add).then_inc(rope_done, 1)

            dve.wait_ge(sp_done, 1)
            for i, f in enumerate((-LRU_C, LRU_C)):
                ins = dve.tensor_scalar(decay[:, i, :], stats[:, 4:12], f, None, ALU.mult)
            ins.then_inc(decay_done, 1)

            def conv(c):
                dve.wait_ge(proj_read, c + 1)
                for tap in range(CONV - 1, -1, -1):
                    if tap < CONV - 1:
                        then()
                    for n in (2 * c, 2 * c + 1):
                        w = cols[:, R_CONVW + KT * tap + n:R_CONVW + KT * tap + n + 1]
                        if tap == CONV - 1:
                            ins = dve.tensor_scalar(xc[:, n, :], lx[:, n, tap:tap + T], w,
                                                    cols[:, R_CONVB + n:R_CONVB + n + 1], ALU.mult, ALU.add)
                        else:
                            ins = dve.scalar_tensor_tensor(xc[:, n, :], lx[:, n, tap:tap + T], w, xc[:, n, :], ALU.mult, ALU.add)
                        if tap:
                            step(ins)
                        else:
                            ins.then_inc(conv_done, 1)

            def rope(c):
                raw = qk_raw[:, c % 2]
                dst = q_r[:, 2 * c:2 * c + 2, :] if c < 4 else k_r
                dve.wait_ge(proj_read, len(LX) + c + 1)
                dve.wait_ge(rope_done, 1)
                if c:
                    dve.wait_ge(rope_q, c)
                for quad in range(4):
                    other = quad ^ 1
                    ins = dve.tensor_copy(swap[32 * quad:32 * (quad + 1)], raw[32 * other:32 * (other + 1)])
                ins.then_inc(swapped, 1)
                step(dve.tensor_tensor(dst, raw, cos_t[:, None, :].broadcast_to([P, 2, T]), ALU.mult))
                dve.wait_ge(times_sin, c + 1)
                then()
                dve.tensor_tensor(dst, dst, swap, ALU.add).then_inc(rope_q, 1)

            for c in range(4):
                conv(c)
            for c in range(5):
                rope(c)
            dve.wait_ge(rope_q, 5)
            for g in range(KV_HEADS):
                for half in range(2):
                    ins = dve.tensor_copy(k_rep[64 * half:64 * (half + 1), g, :], k_r[64 * (g % 2):64 * (g % 2 + 1), g // 2, :])
            ins.then_inc(k_rep_done, 1)
            dve.wait_ge(chunk_used, VC + 1)
            dve.tensor_tensor(v_sb[:, :, :], ps[:, 1, :].rearrange("p (t n) -> p t n", t=TT),
                              b_v[:, None, :].broadcast_to([P, TT, PROJ_W]), ALU.add).then_inc(v_done, 1)

            def lru_squares(b):
                for n in range(4):
                    dve.wait_ge(th_done, 4 * b + n + 1)
                    step(dve.tensor_tensor(lru_tmp[:, n % 2, :], g_a[:, n, :], g_a[:, n, :], ALU.mult))
                    then()
                    dve.scalar_tensor_tensor(g_r[:, n, :], lru_tmp[:, n % 2, :], 1.0, g_r[:, n, :], ALU.add,
                                             ALU.mult).then_inc(m2_done, 1)

            def lru_states(b):
                for n in range(4):
                    dve.wait_ge(mult_done, b + 1)
                    dve.wait_ge(ix_done, 4 * b + n + 1)
                    dve.tensor_tensor(g_i[:, n, :], g_i[:, n, :], g_r[:, n, :], ALU.mult).then_inc(u_done, 1)
                for n in range(4):
                    dve.wait_ge(u_done, 4 * b + n + 1)
                    dve.tensor_tensor_scan(xc[:, 4 * b + n, :], g_a[:, n, :], g_i[:, n, :], 0.0, ALU.mult,
                                           ALU.add).then_inc(state_done, 1)

            def softmax_max(g):
                dve.wait_ge(scores_ps, g + 1)
                if g:
                    dve.wait_ge(pv_ps, GROUP * g)
                for h in range(GROUP):
                    dve.tensor_tensor_reduce(prob[:, h, 0:P], ps[:, 4 + h, 0:P], mask[:, 1, :], 1.0, NEG, ALU.add, ALU.max,
                                             smax[:, h, 0:1])
                    ins = dve.tensor_tensor_reduce(prob[:, h, P:3 * P], ps[:, 4 + h, P:3 * P],
                                                   mask[:, :, :].rearrange("p a b -> p (a b)"), 1.0, NEG,
                                                   ALU.add, ALU.max, smax[:, h, 1:2])
                step(ins)
                then()
                step(dve.tensor_scalar(smax[:, :, :], smax[:, :, :], -HEAD_DIM ** -0.5, None, ALU.mult))
                then()
                sink = sinks[:, GROUP * g:GROUP * (g + 1), None].broadcast_to([P, GROUP, 2])
                nsink = neg_sinks[:, GROUP * g:GROUP * (g + 1), None].broadcast_to([P, GROUP, 2])
                step(dve.tensor_tensor(smax[:, :, :], smax[:, :, :], nsink, ALU.min))
                then()
                dve.tensor_tensor(snk[:, :, :], smax[:, :, :], sink, ALU.add).then_inc(smax_done, 1)

            def softmax_scale(g):
                dve.wait_ge(exp_done, g + 1)
                step(dve.tensor_tensor(ssum[:, :, :], ssum[:, :, :], snk[:, :, :], ALU.add))
                then()
                step(dve.reciprocal(ssum[:, :, :], ssum[:, :, :]))
                then()
                for h in range(GROUP):
                    dve.tensor_scalar(prob[:, h, 0:P], prob[:, h, 0:P], ssum[:, h, 0:1], None, ALU.mult)
                    dve.tensor_scalar(prob[:, h, P:3 * P], prob[:, h, P:3 * P], ssum[:, h, 1:2], None,
                                      ALU.mult).then_inc(prob_done, 1)

            def attn_out(g):
                for m in range(2 * g, 2 * g + 2):
                    dve.wait_ge(pv_ps, 2 * m + 2)
                    dve.wait_ge(lg_done, m + 1)
                    dve.tensor_copy(attn[:, m, :], ps[:, 2 + m % 2, 0:T]).then_inc(attn_done, 1)

            def gelu_in(n):
                i = n % 2
                dve.wait_ge(ly_in, n + 1)
                step(dve.tensor_scalar(ly2[:, i, :], ly2[:, i, :], GELU_A, 1.0, ALU.mult, ALU.add))
                then()
                dve.tensor_tensor(ly2[:, i, :], ly2[:, i, :], ly[:, i, :], ALU.mult).then_inc(z_done, 1)

            def gelu_out(n):
                dve.wait_ge(zsig_done, n + 1)
                dve.tensor_tensor(attn[:, n, :], ly[:, n % 2, :], sg[:, n % 2, :], ALU.mult).then_inc(gelu_done, 1)

            def state_gelu(n):
                dve.wait_ge(state_done, n + 1)
                dve.wait_ge(gelu_done, n + 1)
                dve.tensor_tensor(xc[:, n, :], xc[:, n, :], attn[:, n, :], ALU.mult).then_inc(lg_done, 1)

            def gate_lru(n):
                dve.wait_ge(gate_in, n + 1)
                dve.wait_ge(lg_done, n + 1)
                dve.tensor_tensor(xc[:, n, :], gate[:, n % 2, :], xc[:, n, :], ALU.mult).then_inc(gate_used, 1)

            def gate_attn(n):
                dve.wait_ge(gate_in, KT + n + 1)
                dve.wait_ge(attn_done, n + 1)
                dve.tensor_tensor(attn[:, n, :], gate[:, n % 2, :], attn[:, n, :], ALU.mult).then_inc(gate_used, 1)
                dve.wait_ge(gate_used, KT + n + 1)
                dve.tensor_tensor(attn[:, n, :], attn[:, n, :], xc[:, n, :], ALU.add).then_inc(merged, 1)

            lru_squares(0)
            gelu_in(0)
            lru_states(0)
            gelu_out(0)
            gelu_in(1)
            gelu_out(1)
            state_gelu(0)
            state_gelu(1)
            softmax_max(0)
            softmax_scale(0)
            for n in (2, 3):
                gelu_in(n)
                gelu_out(n)
                state_gelu(n)
            gelu_in(4)
            gelu_out(4)
            lru_squares(1)
            gelu_in(5)
            gelu_out(5)
            attn_out(0)
            softmax_max(1)
            lru_states(1)
            softmax_scale(1)
            for n in (6, 7):
                gelu_in(n)
                gelu_out(n)
            for n in range(4, 8):
                state_gelu(n)
            gate_lru(0)
            gate_lru(1)
            for g in (2, 3):
                attn_out(g - 1)
                softmax_max(g)
                softmax_scale(g)
                for n in range(4 * g - 6, 4 * g - 2):
                    if n < KT:
                        gate_lru(n)
            gate_attn(0)
            gate_attn(1)
            attn_out(3)
            for n in range(2, KT):
                gate_attn(n)

            dve.wait_ge(late_loaded, 16 * 28)
            dve.wait_ge(chunk_used, ADA_B[G1][-1] + 1)
            step(dve.tensor_tensor(mod_row[:, 0:2, :], ps[:, 4, :].rearrange("p (v n) -> p v n", v=2), bada_row[:, 0:2, :], ALU.add))
            then()
            dve.tensor_tensor(mod_row[:, G1, :], mod_row[:, G1, :], gain_row[:, G1, :], ALU.mult).then_inc(mod_row_done, 1)

            def y_tile(t):
                return ps[:, 2 * t:2 * t + 2, :].rearrange("p a b -> p (a b)")

            bc_tile = ps[:, 6:8, :].rearrange("p a b -> p (a b)")
            dve.wait_ge(chunk_used, WO[-1] + 1)
            dve.wait_ge(bc_done, 2)
            for t in range(TT):
                dve.wait_ge(y_sq, t + 1)
                step(dve.reciprocal(stats[:, 2 + t:3 + t], stats[:, t:t + 1]))
                then()
                step(dve.scalar_tensor_tensor(y_g[:, t, :], y_tile(t), stats[:, 2 + t:3 + t], g1_bc, ALU.mult, ALU.mult))
                then()
                dve.tensor_tensor(x1[:, t, :], x1[:, t, :], y_g[:, t, :], ALU.add).then_inc(x1_done, 1)
            dve.wait_ge(chunk_used, ADA_B[SC2][-1] + 1)
            step(dve.scalar_tensor_tensor(mod_row[:, SC2, :], ps[:, 5, 0:256], 1.0, bada_row[:, SC2, :], ALU.add, ALU.add))
            then()
            dve.tensor_tensor(mod_row[:, SC2, :], mod_row[:, SC2, :], gain_row[:, SC2, :], ALU.mult).then_inc(mod_row_done, 1)
            dve.wait_ge(x1_sq, TT)
            step(dve.reciprocal(stats[:, 6:8], stats[:, 4:6]))
            dve.wait_ge(bc_ps, 3)
            for t in range(TT):
                then()
                step(dve.scalar_tensor_tensor(h2[:, t, :], x1[:, t, :], stats[:, 6 + t:7 + t], bc_tile, ALU.mult, ALU.mult))
                then()
                dve.tensor_tensor(h2[:, t, :], h2[:, t, :], sh2_bc, ALU.add).then_inc(h2_done, 1)
            dve.wait_ge(chunk_used, ADA_B[GT2][-1] + 1)
            step(dve.tensor_tensor(mod_row[:, GT2, :], ps[:, 4, 0:256], bada_row[:, GT2, :], ALU.add))
            then()
            dve.tensor_tensor(mod_row[:, GT2, :], mod_row[:, GT2, :], gain_row[:, GT2, :], ALU.mult).then_inc(mod_row_done, 1)
            for t in range(TT):
                dve.wait_ge(h2_t_ps, t + 1)
                dve.tensor_copy(h2_t[:, 0:4, t * P:(t + 1) * P], ps[:, 2 * t, :].rearrange("p (k t) -> p k t", k=4)).then_inc(h2_t_dve, 1)
            dve.wait_ge(part_ps, 1)
            dve.tensor_copy(logit_part, ps[:, 5, 0:T]).then_inc(part_done, 1)
            dve.wait_ge(h2_done, TT)
            dve.memset(z_q[:, 1024:1792], 0.0).then_inc(o_done, 1)

            dve.wait_ge(logits_ps, 1)
            step(dve.tensor_tensor(logits[:, :, :], ps[:, 4, 0:TT * EXPERTS].rearrange("p (t e) -> p t e", t=TT),
                                   b_rt[:, None, :].broadcast_to([P, TT, EXPERTS]), ALU.add))
            then()
            for t in range(TT):
                step(dve.max(top8[:, t, :], logits[:, t, :]))
            then()
            dve.tensor_scalar(neg_max[:, :, :], top8[:, :, 0:1], -1.0, None, ALU.mult).then_inc(top_done, 1)
            for t in range(TT):
                step(dve.max_index(top_i[:, t, :], top8[:, t, :], logits[:, t, :]))
            then()
            step(dve.tensor_copy(top_f[:, :, :], top_i[:, :, :]))
            then()
            for t in range(TT):
                step(dve.tensor_tensor(match[:, t, :, :], expert_no[:, None, :].broadcast_to([P, TOP_K, EXPERTS]),
                                       top_f[:, t, 0:TOP_K, None].broadcast_to([P, TOP_K, EXPERTS]), ALU.is_equal))
            then()
            step(dve.tensor_tensor(match[:, :, 0:2, :], match[:, :, 0:2, :], match[:, :, 2:4, :], ALU.add))
            then()
            step(dve.tensor_tensor(hit[:, :, :], match[:, :, 0, :], match[:, :, 1, :], ALU.add))
            then()
            dve.tensor_copy(hit_b[:, :, :], hit[:, :, :]).then_inc(route_done, 1)
            dve.wait_ge(topexp_done, TT)
            for t in range(TT):
                step(dve.tensor_tensor_reduce(route_w[:, t, :], soft[:, t, :], hit[:, t, :], 1.0, 0.0, ALU.mult, ALU.add,
                                              sums[:, t, 0:1]))
            then()
            step(dve.reciprocal(sums[:, :, :], sums[:, :, :]))
            then()
            dve.tensor_tensor(route_w[:, :, :], route_w[:, :, :], sums[:, :, :].broadcast_to([P, TT, EXPERTS]),
                              ALU.mult).then_inc(route_done, 1)
            dve.wait_ge(rank_ps, 1)
            step(dve.reduce_max(passes_f[:, 0:1], ps[:, 5, 2 * EXPERTS:3 * EXPERTS], axis=AX.X))
            step(dve.scalar_tensor_tensor(rank[:, :, 0:EXPERTS], ps[:, 5, 0:2 * EXPERTS].rearrange("p (t e) -> p t e", t=TT), 1.0,
                                          hit[:, :, :], ALU.add, ALU.mult))
            then()
            step(dve.tensor_scalar(rank[:, :, 0:EXPERTS], rank[:, :, 0:EXPERTS], 1.0, None, ALU.subtract))
            for i in range(1, PASSES):
                step(dve.tensor_scalar(passes_f[:, i:i + 1], passes_f[:, 0:1], float(i * BLOCK), None, ALU.is_gt))
            then()
            step(dve.tensor_scalar(rank[:, :, EXPERTS:], rank[:, :, 0:1], float(BLOCK), None, ALU.subtract))

            def pick_tokens(e):
                for t in range(TT):
                    dve.tensor_scalar(pick[:, t, :], slot_no[:, 0, :], rank[:, t, e], None, ALU.is_equal)
                dve.tensor_scalar(bias_pick[:, :], ones[0:EXPERTS, 0:BLOCK], expert_hot[:, e], None, ALU.mult).then_inc(picked, 1)

            pick_tokens(slice(0, 1))
            step(dve.tensor_tensor(passes_f[:, 1:2], passes_f[:, 1:2], passes_f[:, 2:3], ALU.add))
            then()
            dve.wait_ge(route_t_ps, 1)
            dve.tensor_copy(route_wt[:, :], ps[0:EXPERTS, 4, 0:T]).then_inc(route_t_done, 1)
            dve.tensor_tensor(more_i[:, :], passes_f[:, 1:2], passes_f[:, 3:4], ALU.add).then_inc(rank_done, 1)
            dve.wait_ge(gathered, 1)
            dve.tensor_copy(hsel[:, :, :], ps[:, 7, :].rearrange("p (k s) -> p k s", k=KT)).then_inc(hsel_done, 1)

            def experts(turn, q, p):
                for r in range(UNROLL):
                    done = turn * UNROLL + r
                    e = q * UNROLL + r
                    if p is not None and r == 0:
                        dve.wait_ge(rank_done, p + 2)
                    dve.wait_ge(chunk_used, turn * (UNROLL * EXPERT_CHUNKS) + (MIXER_CHUNKS + r * EXPERT_CHUNKS + 1))
                    for t in range(TT):
                        dve.tensor_scalar(scat[:, t].rearrange("p a s -> p (a s)"), slot_no[:, :, :].rearrange("p a s -> p (a s)"),
                                          rank[:, t, bass.ds(e, 1)], route_w[:, t, bass.ds(e, 1)], ALU.is_equal, ALU.mult)
                    pick_tokens(bass.ds(e + 1, 1))
                    dve.wait_ge(chunk_used, turn * (UNROLL * EXPERT_CHUNKS) + MIXER_CHUNKS + r * EXPERT_CHUNKS + E1_CHUNKS)
                    dve.tensor_scalar(g_c, ps[:, 4, :], LIMIT, None, ALU.min).then_inc(g_done, 1)
                    dve.tensor_scalar(u_c, ps[:, 5, :], LIMIT, -LIMIT, ALU.min, ALU.max).then_inc(g_done, 1)
                    dve.wait_ge(g_done, done * 3 + 2)
                    dve.scalar_tensor_tensor(u_c, u_c, 1.0, g_c, ALU.add, ALU.mult).then_inc(g_done, 1)
                    dve.wait_ge(sig_done, done + 1)
                    dve.wait_ge(g_done, done * 3 + 3)
                    dve.tensor_tensor(g_u, u_c, s_g, ALU.mult).then_inc(act_done, 1)
                    dve.wait_ge(gathered, done + 2)
                    dve.tensor_copy(hsel[:, :, :], ps[:, 7, :].rearrange("p (k s) -> p k s", k=KT)).then_inc(hsel_done, 1)
                    dve.wait_ge(act_t_ps, done * 2 + 1)
                    dve.tensor_copy(act_t[:, 0:2].rearrange("p a b c -> p (a b c)"), ps[:, 6, 0:T]).then_inc(act_t_d, 1)
                    dve.wait_ge(chunk_used, turn * (UNROLL * EXPERT_CHUNKS) + MIXER_CHUNKS + (r + 1) * EXPERT_CHUNKS)
                    dve.tensor_copy(o_sb, ps[:, 6, :]).then_inc(o_done, 1)

            def next_pass(p):
                dve.wait_ge(picked, (p + 1) * EXPERTS + 1)
                dve.tensor_scalar(rank[:, :, :], rank[:, :, :], float(BLOCK), None, ALU.subtract).then_inc(rank_done, 1)

            more = all_experts(dve, experts, next_pass)

            dve.wait_ge(combined, more * EXPERTS + (EXPERTS + 2))
            for t in range(TT):
                dve.wait_ge(y2_sq, t + 1)
                step(dve.reciprocal(stats[:, 10 + t:11 + t], stats[:, 8 + t:9 + t]))
                then()
                step(dve.scalar_tensor_tensor(fin[:, t, :], ps[:, 2 * t:2 * t + 2, :].rearrange("p a b -> p (a b)"),
                                              stats[:, 10 + t:11 + t], g2_bc, ALU.mult, ALU.mult))
                then()
                dve.tensor_tensor(fin[:, t, :], fin[:, t, :], x1[:, t, :], ALU.add).then_inc(fin_done, 1)

        @block.scalar
        def _(act):
            def load(dst, src, s):
                act.dma_start(dst, src).then_inc(s, 16)

            load(x_in, a["x"][0].rearrange("(t p) d -> p t d", p=P), x_loaded)
            load(tmp_b.bitcast(I32), a["positions"][0:1, :].broadcast_to([P, T]), small_loaded)
            load(sinks[:, :], a["sinks"][0:1, :].broadcast_to([P, HEADS]), small_loaded)
            load(b_v[:, :], a["b_in"][0:1, V0:V0 + PROJ_W].broadcast_to([P, PROJ_W]), small_loaded)
            load(b_rt[:, :], a["b_router"][0:1, :].broadcast_to([P, EXPERTS]), small_loaded)
            load(w_rt[:, :, :], a["w_router"][0].rearrange("(k p) e -> p k e", p=P), small_loaded)

            act.wait_ge(eps_set, 1)
            act.wait_ge(x_loaded, 16)
            for t in range(TT):
                ins = act.activation(x_n[:, t, :], x_in[:, t, :], ACT.Square, accum_out=stats[:, t:t + 1])
            ins.then_inc(act_step, 1)
            act.wait_ge(act_step, 1)
            act.activation(stats[:, 0:2], stats[:, 0:2], ACT.Sqrt, bias=eps[:, 0:1], scale=1.0 / D).then_inc(x_sq, 1)
            act.wait_ge(cols_done, 2)
            act.activation(silu_c[:, :], cols[:, R_C:R_C + KT], ACT.Sigmoid).then_inc(c_sig, 1)
            act.activation(stats[:, 4:12], cols[:, R_LRUA:R_LRUA + KT], ACT.Exp).then_inc(act_step, 1)
            act.wait_ge(act_step, 2)
            act.activation(stats[:, 4:12], stats[:, 4:12], ACT.Ln, bias=1.0).then_inc(sp_done, 1)
            act.wait_ge(angle_done, 1)
            act.activation(sin_t, cos_t, ACT.Sin).then_inc(sin_done, 1)
            act.activation(tmp_a, cos_t, ACT.Sin, scale=0.5).then_inc(sin_done, 1)
            act.wait_ge(mod_done, 1)
            act.wait_ge(xn_t, TT)
            for k in range(KT // 2, KT):
                act.activation(h_t[:, k, :], ps[:, 4 + k // 2, (k % 2) * T:(k % 2 + 1) * T], ACT.Identity, bias=mod_a[:, k:k + 1],
                               scale=mod_a[:, KT + k:KT + k + 1]).then_inc(h_act, 1)

            act.wait_ge(pad_set, 1)
            def bias_in(base, n):
                at = R_BIN + (base - LX0) // P + n
                return cols[:, at:at + 1]

            for c in range(4):
                act.wait_ge(chunk_used, LX[c] + 1)
                for i in range(2):
                    ins = act.activation(lx[:, 2 * c + i, CONV - 1:], ps[:, c % 2, i * T:(i + 1) * T], ACT.Identity,
                                         bias=bias_in(LX0, 2 * c + i))
                ins.then_inc(proj_read, 1)
            for c in range(5):
                act.wait_ge(chunk_used, (QC[c] if c < 4 else KC) + 1)
                if c >= 2:
                    act.wait_ge(rope_q, c - 1)
                for i in range(2):
                    ins = act.activation(qk_raw[:, c % 2, i, :], ps[:, c % 2, i * T:(i + 1) * T], ACT.Identity,
                                         bias=cols_qk[:, 2 * c + i:2 * c + i + 1])
                ins.then_inc(proj_read, 1)

            def gate_sigmoids(b):
                for n in range(4 * b, 4 * b + 4):
                    if n % 4 == 3:
                        act.wait_ge(chunk_used, GATES[b] + 1)
                    else:
                        act.wait_ge(gates_ps, 3 * b + n % 4 + 1)
                    if n == 4:
                        act.wait_ge(state_done, 4)
                    act.activation(g_r[:, n % 4, :], ps[:, 2 + n % 2, 0:T], ACT.Sigmoid, bias=cols[:, R_BRG + n:R_BRG + n + 1])
                    act.activation(g_i[:, n % 4, :], ps[:, 2 + n % 2, T:2 * T], ACT.Sigmoid,
                                   bias=cols[:, R_BIG + n:R_BIG + n + 1]).then_inc(gates_read, 1)

            def gate_powers(b):
                act.wait_ge(decay_done, 1)
                for n in range(4 * b, 4 * b + 4):
                    act.wait_ge(gates_read, n + 1)
                    act.activation(g_a[:, n % 4, :], g_r[:, n % 4, :], ACT.Exp, scale=decay[:, 0, n:n + 1]).then_inc(a_done, 1)
                for n in range(4 * b, 4 * b + 4):
                    act.wait_ge(a_done, n + 1)
                    act.activation(g_r[:, n % 4, :], g_r[:, n % 4, :], ACT.Tanh, scale=decay[:, 1, n:n + 1]).then_inc(th_done, 1)

            def gate_roots(b):
                act.wait_ge(m2_done, 4 * b + 4)
                act.activation(z_gate[:, 0:1024], z_gate[:, 0:1024], ACT.Sqrt).then_inc(mult_done, 1)

            def exps(g):
                act.wait_ge(smax_done, g + 1)
                for h in range(GROUP):
                    for b, sl in ((0, slice(0, P)), (1, slice(P, 3 * P))):
                        act.activation(prob[:, h, sl], prob[:, h, sl], ACT.Exp, bias=smax[:, h, b:b + 1],
                                       scale=HEAD_DIM ** -0.5, accum_out=ssum[:, h, b:b + 1])
                act.activation(snk[:, :, :], snk[:, :, :], ACT.Exp).then_inc(exp_done, 1)

            def prob_t(g):
                for h in range(GROUP):
                    act.wait_ge(prob_t_ps, GROUP * g + h + 1)
                    act.activation(prob[:, h, :], ps[:, 4 + h, 0:3 * P], ACT.Copy).then_inc(prob_t_done, 1)

            def read_ly(n):
                i = n % 2
                j = PROJ.index(LY[n // 2])
                if i == 0:
                    act.wait_ge(chunk_used, LY[n // 2] + 1)
                if n == 0:
                    act.wait_ge(rope_q, 5)
                if n >= 2:
                    act.wait_ge(gelu_done, n - 1)
                src = ps[:, j % 2, i * T:(i + 1) * T]
                act.activation(ly[:, i, :], src, ACT.Identity, bias=bias_in(LY0, n))
                act.activation(ly2[:, i, :], src, ACT.Square, bias=bias_in(LY0, n)).then_inc(ly_in, 1)

            def gelu_sig(n):
                act.wait_ge(z_done, n + 1)
                act.activation(sg[:, n % 2, :], ly2[:, n % 2, :], ACT.Sigmoid, scale=GELU_B).then_inc(zsig_done, 1)

            def read_gate(n):
                base, m = (GL0, n) if n < KT else (GA0, n - KT)
                chunk = (GL if n < KT else GA)[m // 2]
                i = n % 2
                if i == 0:
                    act.wait_ge(chunk_used, chunk + 1)
                if n >= 2:
                    act.wait_ge(gate_used, n - 1)
                act.activation(gate[:, i, :], ps[:, PROJ.index(chunk) % 2, i * T:(i + 1) * T], ACT.Sigmoid,
                               bias=bias_in(base, m)).then_inc(gate_in, 1)

            gate_sigmoids(0)
            gate_powers(0)
            read_ly(0)
            gate_roots(0)
            gelu_sig(0)
            read_ly(1)
            gelu_sig(1)
            exps(0)
            for n in (2, 3):
                read_ly(n)
                gelu_sig(n)
            gate_sigmoids(1)
            prob_t(0)
            read_ly(4)
            gelu_sig(4)
            gate_powers(1)
            read_ly(5)
            gelu_sig(5)
            gate_roots(1)
            exps(1)
            for n in (6, 7):
                read_ly(n)
                gelu_sig(n)
            prob_t(1)
            read_gate(0)
            read_gate(1)
            exps(2)
            act.wait_ge(state_done, KT)
            load(x1, a["x"][0].rearrange("(t p) d -> p t d", p=P), x_again)
            for q in range(4):
                load(b_out[32 * q:32 * q + 1, :], a["b_out"][0:1, 512 * (q % 2):512 * (q % 2 + 1)], x_again)
            act.wait_ge(gelu_done, KT)
            for quad in range(4):
                for v in range(4):
                    at = D * VECTOR_AT[v] + 256 * quad
                    load(bada_row[32 * quad:32 * quad + 1, v, :], a["b_ada"][0:1, at:at + 256], late_loaded)
            read_gate(2)
            read_gate(3)
            prob_t(2)
            read_gate(4)
            read_gate(5)
            exps(3)
            read_gate(6)
            read_gate(7)
            prob_t(3)
            for n in range(8, 2 * KT):
                read_gate(n)
            act.wait_ge(pool_set, 11)
            for v, name in ((G1, "g_post_mix"), (SC2, "g_pre_ffn"), (GT2, "g_post_ffn")):
                for quad in range(4):
                    load(gain_row[32 * quad:32 * quad + 1, v, :], a[name][0:1, 256 * quad:256 * (quad + 1)], late_loaded)
            act.wait_ge(merged, KT)
            load(b_e1[0:EXPERTS, :], a["b_e1"][0], moe_loaded)
            act.wait_ge(bc_ps, 1)
            act.activation(sh2_bc, ps[:, 6:8, :].rearrange("p a b -> p (a b)"), ACT.Copy).then_inc(bc_done, 1)
            act.wait_ge(chunk_used, WO[0] + 1)
            load(b_e2[:, :], a["b_e2"][0], moe_loaded)
            act.wait_ge(bc_ps, 2)
            act.activation(g1_bc, ps[:, 6:8, :].rearrange("p a b -> p (a b)"), ACT.Copy).then_inc(bc_done, 1)

            act.wait_ge(chunk_used, WO[-1] + 1)
            for t in range(TT):
                act.activation(junk, ps[:, 2 * t:2 * t + 2, :].rearrange("p a b -> p (a b)"), ACT.Square,
                               accum_out=stats[:, t:t + 1]).then_inc(act_step, 1)
                act.wait_ge(act_step, 3 + t)
                act.activation(stats[:, t:t + 1], stats[:, t:t + 1], ACT.Sqrt, bias=eps[:, 0:1], scale=1.0 / D).then_inc(y_sq, 1)
            for t in range(TT):
                act.wait_ge(x1_done, t + 1)
                act.activation(junk, x1[:, t, :], ACT.Square, accum_out=stats[:, 4 + t:5 + t]).then_inc(act_step, 1)
                act.wait_ge(act_step, 5 + t)
                act.activation(stats[:, 4 + t:5 + t], stats[:, 4 + t:5 + t], ACT.Sqrt, bias=eps[:, 0:1],
                               scale=1.0 / D).then_inc(x1_sq, 1)
            for t in range(TT):
                act.wait_ge(h2_t_ps, t + 1)
                act.activation(h2_t[:, 4:8, t * P:(t + 1) * P], ps[:, 2 * t + 1, :].rearrange("p (k t) -> p k t", k=4),
                               ACT.Copy).then_inc(h2_t_act, 1)
            act.wait_ge(top_done, 1)
            for t in range(TT):
                act.activation(soft[:, t, :], logits[:, t, :], ACT.Exp, bias=neg_max[:, t, :]).then_inc(topexp_done, 1)
            act.wait_ge(bc_ps, 4)
            act.activation(g2_bc, ps[:, 6:8, :].rearrange("p a b -> p (a b)"), ACT.Copy).then_inc(bc_done, 1)

            def experts(turn, q, p):
                for r in range(UNROLL):
                    done = turn * UNROLL + r
                    act.wait_ge(g_done, done * 3 + 1)
                    act.activation(s_g, g_c, ACT.Sigmoid, scale=ALPHA).then_inc(sig_done, 1)
                    act.wait_ge(act_t_ps, done * 2 + 1)
                    act.activation(act_t[:, 2:4].rearrange("p a b c -> p (a b c)"), ps[:, 5, 0:T], ACT.Copy).then_inc(act_t_a, 1)
                    act.wait_ge(act_t_ps, done * 2 + 2)
                    act.activation(scat_t[:, :, :], ps[:, 4, 0:T].rearrange("p (t s) -> p t s", t=TT), ACT.Copy).then_inc(scat_t_done, 1)

            more = all_experts(act, experts)

            act.wait_ge(combined, more * EXPERTS + (EXPERTS + 2))
            for t in range(TT):
                act.activation(junk, ps[:, 2 * t:2 * t + 2, :].rearrange("p a b -> p (a b)"), ACT.Square,
                               accum_out=stats[:, 8 + t:9 + t]).then_inc(act_step, 1)
                act.wait_ge(act_step, 7 + t)
                act.activation(stats[:, 8 + t:9 + t], stats[:, 8 + t:9 + t], ACT.Sqrt, bias=eps[:, 0:1],
                               scale=1.0 / D).then_inc(y2_sq, 1)
            for t in range(TT):
                act.wait_ge(fin_done, t + 1)
                act.dma_start(out[0, t * P:(t + 1) * P, :], fin[:, t, :]).then_inc(out_stored, 16)
            act.wait_ge(out_stored, 16 * TT)

        @block.gpsimd
        def _(pool):
            pool.memset(ones[:, :], 1.0).then_inc(pool_set, 1)
            pool.memset(ident[:, :], 0.0).then_inc(pool_set, 1)
            pool.memset(mask[:, :, :], 0.0).then_inc(pool_set, 1)
            pool.wait_ge(pool_set, 3)
            pool.affine_select(out=ident[:, :], in_=ident[:, :], compare_op=ALU.not_equal, fill=1.0, base=0,
                               pattern=[[-1, P]], channel_multiplier=1).then_inc(pool_set, 1)
            pool.affine_select(out=mask[:, 1, :], in_=mask[:, 1, :], compare_op=ALU.is_ge, fill=NEG, base=0,
                               pattern=[[-1, P]], channel_multiplier=1).then_inc(pool_set, 1)
            pool.affine_select(out=mask[:, 0, :], in_=mask[:, 0, :], compare_op=ALU.is_gt, fill=NEG, base=0,
                               pattern=[[1, P]], channel_multiplier=-1).then_inc(pool_set, 1)
            pool.memset(ones_b[:, :], 1.0).then_inc(pool_set, 1)
            pool.wait_ge(pool_set, 7)
            pool.affine_select(out=before[:, :], in_=ones_b[:, :], compare_op=ALU.is_gt, fill=0.0, base=0,
                               pattern=[[1, P]], channel_multiplier=-1).then_inc(pool_set, 1)
            pool.iota(slot_no[:, :, :], pattern=[[0, 2], [1, BLOCK]], base=0, channel_multiplier=0,
                      allow_small_or_imprecise_dtypes=True).then_inc(pool_set, 1)
            pool.iota(expert_no[:, :], pattern=[[1, EXPERTS]], base=0, channel_multiplier=0,
                      allow_small_or_imprecise_dtypes=True).then_inc(pool_set, 1)
            pool.memset(gain_row[:, :, :], 1.0).then_inc(pool_set, 1)
            pool.wait_ge(xn_done, TT)
            pool.memset(lx[:, :, 0:CONV - 1], 0.0).then_inc(pad_set, 1)
            for c in range(5):
                pool.wait_ge(swapped, c + 1)
                pool.tensor_tensor(swap, swap, sin_t[:, None, :].broadcast_to([P, 2, T]), ALU.mult).then_inc(times_sin, 1)
            for n in range(KT):
                pool.wait_ge(gates_read, n + 1)
                pool.tensor_tensor(g_i[:, n % 4, :], g_i[:, n % 4, :], xc[:, n, :], ALU.mult).then_inc(ix_done, 1)


_INS = ["x", "c", "positions", "w_ada", "b_ada", "g_pre_mix", "g_post_mix", "w_in", "b_in", "sinks", "conv_w", "conv_b",
        "w_rg", "b_rg", "w_ig", "b_ig", "lru_a", "w_out", "b_out", "g_pre_ffn", "g_post_ffn", "w_router", "b_router",
        "w_e1", "b_e1", "w_e2", "b_e2"]


def kernel(**inputs):
    import concourse.bacc as _bacc
    from concourse.bass_utils import run_bass_kernel_spmd as _run

    nc = _bacc.Bacc("TRN2", target_bir_lowering=False, num_devices=1)
    arrays, aps = {}, {}
    for name in _INS:
        arrays[f"in_{name}"] = np.ascontiguousarray(inputs[name])
    freqs = np.float32(ROPE_THETA) ** (-np.arange(0, HEAD_DIM, 2, dtype=np.float32) / np.float32(HEAD_DIM))
    arrays["in_inv_freq"] = np.tile(freqs.astype(np.float32), P // HALF).reshape(P, 1)
    for name, v in arrays.items():
        aps[name[3:]] = nc.dram_tensor(name, v.shape, mybir.dt.from_np(v.dtype), kind="ExternalInput").ap()
    out = nc.dram_tensor("out_0", (1, T, D), F32, kind="ExternalOutput").ap()
    layer(nc, aps, out)
    r = _run(nc, [arrays], core_ids=[0])
    return r.results[0]["out_0"]
```

```python
from contextlib import ExitStack

import numpy as np

import concourse.bass as bass
import concourse.mybir as mybir

F32 = mybir.dt.float32
BF16 = mybir.dt.bfloat16
I32 = mybir.dt.int32
U32 = mybir.dt.uint32
ALU = mybir.AluOpType
ACT = mybir.ActivationFunctionType
AX = mybir.AxisListType

P = 128
D = 1024
T = 256
TT = T // P
KT = D // P
HEADS, KV_HEADS, HEAD_DIM = 16, 4, 64
HALF = HEAD_DIM // 2
GROUP = HEADS // KV_HEADS
CONV = 4
EXPERTS, TOP_K = 32, 4
LIMIT, ALPHA = 7.0, 1.702
LRU_C = 8.0
EPS = 1e-6
ROPE_THETA = 10000.0
NEG = -1.0e30
GELU_A = 0.044715
GELU_B = float(np.sqrt(2.0 / np.pi))
BLOCK = 64
PASSES = T // BLOCK

Q0, K0, V0 = 0, HEADS * HEAD_DIM, HEADS * HEAD_DIM + KV_HEADS * HEAD_DIM
LX0 = V0 + KV_HEADS * HEAD_DIM
LY0, GA0, GL0 = LX0 + D, LX0 + 2 * D, LX0 + 3 * D

RING = 16
SLOT = 2048
PROJ_W = 256
N_ADA_A = KT
LX = [N_ADA_A + i for i in range(4)]
QC = [LX[-1] + 1 + i for i in range(4)]
KC = QC[-1] + 1
VC = KC + 1
GATES_A = VC + 1
LY_A = [GATES_A + 1, GATES_A + 2, GATES_A + 3]
GATES_B = LY_A[-1] + 1
LY = [*LY_A, GATES_B + 1]
GATES = (GATES_A, GATES_B)
GL = [LY[-1] + 1 + i for i in range(4)]
GA = [GL[-1] + 1 + i for i in range(4)]
G1, SH2, SC2, GT2 = range(4)
ADA_B = [[GA[-1] + 1 + 4 * v + (4 if v >= SC2 else 0) + i for i in range(4)] for v in range(4)]
WO = [ADA_B[SH2][-1] + 1 + i for i in range(4)]
MIXER_CHUNKS = ADA_B[GT2][-1] + 1
E1_CHUNKS, E2_CHUNKS = KT, KT // 2
EXPERT_CHUNKS = E1_CHUNKS + E2_CHUNKS
UNROLL = 4
assert UNROLL * EXPERT_CHUNKS % RING == 0
TURNS = UNROLL * EXPERT_CHUNKS // RING
PROJ = [*LX, *QC, KC, VC, *LY, *GL, *GA]

ROW_BANK = (4, 4, 5, 4)
ROW_AT = (0, 256, 0, 0)

R_C, R_GPRE, R_BADA, ROWS_A = 0, 8, 16, 32
R_BIN, R_CONVW, R_CONVB, R_BRG, R_BIG, R_LRUA, ROWS_B = 0, 44, 76, 84, 92, 100, 108


def layer(nc, a, out):
    with ExitStack() as ctx:
        def sb(name, shape, dt=F32):
            return ctx.enter_context(nc.sbuf_tensor(name, shape, dt))

        def sem(name):
            return ctx.enter_context(nc.semaphore(name))

        ps = ctx.enter_context(nc.psum_tensor("ps", [P, 8, 512], F32))

        ring = sb("ring", [P, RING, SLOT])
        ident = sb("ident", [P, P])
        ones = sb("ones", [P, P])
        before = sb("before", [P, P], BF16)
        ones_b = sb("ones_b", [P, P], BF16)
        mask = sb("mask", [P, 2, P])
        slot_no = sb("slot_no", [P, 2, BLOCK])
        expert_no = sb("expert_no", [P, EXPERTS])
        rows_a = sb("rows_a", [ROWS_A, P])
        rows = sb("rows", [ROWS_B, P])
        cols_a = sb("cols_a", [P, ROWS_A])
        cols = sb("cols", [P, ROWS_B])
        freq = sb("freq", [P, 1])
        half_bias = sb("half_bias", [P, 3 * KT])
        silu_c = sb("silu_c", [P, KT])
        mod_a = sb("mod_a", [P, 2 * KT])
        decay = sb("decay", [P, 2, KT])
        stats = sb("stats", [P, 16])
        sinks = sb("sinks", [P, HEADS])
        neg_sinks = sb("neg_sinks", [P, HEADS])
        smax = sb("smax", [P, GROUP, 2])
        ssum = sb("ssum", [P, GROUP, 2])
        snk = sb("snk", [P, GROUP, 2])
        b_v = sb("b_v", [P, KV_HEADS * HEAD_DIM])
        w_rt = sb("w_rt", [P, KT, EXPERTS])
        b_rt = sb("b_rt", [P, EXPERTS])
        fold = sb("fold", [P, EXPERTS])
        expert_hot = sb("expert_hot", [EXPERTS, EXPERTS + 1])
        eps = sb("eps", [P, 1])
        logits = sb("logits", [P, TT, EXPERTS])
        top8 = sb("top8", [P, TT, 8])
        top_i = sb("top_i", [P, TT, 8], U32)
        top_f = sb("top_f", [P, TT, 8])
        neg_max = sb("neg_max", [P, TT, 1])
        sums = sb("sums", [P, TT, 1])
        hit = sb("hit", [P, TT, EXPERTS])
        hit_b = sb("hit_b", [P, TT, EXPERTS], BF16)
        route_w = sb("route_w", [P, TT, EXPERTS])
        rank = sb("rank", [P, TT, EXPERTS + 1])
        passes_f = sb("passes_f", [P, 4])
        more_i = sb("more_i", [P, 1], I32)

        z_h = sb("z_h", [P, 2048])
        z_attn = sb("z_attn", [P, KT * (T + CONV - 1)])
        z_lru = sb("z_lru", [P, 2048])
        z_gate = sb("z_gate", [P, 3072])
        z_q = sb("z_q", [P, 2048])
        z_k = sb("z_k", [P, 2048])
        z_p = sb("z_p", [P, GROUP * 3 * P])
        z_t = sb("z_t", [P, 1536])
        z_c = sb("z_c", [P, 1536])

        def v3(t, at, a_, b_):
            return t[:, at:at + a_ * b_].rearrange("p (a b) -> p a b", a=a_)

        def v4(t, at, a_, b_, c_):
            return t[:, at:at + a_ * b_ * c_].rearrange("p (a b c) -> p a b c", a=a_, b=b_)

        x_in = v3(z_attn, 0, TT, D)
        x_n = v3(z_gate, 0, TT, D)
        mod_a_rows = z_t[:, 0:512]
        h_t = v3(z_h, 0, KT, T)
        lx = v3(z_attn, 0, KT, T + CONV - 1)
        xc = v3(z_lru, 0, KT, T)
        g_r, g_i, g_a = (v3(z_gate, 1024 * i, 4, T) for i in range(3))
        q_r = v3(z_q, 0, KT, T)
        k_rep = v3(z_k, 0, KV_HEADS, T)
        qk_raw = v4(z_t, 0, 2, 2, T)
        swap = v3(z_t, 1024, 2, T)
        k_r = v3(z_p, 0, 2, T)
        prob = v3(z_p, 0, GROUP, 3 * P)
        cos_t, sin_t, tmp_a, tmp_b = (z_c[:, T * i:T * (i + 1)] for i in range(4))
        v_sb = v3(z_c, 1024, TT, KV_HEADS * HEAD_DIM)
        lru_tmp = v3(z_c, 0, 2, T)
        gate = v3(z_c, 512, 2, T)
        attn = v3(z_attn, 0, KT, T)
        ly = v3(z_t, 0, 2, T)
        ly2 = v3(z_t, 512, 2, T)
        sg = v3(z_t, 1024, 2, T)
        x1 = v3(z_gate, 0, TT, D)
        b_out = z_gate[0:96, 2048:3072]
        b_out_parts = z_p[0:96, 1024:1536].bitcast(BF16)
        g1_bc = z_q[:, 0:1024]
        sh2_bc = z_q[:, 1024:2048]
        g2_bc = z_k[:, 0:1024]
        gain_row = v3(z_k, 1024, 4, 256)
        mod_row = v3(z_p, 0, 4, 256)
        bada_row = v3(z_t, 0, 4, 256)
        y_g = v3(z_attn, 0, TT, D)
        logit_part = z_p[:, 1280:1536]
        soft = v3(z_c, 512, TT, EXPERTS)
        match = v4(z_c, 0, TT, TOP_K, EXPERTS)
        h2 = v3(z_h, 0, TT, D)
        h2_t = v3(z_attn, 0, KT, T)
        b_e1 = z_lru[:, 0:2048]
        hsel = v3(z_attn, 0, KT, BLOCK)
        g_c, u_c, s_g = (z_attn[:, 512 * i:512 * (i + 1)] for i in (1, 2, 3))
        act_t = v4(z_q, 0, 4, 2, BLOCK)
        g_u = z_q[:, 512:1024]
        o_sb = z_q[:, 1024:1536]
        scat_t = v3(z_q, 1536, TT, P)
        scat = v4(z_q, 1792, TT, 2, BLOCK)
        b_e2 = z_gate[:, 2560:3072]
        zero_row = z_q[32:33, 1024:1280].bitcast(BF16)
        pick = v3(z_t, 0, TT, BLOCK)
        bias_pick = z_t[0:EXPERTS, 256:256 + BLOCK]
        fin = v3(z_lru, 0, TT, D)
        junk = z_c[:, 0:1024]

        landed = [sem(f"landed{i}") for i in range(RING)]
        chunk_used = sem("chunk_used")
        x_loaded, rows_loaded, small_loaded, x_again = sem("x_loaded"), sem("rows_loaded"), sem("small_loaded"), sem("x_again")
        late_loaded, moe_loaded, pad_set = sem("late_loaded"), sem("moe_loaded"), sem("pad_set")
        out_stored = sem("out_stored")
        pool_set = sem("pool_set")
        dve_step, act_step = sem("dve_step"), sem("act_step")
        rows_a_loaded = sem("rows_a_loaded")
        eps_set, gain_set = sem("eps_set"), sem("gain_set")
        x_sq, xn_done, xn_t, rows_t, cols_done, c_sig, silu_done = (sem(n) for n in (
            "x_sq", "xn_done", "xn_t", "rows_t", "cols_done", "c_sig", "silu_done"))
        mod_rows, mod_cols, mod_done = sem("mod_rows"), sem("mod_cols"), sem("mod_done")
        h_dve, h_act = sem("h_dve"), sem("h_act")
        proj_read, v_done = sem("proj_read"), sem("v_done")
        angle_done, sin_done, rope_done = sem("angle_done"), sem("sin_done"), sem("rope_done")
        swapped, times_sin, rope_q, k_rep_done = sem("swapped"), sem("times_sin"), sem("rope_q"), sem("k_rep_done")
        conv_done, gates_ps, gates_read = sem("conv_done"), sem("gates_ps"), sem("gates_read")
        half_done = sem("half_done")
        decay_done, sp_done = sem("decay_done"), sem("sp_done")
        a_done, th_done, m2_done, mult_done, ix_done, u_done, state_done = (sem(n) for n in (
            "a_done", "th_done", "m2_done", "mult_done", "ix_done", "u_done", "state_done"))
        scores_ps, smax_done, exp_done, prob_done = sem("scores_ps"), sem("smax_done"), sem("exp_done"), sem("prob_done")
        prob_t_ps, prob_t_done, pv_ps, attn_done = sem("prob_t_ps"), sem("prob_t_done"), sem("pv_ps"), sem("attn_done")
        ly_in, gelu_done, z_done, zsig_done, lg_done = (sem(n) for n in ("ly_in", "gelu_done", "z_done", "zsig_done", "lg_done"))
        gate_in, gate_used, merged = sem("gate_in"), sem("gate_used"), sem("merged")
        mod_row_done, bc_ps, bc_done = sem("mod_row_done"), sem("bc_ps"), sem("bc_done")
        bias_split = sem("bias_split")
        y_ps, zero_set = sem("y_ps"), sem("zero_set")
        part_ps, part_done = sem("part_ps"), sem("part_done")
        y_sq, x1_done, x1_sq, h2_done, h2_t_ps, h2_t_act, h2_t_dve = (sem(n) for n in (
            "y_sq", "x1_done", "x1_sq", "h2_done", "h2_t_ps", "h2_t_act", "h2_t_dve"))
        logits_ps, top_done, topexp_done, route_done, rank_ps, rank_done = (sem(n) for n in (
            "logits_ps", "top_done", "topexp_done", "route_done", "rank_ps", "rank_done"))
        route_t_ps, route_t_done = sem("route_t_ps"), sem("route_t_done")
        picked, gathered, hsel_done = sem("picked"), sem("gathered"), sem("hsel_done")
        g_done, sig_done, act_done = sem("g_done"), sem("sig_done"), sem("act_done")
        act_t_ps, act_t_a, act_t_d, scat_t_done = sem("act_t_ps"), sem("act_t_a"), sem("act_t_d"), sem("scat_t_done")
        o_done, combined = sem("o_done"), sem("combined")
        y2_sq, fin_done = sem("y2_sq"), sem("fin_done")

        def loads(n):
            return n // RING + 1 + sum(g <= n and g % RING == n % RING for g in GATES)

        def wait_chunk(eng, n):
            eng.wait_ge(landed[n % RING], 16 * loads(n))

        def wait_expert_chunk(eng, r, m, turn):
            n = MIXER_CHUNKS + r * EXPERT_CHUNKS + m
            eng.wait_ge(landed[n % RING], turn * (16 * TURNS) + 16 * loads(n))

        def expert_slot(r, m):
            return (MIXER_CHUNKS + r * EXPERT_CHUNKS + m) % RING

        def all_experts(eng, body, pool=None):
            groups = EXPERTS // UNROLL
            with eng.Fori(0, groups) as q:
                body(q, q, None)
            eng.wait_ge(rank_done, 1)
            more = eng.value_load(more_i[0:1, 0:1], min_val=0, max_val=PASSES - 1)
            with eng.If(more > 0):
                with eng.Fori(0, more) as p:
                    if pool is not None:
                        pool(p)
                    with eng.Fori(0, groups) as q:
                        body(p * groups + q + groups, q, p)
            return more

        block = ctx.enter_context(nc.Block())

        @block.sync
        def _(sp):
            def load(n, dst, src):
                if n >= RING:
                    sp.wait_ge(chunk_used, n - RING + 1)
                sp.dma_start(dst, src).then_inc(landed[n % RING], 16)

            for at, n, name in ((R_C, KT, "c"), (R_GPRE, KT, "g_pre_mix"), (R_BADA, 2 * KT, "b_ada")):
                sp.dma_start(rows_a[at:at + n, :],
                             a[name].rearrange("l (r p) -> (l r) p", p=P)[0:n]).then_inc(rows_a_loaded, 16)

            w_ada = a["w_ada"][0].rearrange("(k p) n -> k p n", p=P)
            for k in range(KT):
                load(k, ring[:, k % RING, :], w_ada[k, :, 0:2 * D])
            w_in = a["w_in"][0].rearrange("(k p) n -> p k n", p=P)
            starts = {**{n: LX0 + PROJ_W * i for i, n in enumerate(LX)},
                      **{n: Q0 + PROJ_W * i for i, n in enumerate(QC)}, KC: K0, VC: V0,
                      **{n: LY0 + PROJ_W * i for i, n in enumerate(LY)},
                      **{n: GA0 + PROJ_W * i for i, n in enumerate(GA)},
                      **{n: GL0 + PROJ_W * i for i, n in enumerate(GL)}}
            for n in range(LX[0], GA[-1] + 1):
                slot = ring[:, n % RING, :]
                if n in GATES:
                    half = GATES.index(n)
                    w = slot[:, 0:1024].rearrange("p (g n e) -> p g n e", g=2, n=4)
                    load(n, w[:, 0], a["w_rg"][0, 4 * half:4 * half + 4].rearrange("n d e -> d n e"))
                    load(n, w[:, 1], a["w_ig"][0, 4 * half:4 * half + 4].rearrange("n d e -> d n e"))
                else:
                    c = starts[n]
                    load(n, slot.rearrange("p (k n) -> p k n", k=KT), w_in[:, :, c:c + PROJ_W])
            w_ada2 = a["w_ada"][0].rearrange("(c k p) n -> c p k n", k=2, p=P)
            w_out = a["w_out"][0].rearrange("(c k p) n -> c p k n", k=2, p=P)

            def load_vector(v):
                for i, n in enumerate(ADA_B[v]):
                    at = D * (2 + v)
                    load(n, ring[:, n % RING, :].rearrange("p (k n) -> p k n", k=2), w_ada2[i, :, :, at:at + D])

            load_vector(G1)
            load_vector(SH2)
            for i, n in enumerate(WO):
                load(n, ring[:, n % RING, :].rearrange("p (k n) -> p k n", k=2), w_out[i])
            load_vector(SC2)
            load_vector(GT2)

            w_e1 = a["w_e1"][0].rearrange("e (k p) n -> e k p n", p=P)
            w_e2 = a["w_e2"][0].rearrange("e (c k p) n -> e c p k n", k=2, p=P)

            def experts(turn, q, p):
                for r in range(UNROLL):
                    for m in range(EXPERT_CHUNKS):
                        n = MIXER_CHUNKS + r * EXPERT_CHUNKS + m
                        sp.wait_ge(chunk_used, turn * (UNROLL * EXPERT_CHUNKS) + (n - RING + 1))
                        slot = ring[:, n % RING, :]
                        if m < E1_CHUNKS:
                            src = w_e1[bass.ds(q * UNROLL + r, 1), m].rearrange("e p n -> (e p) n")
                        else:
                            slot = slot.rearrange("p (k n) -> p k n", k=2)
                            src = w_e2[bass.ds(q * UNROLL + r, 1), m - E1_CHUNKS].rearrange("e p k n -> (e p) k n")
                        sp.dma_start(slot, src).then_inc(landed[n % RING], 16)

            all_experts(sp, experts)

        @block.tensor
        def _(pe):
            pe.wait_ge(pool_set, 4)
            pe.wait_ge(rows_a_loaded, 16 * 3)
            pe.transpose(ps[:, 1, 0:ROWS_A], rows_a[:, :], ident[0:ROWS_A, 0:ROWS_A]).then_inc(rows_t, 1)

            pe.wait_ge(silu_done, 1)
            for k in range(N_ADA_A):
                wait_chunk(pe, k)
                for c in range(4):
                    mm = pe.matmul(ps[32 * c:32 * (c + 1), 0, :], silu_c[:, k:k + 1].broadcast_to([P, 32]),
                                   ring[:, k % RING, 512 * c:512 * (c + 1)], start=(k == 0), stop=(k == KT - 1),
                                   tile_position=(0, 32 * c))
                mm.then_inc(chunk_used, 1)
                if k in (5, 7):
                    t = (k - 5) // 2
                    pe.wait_ge(xn_done, t + 1)
                    for f in range(KT):
                        mm = pe.transpose(ps[:, 4 + f // 2, (f % 2) * T + t * P:(f % 2) * T + (t + 1) * P],
                                          x_n[:, t, f * P:(f + 1) * P], ident[:, :])
                    mm.then_inc(xn_t, 1)
            pe.wait_ge(rows_loaded, 16 * 6)
            pe.wait_ge(cols_done, 1)
            pe.transpose(ps[:, 1, 0:ROWS_B], rows[:, :], ident[0:ROWS_B, 0:ROWS_B]).then_inc(rows_t, 1)
            pe.wait_ge(mod_rows, 1)
            for j in range(4):
                mm = pe.transpose(ps[:, 1, j * P:(j + 1) * P], mod_a_rows[:, j * P:(j + 1) * P], ident[:, :])
            mm.then_inc(mod_cols, 1)

            def proj_bank_free(j):
                if j == 0:
                    pe.wait_ge(mod_done, 1)
                elif j == 1:
                    pe.wait_ge(mod_done, 1)
                elif PROJ[j - 2] == VC:
                    pe.wait_ge(v_done, 1)
                elif PROJ[j - 2] in LY:
                    pe.wait_ge(ly_in, 2 * LY.index(PROJ[j - 2]) + 2)
                elif PROJ[j - 2] in GL + GA:
                    pe.wait_ge(gate_in, 2 * (GL + GA).index(PROJ[j - 2]) + 2)
                else:
                    pe.wait_ge(proj_read, j - 1)

            def project_tile(j, i):
                n = PROJ[j]
                w = ring[:, n % RING, :].rearrange("p (k n) -> p k n", k=KT)
                dst = ps[:, j % 2, i * T:(i + 1) * T]
                if i == 0:
                    proj_bank_free(j)
                    wait_chunk(pe, n)
                for k in range(KT):
                    if j == 0 and i == 0:
                        pe.wait_ge(h_dve if k < KT // 2 else h_act, k % (KT // 2) + 1)
                    if n == VC:
                        mm = pe.matmul(dst, h_t[:, k, i * P:(i + 1) * P], w[:, k, :], start=(k == 0), stop=(k == KT - 1))
                    else:
                        mm = pe.matmul(dst, w[:, k, i * P:(i + 1) * P], h_t[:, k, :], start=(k == 0), stop=(k == KT - 1))
                if i == 1:
                    mm.then_inc(chunk_used, 1)

            def gates(blocks):
                half = blocks[0] // 4
                wait_chunk(pe, GATES[half])
                w = ring[:, GATES[half] % RING, 0:1024].rearrange("p (g n e) -> p g n e", g=2, n=4)
                for n in blocks:
                    pe.wait_ge(conv_done, n + 1)
                    if n >= 2:
                        pe.wait_ge(gates_read, n - 1)
                    for g in range(2):
                        mm = pe.matmul(ps[:, 2 + n % 2, g * T:(g + 1) * T], w[:, g, n % 4, :], xc[:, n, :],
                                       start=True, stop=True)
                    if n % 4 == 3:
                        mm.then_inc(chunk_used, 1)
                    else:
                        mm.then_inc(gates_ps, 1)

            for j in range(len(LX) + len(QC) + 2):
                project_tile(j, 0)
                project_tile(j, 1)
            gates(range(0, 4))
            def scores(g):
                pe.wait_ge(rope_q, 5)
                pe.wait_ge(k_rep_done, 1)
                if g:
                    pe.wait_ge(prob_t_done, GROUP * g)
                for blk in range(2):
                    for h in range(GROUP):
                        half = slice(h % 2 * HEAD_DIM, (h % 2 + 1) * HEAD_DIM)
                        dst = ps[:, 4 + h, 0:P] if blk == 0 else ps[:, 4 + h, P:3 * P]
                        mm = pe.matmul(dst, q_r[half, 2 * g + h // 2, blk * P:(blk + 1) * P],
                                       k_rep[half, g, 0:(blk + 1) * P], start=True, stop=True,
                                       tile_position=(h % 2 * HEAD_DIM, 0))
                mm.then_inc(scores_ps, 1)

            def transposes(g):
                for h in range(GROUP):
                    pe.wait_ge(prob_done, GROUP * g + h + 1)
                    for b in range(3):
                        mm = pe.transpose(ps[:, 4 + h, b * P:(b + 1) * P], prob[:, h, b * P:(b + 1) * P], ident[:, :])
                    mm.then_inc(prob_t_ps, 1)

            def weighted_values(g):
                for h in range(GROUP):
                    tile_no = 2 * g + h // 2
                    pe.wait_ge(prob_t_done, GROUP * g + h + 1)
                    if h == 0:
                        pe.wait_ge(v_done, 1)
                        if g == 0:
                            pe.wait_ge(gates_read, KT)
                        else:
                            pe.wait_ge(attn_done, 2 * g)
                    at = (h % 2) * HEAD_DIM
                    v = v_sb[:, :, g * HEAD_DIM:(g + 1) * HEAD_DIM]
                    dst = ps[at:at + HEAD_DIM, 2 + tile_no % 2, :]
                    pe.matmul(dst[:, 0:P], v[:, 0], prob[:, h, 0:P], start=True, stop=True)
                    pe.matmul(dst[:, P:2 * P], v[:, 0], prob[:, h, P:2 * P], start=True, stop=False)
                    mm = pe.matmul(dst[:, P:2 * P], v[:, 1], prob[:, h, 2 * P:3 * P], start=False, stop=True)
                    mm.then_inc(pv_ps, 1)

            for u in range(len(LY) + len(GL) + len(GA)):
                if u == 3:
                    gates(range(4, 6))
                    scores(1)
                    gates(range(6, 8))
                if u % 2 and 3 <= u <= 9:
                    weighted_values((u - 3) // 2)
                if u % 2 and u <= 7 and u != 3:
                    scores((u - 1) // 2)
                project_tile(10 + u, 0)
                if u % 2 == 0 and 2 <= u <= 8:
                    transposes((u - 2) // 2)
                project_tile(10 + u, 1)

            def vector_rows(v, part):
                n = ADA_B[v][part]
                wait_chunk(pe, n)
                w = ring[:, n % RING, :].rearrange("p (k n) -> p k n", k=2)
                for k in range(2):
                    kt = 2 * part + k
                    for c in range(4):
                        mm = pe.matmul(ps[32 * c:32 * (c + 1), ROW_BANK[v], ROW_AT[v]:ROW_AT[v] + 256],
                                       silu_c[:, kt:kt + 1].broadcast_to([P, 32]), w[:, k, 256 * c:256 * (c + 1)],
                                       start=(kt == 0), stop=(kt == KT - 1), tile_position=(0, 32 * c))
                mm.then_inc(chunk_used, 1)

            def spread(v):
                for c in range(4):
                    mm = pe.matmul(ps[:, 6 + c // 2, 256 * (c % 2):256 * (c % 2 + 1)],
                                   ident[:, 32 * c:32 * c + 1].broadcast_to([P, P]), mod_row[:, v, :], start=True, stop=True)
                mm.then_inc(bc_ps, 1)

            pe.wait_ge(prob_t_done, HEADS)
            for v in (G1, SH2):
                for part in range(4):
                    vector_rows(v, part)

            pe.wait_ge(gate_in, 2 * KT)
            pe.wait_ge(attn_done, KT)
            pe.wait_ge(bias_split, 4)
            for q in range(4):
                pe.matmul(ps[:, q, :], ones_b[0:96, :], b_out_parts[:, 512 * (q % 2):512 * (q % 2 + 1)], start=True, stop=False)
            for i, n in enumerate(WO):
                wait_chunk(pe, n)
                w = ring[:, n % RING, :].rearrange("p (k n) -> p k n", k=2)
                for t in range(TT):
                    for k in (2 * i, 2 * i + 1):
                        if t == 0:
                            pe.wait_ge(merged, k + 1)
                        for c in range(2):
                            mm = pe.matmul(ps[:, 2 * t + c, :], attn[:, k, t * P:(t + 1) * P],
                                           w[:, k % 2, 512 * c:512 * (c + 1)], start=False, stop=(k == KT - 1))
                    if t == 0 and n == WO[-1]:
                        mm.then_inc(y_ps, 1)
                mm.then_inc(chunk_used, 1)
                if i == 0:
                    pe.wait_ge(mod_row_done, 1)
                    spread(G1)
                if i == 1:
                    pe.wait_ge(bc_done, 1)
                    spread(SH2)

            def turn_h2(t):
                pe.wait_ge(h2_done, t + 1)
                for f in range(KT):
                    mm = pe.transpose(ps[:, 2 * t + f // 4, (f % 4) * P:(f % 4 + 1) * P],
                                      h2[:, t, f * P:(f + 1) * P], ident[:, :])
                mm.then_inc(h2_t_ps, 1)

            for part in range(4):
                vector_rows(SC2, part)
            vector_rows(GT2, 0)
            pe.wait_ge(mod_row_done, 2)
            pe.wait_ge(bc_done, 2)
            spread(SC2)
            vector_rows(GT2, 1)
            vector_rows(GT2, 2)
            turn_h2(0)
            vector_rows(GT2, 3)
            turn_h2(1)
            pe.wait_ge(h2_t_act, 2)
            pe.wait_ge(h2_t_dve, 2)
            for k in range(KT):
                c = k % 4
                mm = pe.matmul(ps[32 * c:32 * (c + 1), 5, 0:T], w_rt[:, k, :], h2_t[:, k, :], start=(k < 4), stop=(k >= 4),
                               tile_position=(0, 32 * c))
            mm.then_inc(part_ps, 1)
            pe.wait_ge(part_done, 1)
            for t in range(TT):
                mm = pe.matmul(ps[:, 5, t * EXPERTS:(t + 1) * EXPERTS], logit_part[:, t * P:(t + 1) * P], fold[:, :],
                               start=True, stop=True)
            mm.then_inc(logits_ps, 1)
            pe.wait_ge(mod_row_done, 3)
            spread(GT2)
            pe.wait_ge(route_done, 1)
            pe.matmul(ps[:, 5, 0:EXPERTS], before[:, :], hit_b[:, 0, :], start=True, stop=True)
            pe.matmul(ps[:, 5, EXPERTS:2 * EXPERTS], ones_b[:, :], hit_b[:, 0, :], start=True, stop=False)
            pe.matmul(ps[:, 5, EXPERTS:2 * EXPERTS], before[:, :], hit_b[:, 1, :], start=False, stop=True)
            pe.matmul(ps[:, 5, 2 * EXPERTS:3 * EXPERTS], ones_b[:, :], hit_b[:, 0, :], start=True, stop=False)
            pe.matmul(ps[:, 5, 2 * EXPERTS:3 * EXPERTS], ones_b[:, :], hit_b[:, 1, :], start=False,
                      stop=True).then_inc(rank_ps, 1)
            pe.wait_ge(route_done, 2)
            for t in range(TT):
                mm = pe.transpose(ps[0:EXPERTS, 4, t * P:(t + 1) * P], route_w[:, t, :], ident[:, :])
            mm.then_inc(route_t_ps, 1)

            def gather(count):
                pe.wait_ge(picked, count)
                for k in range(KT):
                    for t in range(TT):
                        mm = pe.matmul(ps[:, 7, k * BLOCK:(k + 1) * BLOCK], h2[:, t, k * P:(k + 1) * P], pick[:, t, :],
                                       start=(t == 0), stop=(t == TT - 1))
                mm.then_inc(gathered, 1)

            def combine():
                for t in range(TT):
                    for c in range(2):
                        mm = pe.matmul(ps[:, 2 * t + c, :], scat_t[64 * c:64 * (c + 1), t, :], o_sb[64 * c:64 * (c + 1), :],
                                       start=False, stop=False, skip_group_check=True, tile_position=(64 * c, 0))
                    mm.then_inc(combined, 1)

            pe.wait_ge(zero_set, 1)
            for bank in range(4):
                mm = pe.matmul(ps[:, bank, :], zero_row[:, 0:P], zero_row[:, :], start=True, stop=False,
                               skip_group_check=True, tile_position=(32, 0))
            mm.then_inc(combined, 1)
            pe.wait_ge(bc_done, 3)
            for _ in range(8):
                pe.matmul(ps[:, 7, 0:2 * P], ones_b[:, :], ones[:, :].bitcast(BF16), start=True, stop=True)
            gather(1)
            pe.wait_ge(route_t_done, 1)
            pe.wait_ge(o_done, 1)
            pe.wait_ge(combined, 1)
            pe.wait_ge(rank_done, 1)

            def experts(turn, q, p):
                for r in range(UNROLL):
                    done = turn * UNROLL + r
                    for b in range(2):
                        for c in range(2):
                            pe.matmul(ps[64 * c:64 * (c + 1), 4 + b, :], bias_pick[:, :],
                                      b_e1[0:EXPERTS, b * D + 512 * c:b * D + 512 * (c + 1)], start=True, stop=False,
                                      tile_position=(0, 64 * c))
                    for k in range(KT):
                        if k == 0:
                            pe.wait_ge(hsel_done, done + 1)
                        wait_expert_chunk(pe, r, k, turn)
                        w = ring[:, expert_slot(r, k), :]
                        for b in range(2):
                            for c in range(2):
                                mm = pe.matmul(ps[64 * c:64 * (c + 1), 4 + b, :], hsel[:, k, :],
                                               w[:, b * D + 512 * c:b * D + 512 * (c + 1)], start=False, stop=(k == KT - 1),
                                               tile_position=(0, 64 * c))
                        mm.then_inc(chunk_used, 1)
                        if k == 1:
                            pe.wait_ge(o_done, done + 1)
                            combine()
                    gather(done + 2)
                    pe.wait_ge(act_done, done + 1)
                    for c in range(4):
                        mm = pe.transpose(ps[:, 6 - c // 2, c % 2 * P:(c % 2 + 1) * P], g_u[:, c * P:(c + 1) * P], ident[:, :])
                    mm.then_inc(act_t_ps, 1)
                    for t in range(TT):
                        mm = pe.transpose(ps[:, 4, t * P:(t + 1) * P], scat[:, t].rearrange("p a s -> p (a s)"), ident[:, :])
                    mm.then_inc(act_t_ps, 1)
                    pe.wait_ge(act_t_a, done + 1)
                    pe.wait_ge(act_t_d, done + 1)
                    for k in range(KT):
                        if k % 2 == 0:
                            wait_expert_chunk(pe, r, E1_CHUNKS + k // 2, turn)
                        w = ring[:, expert_slot(r, E1_CHUNKS + k // 2), :]
                        for c in range(2):
                            mm = pe.matmul(ps[64 * c:64 * (c + 1), 6, :], act_t[:, k % 4, k // 4, :],
                                           w[:, (k % 2) * D + 512 * c:(k % 2) * D + 512 * (c + 1)],
                                           start=(k == 0), stop=(k == KT - 1), tile_position=(0, 64 * c))
                        if k % 2:
                            mm.then_inc(chunk_used, 1)
                    pe.wait_ge(scat_t_done, done + 1)

            more = all_experts(pe, experts)
            pe.wait_ge(o_done, more * EXPERTS + (EXPERTS + 1))
            combine()

        @block.vector
        def _(dve):
            steps = [0]

            def step(ins):
                ins.then_inc(dve_step, 1)
                steps[0] += 1
                return steps[0]

            def then(n=None):
                dve.wait_ge(dve_step, steps[0] if n is None else n)

            dve.memset(eps[:, :], EPS).then_inc(eps_set, 1)
            dve.wait_ge(x_sq, 1)
            step(dve.reciprocal(stats[:, 2:4], stats[:, 0:2]))
            then()
            for t in range(TT):
                dve.tensor_scalar(x_n[:, t, :], x_in[:, t, :], stats[:, 2 + t:3 + t], None, ALU.mult).then_inc(xn_done, 1)
            dve.wait_ge(pool_set, 4)
            for q in range(4):
                dve.tensor_copy(fold[32 * q:32 * (q + 1), :], ident[32 * q:32 * (q + 1), 32 * q:32 * (q + 1)])
            dve.tensor_copy(expert_hot[:, 0:EXPERTS], ident[0:EXPERTS, 0:EXPERTS])
            step(dve.tensor_copy(expert_hot[:, EXPERTS:], ident[0:EXPERTS, 0:1]))
            dve.wait_ge(rows_t, 1)
            dve.tensor_copy(cols_a[:, :], ps[:, 1, 0:ROWS_A]).then_inc(cols_done, 1)
            dve.wait_ge(cols_done, 1)
            dve.wait_ge(c_sig, 1)
            dve.tensor_tensor(silu_c[:, :], cols_a[:, R_C:R_C + KT], silu_c[:, :], ALU.mult).then_inc(silu_done, 1)
            dve.wait_ge(rows_t, 2)
            dve.tensor_copy(cols[:, :], ps[:, 1, 0:ROWS_B]).then_inc(cols_done, 1)
            dve.wait_ge(chunk_used, N_ADA_A)
            dve.tensor_copy(mod_a_rows, ps[:, 0, :]).then_inc(mod_rows, 1)
            dve.wait_ge(mod_cols, 1)
            step(dve.tensor_tensor(mod_a[:, :].rearrange("p (c j) -> p c j", c=4),
                                   ps[:, 1, :].rearrange("p (j c x) -> p c j x", j=4, c=4)[:, :, :, 0],
                                   cols_a[:, R_BADA:R_BADA + 2 * KT].rearrange("p (c j) -> p c j", c=4), ALU.add))
            then()
            dve.scalar_tensor_tensor(mod_a[:, KT:], mod_a[:, KT:], 1.0, cols_a[:, R_GPRE:R_GPRE + KT], ALU.add,
                                     ALU.mult).then_inc(mod_done, 1)
            dve.wait_ge(mod_done, 1)
            dve.wait_ge(xn_t, TT)
            for k in range(KT // 2):
                dve.tensor_scalar(h_t[:, k, :], ps[:, 4 + k // 2, (k % 2) * T:(k % 2 + 1) * T], mod_a[:, KT + k:KT + k + 1], mod_a[:, k:k + 1],
                                  ALU.mult, ALU.add).then_inc(h_dve, 1)
            ang, turns_, red = tmp_a, sin_t, cos_t
            dve.wait_ge(small_loaded, 16 * 6)
            step(dve.tensor_copy(ang, tmp_b.bitcast(I32)))
            step(dve.tensor_scalar(neg_sinks[:, :], sinks[:, :], -1.0, None, ALU.mult))
            then()
            step(dve.tensor_scalar(ang, ang, freq[:, 0:1], None, ALU.mult))
            then()
            step(dve.tensor_scalar(turns_, ang, 1.0 / (2.0 * np.pi), 12582912.0, ALU.mult, ALU.add))
            then()
            step(dve.tensor_scalar(turns_, turns_, 12582912.0, None, ALU.subtract))
            two_pi = 2.0 * np.pi
            hi = 6.28125
            mid = float(np.float32(np.round((two_pi - hi) * 2 ** 20) / 2 ** 20))
            lo = float(np.float32(two_pi - hi - mid))
            src = ang
            for part in (hi, mid, lo):
                then()
                step(dve.scalar_tensor_tensor(red, turns_, -part, src, ALU.mult, ALU.add))
                src = red
            then()
            dve.tensor_scalar(red, red, 3.1415925, -3.1415925, ALU.min, ALU.max).then_inc(angle_done, 1)
            dve.wait_ge(sin_done, 2)
            step(dve.tensor_tensor(tmp_a, tmp_a, tmp_a, ALU.mult))
            for quad in (0, 2):
                step(dve.tensor_scalar(sin_t[32 * quad:32 * (quad + 1), :], sin_t[32 * quad:32 * (quad + 1), :], -1.0, None,
                                       ALU.mult))
            then()
            dve.tensor_scalar(cos_t, tmp_a, -2.0, 1.0, ALU.mult, ALU.add).then_inc(rope_done, 1)

            dve.wait_ge(sp_done, 1)
            for i, f in enumerate((-LRU_C, LRU_C)):
                ins = dve.tensor_scalar(decay[:, i, :], stats[:, 4:12], f, None, ALU.mult)
            ins.then_inc(decay_done, 1)
            dve.tensor_scalar(half_bias[:, :], cols[:, R_BIN + LY0 // P:R_BIN + (LY0 + 3 * D) // P], 0.5, None, ALU.mult).then_inc(half_done, 1)

            def conv(c):
                dve.wait_ge(proj_read, c + 1)
                for tap in range(CONV - 1, -1, -1):
                    if tap < CONV - 1:
                        then()
                    for n in (2 * c, 2 * c + 1):
                        w = cols[:, R_CONVW + KT * tap + n:R_CONVW + KT * tap + n + 1]
                        if tap == CONV - 1:
                            ins = dve.tensor_scalar(xc[:, n, :], lx[:, n, tap:tap + T], w,
                                                    cols[:, R_CONVB + n:R_CONVB + n + 1], ALU.mult, ALU.add)
                        else:
                            ins = dve.scalar_tensor_tensor(xc[:, n, :], lx[:, n, tap:tap + T], w, xc[:, n, :], ALU.mult, ALU.add)
                        if tap:
                            step(ins)
                        else:
                            ins.then_inc(conv_done, 1)

            def rope(c):
                raw = qk_raw[:, c % 2]
                dst = q_r[:, 2 * c:2 * c + 2, :] if c < 4 else k_r
                dve.wait_ge(proj_read, len(LX) + c + 1)
                dve.wait_ge(rope_done, 1)
                if c:
                    dve.wait_ge(rope_q, c)
                for quad in range(4):
                    other = quad ^ 1
                    ins = dve.tensor_copy(swap[32 * quad:32 * (quad + 1)], raw[32 * other:32 * (other + 1)])
                ins.then_inc(swapped, 1)
                step(dve.tensor_tensor(dst, raw, cos_t[:, None, :].broadcast_to([P, 2, T]), ALU.mult))
                dve.wait_ge(times_sin, c + 1)
                then()
                dve.tensor_tensor(dst, dst, swap, ALU.add).then_inc(rope_q, 1)

            for c in range(4):
                conv(c)
            for c in range(5):
                rope(c)
            dve.wait_ge(rope_q, 5)
            for g in range(KV_HEADS):
                for half in range(2):
                    ins = dve.tensor_copy(k_rep[64 * half:64 * (half + 1), g, :], k_r[64 * (g % 2):64 * (g % 2 + 1), g // 2, :])
            ins.then_inc(k_rep_done, 1)
            dve.wait_ge(chunk_used, VC + 1)
            dve.tensor_tensor(v_sb[:, :, :], ps[:, 1, :].rearrange("p (t n) -> p t n", t=TT),
                              b_v[:, None, :].broadcast_to([P, TT, PROJ_W]), ALU.add).then_inc(v_done, 1)

            def lru_squares(b):
                for n in range(4):
                    dve.wait_ge(th_done, 4 * b + n + 1)
                    step(dve.tensor_tensor(lru_tmp[:, n % 2, :], g_a[:, n, :], g_a[:, n, :], ALU.mult))
                    then()
                    dve.scalar_tensor_tensor(g_r[:, n, :], lru_tmp[:, n % 2, :], 1.0, g_r[:, n, :], ALU.add,
                                             ALU.mult).then_inc(m2_done, 1)

            def lru_states(b):
                for n in range(4):
                    dve.wait_ge(mult_done, b + 1)
                    dve.wait_ge(ix_done, 4 * b + n + 1)
                    dve.tensor_tensor(g_i[:, n, :], g_i[:, n, :], g_r[:, n, :], ALU.mult).then_inc(u_done, 1)
                for n in range(4):
                    dve.wait_ge(u_done, 4 * b + n + 1)
                    dve.tensor_tensor_scan(xc[:, 4 * b + n, :], g_a[:, n, :], g_i[:, n, :], 0.0, ALU.mult,
                                           ALU.add).then_inc(state_done, 1)

            def softmax_max(g):
                dve.wait_ge(scores_ps, g + 1)
                if g:
                    dve.wait_ge(pv_ps, GROUP * g)
                for h in range(GROUP):
                    dve.tensor_tensor_reduce(prob[:, h, 0:P], ps[:, 4 + h, 0:P], mask[:, 1, :], 1.0, NEG, ALU.add, ALU.max,
                                             smax[:, h, 0:1])
                    ins = dve.tensor_tensor_reduce(prob[:, h, P:3 * P], ps[:, 4 + h, P:3 * P],
                                                   mask[:, :, :].rearrange("p a b -> p (a b)"), 1.0, NEG,
                                                   ALU.add, ALU.max, smax[:, h, 1:2])
                step(ins)
                then()
                step(dve.tensor_scalar(smax[:, :, :], smax[:, :, :], -HEAD_DIM ** -0.5, None, ALU.mult))
                then()
                sink = sinks[:, GROUP * g:GROUP * (g + 1), None].broadcast_to([P, GROUP, 2])
                nsink = neg_sinks[:, GROUP * g:GROUP * (g + 1), None].broadcast_to([P, GROUP, 2])
                step(dve.tensor_tensor(smax[:, :, :], smax[:, :, :], nsink, ALU.min))
                then()
                dve.tensor_tensor(snk[:, :, :], smax[:, :, :], sink, ALU.add).then_inc(smax_done, 1)

            def softmax_scale(g):
                dve.wait_ge(exp_done, g + 1)
                step(dve.tensor_tensor(ssum[:, :, :], ssum[:, :, :], snk[:, :, :], ALU.add))
                then()
                step(dve.reciprocal(ssum[:, :, :], ssum[:, :, :]))
                then()
                for h in range(GROUP):
                    dve.tensor_scalar(prob[:, h, 0:P], prob[:, h, 0:P], ssum[:, h, 0:1], None, ALU.mult)
                    dve.tensor_scalar(prob[:, h, P:3 * P], prob[:, h, P:3 * P], ssum[:, h, 1:2], None,
                                      ALU.mult).then_inc(prob_done, 1)

            def attn_out(g):
                for m in range(2 * g, 2 * g + 2):
                    dve.wait_ge(pv_ps, 2 * m + 2)
                    dve.wait_ge(lg_done, m + 1)
                    dve.tensor_scalar(attn[:, m, :], ps[:, 2 + m % 2, 0:T], 0.5, None, ALU.mult).then_inc(attn_done, 1)

            def gelu_in(n):
                i = n % 2
                dve.wait_ge(ly_in, n + 1)
                step(dve.tensor_scalar(ly2[:, i, :], ly2[:, i, :], GELU_A, 1.0, ALU.mult, ALU.add))
                then()
                dve.tensor_tensor(ly2[:, i, :], ly2[:, i, :], ly[:, i, :], ALU.mult).then_inc(z_done, 1)

            def gelu_out(n):
                dve.wait_ge(zsig_done, n + 1)
                dve.scalar_tensor_tensor(attn[:, n, :], sg[:, n % 2, :], 1.0, ly[:, n % 2, :], ALU.add, ALU.mult).then_inc(gelu_done, 1)

            def state_gelu(n):
                dve.wait_ge(state_done, n + 1)
                dve.wait_ge(gelu_done, n + 1)
                dve.tensor_tensor(xc[:, n, :], xc[:, n, :], attn[:, n, :], ALU.mult).then_inc(lg_done, 1)

            def gate_lru(n):
                dve.wait_ge(gate_in, n + 1)
                dve.wait_ge(lg_done, n + 1)
                dve.scalar_tensor_tensor(xc[:, n, :], gate[:, n % 2, :], 1.0, xc[:, n, :], ALU.add, ALU.mult).then_inc(gate_used, 1)

            def gate_attn(n):
                dve.wait_ge(gate_in, KT + n + 1)
                dve.wait_ge(attn_done, n + 1)
                dve.scalar_tensor_tensor(attn[:, n, :], gate[:, n % 2, :], 1.0, attn[:, n, :], ALU.add, ALU.mult).then_inc(gate_used, 1)
                dve.wait_ge(gate_used, KT + n + 1)
                dve.scalar_tensor_tensor(attn[:, n, :], xc[:, n, :], 0.25, attn[:, n, :], ALU.mult, ALU.add).then_inc(merged, 1)

            lru_squares(0)
            gelu_in(0)
            gelu_out(0)
            softmax_max(0)
            gelu_in(1)
            gelu_out(1)
            softmax_scale(0)
            lru_states(0)
            state_gelu(0)
            state_gelu(1)
            for n in (2, 3):
                gelu_in(n)
                gelu_out(n)
                state_gelu(n)
            for n in (4, 5):
                gelu_in(n)
                gelu_out(n)
            attn_out(0)
            softmax_max(1)
            softmax_scale(1)
            lru_squares(1)
            for n in (6, 7):
                gelu_in(n)
                gelu_out(n)
            attn_out(1)
            softmax_max(2)
            softmax_scale(2)
            gate_lru(0)
            gate_lru(1)
            lru_states(1)
            for n in range(4, 8):
                state_gelu(n)
            for n in range(2, 6):
                gate_lru(n)
            attn_out(2)
            softmax_max(3)
            softmax_scale(3)
            gate_lru(6)
            gate_lru(7)
            gate_attn(0)
            gate_attn(1)
            attn_out(3)

            def bias_part(q, count):
                raw, part = b_out[32 * q:32 * (q + 1), :], b_out_parts[32 * q:32 * (q + 1), :]
                step(dve.tensor_tensor(raw, raw, part, ALU.subtract))
                then()
                dve.tensor_copy(part, raw).then_inc(bias_split, 1)
                dve.wait_ge(bias_split, count)

            dve.wait_ge(x_again, 16 * 4)
            dve.wait_ge(pv_ps, HEADS)
            dve.tensor_copy(b_out_parts, b_out).then_inc(bias_split, 1)
            dve.wait_ge(bias_split, 1)
            bias_part(1, 2)
            for n in range(2, KT):
                gate_attn(n)
                if n in (3, 5):
                    bias_part(2, 3 + (n - 3) // 2)

            dve.wait_ge(late_loaded, 16 * 16)
            dve.wait_ge(chunk_used, ADA_B[SH2][-1] + 1)
            step(dve.tensor_tensor(mod_row[:, 0:2, :], ps[:, 4, :].rearrange("p (v n) -> p v n", v=2), bada_row[:, 0:2, :], ALU.add))
            then()
            dve.tensor_tensor(mod_row[:, G1, :], mod_row[:, G1, :], gain_row[:, G1, :], ALU.mult).then_inc(mod_row_done, 1)

            def y_tile(t):
                return ps[:, 2 * t:2 * t + 2, :].rearrange("p a b -> p (a b)")

            bc_tile = ps[:, 6:8, :].rearrange("p a b -> p (a b)")
            dve.wait_ge(bc_done, 2)
            for t in range(TT):
                dve.wait_ge(y_sq, t + 1)
                step(dve.reciprocal(stats[:, 2 + t:3 + t], stats[:, t:t + 1]))
                then()
                step(dve.scalar_tensor_tensor(y_g[:, t, :], y_tile(t), stats[:, 2 + t:3 + t], g1_bc, ALU.mult, ALU.mult))
                then()
                dve.tensor_tensor(x1[:, t, :], x1[:, t, :], y_g[:, t, :], ALU.add).then_inc(x1_done, 1)
            dve.wait_ge(chunk_used, ADA_B[SC2][-1] + 1)
            step(dve.scalar_tensor_tensor(mod_row[:, SC2, :], ps[:, 5, 0:256], 1.0, bada_row[:, SC2, :], ALU.add, ALU.add))
            then()
            dve.tensor_tensor(mod_row[:, SC2, :], mod_row[:, SC2, :], gain_row[:, SC2, :], ALU.mult).then_inc(mod_row_done, 1)
            for t in range(TT):
                dve.wait_ge(x1_sq, t + 1)
                step(dve.reciprocal(stats[:, 6 + t:7 + t], stats[:, 4 + t:5 + t]))
                dve.wait_ge(bc_ps, 3)
                then()
                step(dve.scalar_tensor_tensor(h2[:, t, :], x1[:, t, :], stats[:, 6 + t:7 + t], bc_tile, ALU.mult, ALU.mult))
                then()
                dve.tensor_tensor(h2[:, t, :], h2[:, t, :], sh2_bc, ALU.add).then_inc(h2_done, 1)
            for t in range(TT):
                dve.wait_ge(h2_t_ps, t + 1)
                dve.tensor_copy(h2_t[:, 0:4, t * P:(t + 1) * P], ps[:, 2 * t, :].rearrange("p (k t) -> p k t", k=4)).then_inc(h2_t_dve, 1)
            dve.wait_ge(part_ps, 1)
            dve.tensor_copy(logit_part, ps[:, 5, 0:T]).then_inc(part_done, 1)
            dve.wait_ge(chunk_used, ADA_B[GT2][-1] + 1)
            step(dve.tensor_tensor(mod_row[:, GT2, :], ps[:, 4, 0:256], bada_row[:, GT2, :], ALU.add))
            then()
            dve.tensor_tensor(mod_row[:, GT2, :], mod_row[:, GT2, :], gain_row[:, GT2, :], ALU.mult).then_inc(mod_row_done, 1)

            dve.wait_ge(logits_ps, 1)
            step(dve.tensor_tensor(logits[:, :, :], ps[:, 5, 0:TT * EXPERTS].rearrange("p (t e) -> p t e", t=TT),
                                   b_rt[:, None, :].broadcast_to([P, TT, EXPERTS]), ALU.add))
            then()
            for t in range(TT):
                step(dve.max(top8[:, t, :], logits[:, t, :]))
            then()
            dve.tensor_scalar(neg_max[:, :, :], top8[:, :, 0:1], -1.0, None, ALU.mult).then_inc(top_done, 1)
            for t in range(TT):
                step(dve.max_index(top_i[:, t, :], top8[:, t, :], logits[:, t, :]))
            then()
            step(dve.tensor_copy(top_f[:, :, :], top_i[:, :, :]))
            then()
            for t in range(TT):
                step(dve.tensor_tensor(match[:, t, :, :], expert_no[:, None, :].broadcast_to([P, TOP_K, EXPERTS]),
                                       top_f[:, t, 0:TOP_K, None].broadcast_to([P, TOP_K, EXPERTS]), ALU.is_equal))
            then()
            step(dve.tensor_tensor(match[:, :, 0:2, :], match[:, :, 0:2, :], match[:, :, 2:4, :], ALU.add))
            then()
            step(dve.tensor_tensor(hit[:, :, :], match[:, :, 0, :], match[:, :, 1, :], ALU.add))
            then()
            dve.tensor_copy(hit_b[:, :, :], hit[:, :, :]).then_inc(route_done, 1)
            dve.wait_ge(topexp_done, TT)
            for t in range(TT):
                step(dve.tensor_tensor_reduce(route_w[:, t, :], soft[:, t, :], hit[:, t, :], 1.0, 0.0, ALU.mult, ALU.add,
                                              sums[:, t, 0:1]))
            then()
            step(dve.reciprocal(sums[:, :, :], sums[:, :, :]))
            then()
            dve.tensor_tensor(route_w[:, :, :], route_w[:, :, :], sums[:, :, :].broadcast_to([P, TT, EXPERTS]),
                              ALU.mult).then_inc(route_done, 1)
            dve.wait_ge(rank_ps, 1)
            step(dve.reduce_max(passes_f[:, 0:1], ps[:, 5, 2 * EXPERTS:3 * EXPERTS], axis=AX.X))
            step(dve.scalar_tensor_tensor(rank[:, :, 0:EXPERTS], ps[:, 5, 0:2 * EXPERTS].rearrange("p (t e) -> p t e", t=TT), 1.0,
                                          hit[:, :, :], ALU.add, ALU.mult))
            then()
            step(dve.tensor_scalar(rank[:, :, 0:EXPERTS], rank[:, :, 0:EXPERTS], 1.0, None, ALU.subtract))
            then()

            def pick_tokens(e):
                for t in range(TT):
                    dve.tensor_scalar(pick[:, t, :], slot_no[:, 0, :], rank[:, t, e], None, ALU.is_equal)
                dve.tensor_scalar(bias_pick[:, :], ones[0:EXPERTS, 0:BLOCK], expert_hot[:, e], None, ALU.mult).then_inc(picked, 1)

            pick_tokens(slice(0, 1))
            for i in range(1, PASSES):
                step(dve.tensor_scalar(passes_f[:, i:i + 1], passes_f[:, 0:1], float(i * BLOCK), None, ALU.is_gt))
            then()
            step(dve.tensor_scalar(rank[:, :, EXPERTS:], rank[:, :, 0:1], float(BLOCK), None, ALU.subtract))
            step(dve.tensor_tensor(passes_f[:, 1:2], passes_f[:, 1:2], passes_f[:, 2:3], ALU.add))
            then()
            dve.wait_ge(route_t_ps, 1)
            dve.wait_ge(zero_set, 1)
            for c in range(2):
                ins = dve.tensor_copy(scat_t[64 * c:64 * c + EXPERTS, :, :],
                                      ps[0:EXPERTS, 4, 0:T].rearrange("p (t s) -> p t s", t=TT))
            ins.then_inc(route_t_done, 1)
            dve.tensor_tensor(more_i[:, :], passes_f[:, 1:2], passes_f[:, 3:4], ALU.add).then_inc(rank_done, 1)
            dve.wait_ge(gathered, 1)
            dve.tensor_copy(hsel[:, :, :], ps[:, 7, :].rearrange("p (k s) -> p k s", k=KT)).then_inc(hsel_done, 1)

            def experts(turn, q, p):
                for r in range(UNROLL):
                    done = turn * UNROLL + r
                    e = q * UNROLL + r
                    if p is not None and r == 0:
                        dve.wait_ge(rank_done, p + 2)
                    dve.wait_ge(chunk_used, turn * (UNROLL * EXPERT_CHUNKS) + (MIXER_CHUNKS + r * EXPERT_CHUNKS + 1))
                    for t in range(TT):
                        dve.tensor_scalar(scat[:, t].rearrange("p a s -> p (a s)"), slot_no[:, :, :].rearrange("p a s -> p (a s)"),
                                          rank[:, t, bass.ds(e, 1)], route_w[:, t, bass.ds(e, 1)], ALU.is_equal, ALU.mult)
                    pick_tokens(bass.ds(e + 1, 1))
                    dve.wait_ge(chunk_used, turn * (UNROLL * EXPERT_CHUNKS) + MIXER_CHUNKS + r * EXPERT_CHUNKS + E1_CHUNKS)
                    dve.tensor_scalar(g_c, ps[:, 4, :], LIMIT, None, ALU.min).then_inc(g_done, 1)
                    dve.tensor_scalar(u_c, ps[:, 5, :], LIMIT, -LIMIT, ALU.min, ALU.max).then_inc(g_done, 1)
                    dve.wait_ge(g_done, done * 3 + 2)
                    dve.scalar_tensor_tensor(u_c, u_c, 1.0, g_c, ALU.add, ALU.mult).then_inc(g_done, 1)
                    dve.wait_ge(sig_done, done + 1)
                    dve.wait_ge(g_done, done * 3 + 3)
                    dve.tensor_tensor(g_u, u_c, s_g, ALU.mult).then_inc(act_done, 1)
                    dve.wait_ge(gathered, done + 2)
                    dve.tensor_copy(hsel[:, :, :], ps[:, 7, :].rearrange("p (k s) -> p k s", k=KT)).then_inc(hsel_done, 1)
                    dve.wait_ge(act_t_ps, done * 2 + 1)
                    dve.tensor_copy(act_t[:, 0:2].rearrange("p a b c -> p (a b c)"), ps[:, 6, 0:T]).then_inc(act_t_d, 1)
                    dve.wait_ge(chunk_used, turn * (UNROLL * EXPERT_CHUNKS) + MIXER_CHUNKS + (r + 1) * EXPERT_CHUNKS)
                    dve.tensor_copy(o_sb, ps[:, 6, :]).then_inc(o_done, 1)

            def next_pass(p):
                dve.wait_ge(picked, (p + 1) * EXPERTS + 1)
                dve.tensor_scalar(rank[:, :, :], rank[:, :, :], float(BLOCK), None, ALU.subtract).then_inc(rank_done, 1)

            more = all_experts(dve, experts, next_pass)

            for t in range(TT):
                dve.wait_ge(y2_sq, t + 1)
                step(dve.reciprocal(stats[:, 10 + t:11 + t], stats[:, 8 + t:9 + t]))
                then()
                step(dve.scalar_tensor_tensor(fin[:, t, :], ps[:, 2 * t:2 * t + 2, :].rearrange("p a b -> p (a b)"),
                                              stats[:, 10 + t:11 + t], g2_bc, ALU.mult, ALU.mult))
                then()
                dve.tensor_tensor(fin[:, t, :], fin[:, t, :], x1[:, t, :], ALU.add).then_inc(fin_done, 1)

        @block.scalar
        def _(act):
            def load(dst, src, s):
                act.dma_start(dst, src).then_inc(s, 16)

            load(x_in, a["x"][0].rearrange("(t p) d -> p t d", p=P), x_loaded)
            for at, n, name in ((R_BIN, (LX0 + 4 * D) // P, "b_in"), (R_CONVB, KT, "conv_b"), (R_BRG, KT, "b_rg"),
                                (R_BIG, KT, "b_ig"), (R_LRUA, KT, "lru_a")):
                load(rows[at:at + n, :], a[name].rearrange("l (r p) -> (l r) p", p=P), rows_loaded)
            load(rows[R_CONVW:R_CONVW + CONV * KT, :], a["conv_w"][0].rearrange("t (r p) -> (t r) p", p=P), rows_loaded)
            load(freq[:, :], a["inv_freq"], small_loaded)
            load(tmp_b.bitcast(I32), a["positions"][0:1, :].broadcast_to([P, T]), small_loaded)
            load(sinks[:, :], a["sinks"][0:1, :].broadcast_to([P, HEADS]), small_loaded)
            load(b_v[:, :], a["b_in"][0:1, V0:V0 + PROJ_W].broadcast_to([P, PROJ_W]), small_loaded)
            load(b_rt[:, :], a["b_router"][0:1, :].broadcast_to([P, EXPERTS]), small_loaded)
            load(w_rt[:, :, :], a["w_router"][0].rearrange("(k p) e -> p k e", p=P), small_loaded)

            act.wait_ge(eps_set, 1)
            act.wait_ge(x_loaded, 16)
            for t in range(TT):
                ins = act.activation(x_n[:, t, :], x_in[:, t, :], ACT.Square, accum_out=stats[:, t:t + 1])
            ins.then_inc(act_step, 1)
            act.wait_ge(act_step, 1)
            act.activation(stats[:, 0:2], stats[:, 0:2], ACT.Sqrt, bias=eps[:, 0:1], scale=1.0 / D).then_inc(x_sq, 1)
            act.wait_ge(cols_done, 1)
            act.activation(silu_c[:, :], cols_a[:, R_C:R_C + KT], ACT.Sigmoid).then_inc(c_sig, 1)
            act.wait_ge(cols_done, 2)
            act.activation(stats[:, 4:12], cols[:, R_LRUA:R_LRUA + KT], ACT.Exp).then_inc(act_step, 1)
            act.wait_ge(act_step, 2)
            act.activation(stats[:, 4:12], stats[:, 4:12], ACT.Ln, bias=1.0).then_inc(sp_done, 1)
            act.wait_ge(mod_done, 1)
            act.wait_ge(xn_t, TT)
            for k in range(KT // 2, KT):
                act.activation(h_t[:, k, :], ps[:, 4 + k // 2, (k % 2) * T:(k % 2 + 1) * T], ACT.Identity, bias=mod_a[:, k:k + 1],
                               scale=mod_a[:, KT + k:KT + k + 1]).then_inc(h_act, 1)

            act.wait_ge(angle_done, 1)
            act.activation(sin_t, cos_t, ACT.Sin).then_inc(sin_done, 1)
            act.activation(tmp_a, cos_t, ACT.Sin, scale=0.5).then_inc(sin_done, 1)
            act.wait_ge(gain_set, 1)
            for v, name in ((G1, "g_post_mix"), (SC2, "g_pre_ffn"), (GT2, "g_post_ffn")):
                for quad in range(4):
                    load(gain_row[32 * quad:32 * quad + 1, v, :], a[name][0:1, 256 * quad:256 * (quad + 1)], late_loaded)

            act.wait_ge(pad_set, 1)
            def bias_in(base, n):
                at = R_BIN + base // P + n
                return cols[:, at:at + 1]

            for c in range(4):
                act.wait_ge(chunk_used, LX[c] + 1)
                for i in range(2):
                    ins = act.activation(lx[:, 2 * c + i, CONV - 1:], ps[:, c % 2, i * T:(i + 1) * T], ACT.Identity,
                                         bias=bias_in(LX0, 2 * c + i))
                ins.then_inc(proj_read, 1)
            for c in range(5):
                act.wait_ge(chunk_used, (QC[c] if c < 4 else KC) + 1)
                if c >= 2:
                    act.wait_ge(rope_q, c - 1)
                for i in range(2):
                    ins = act.activation(qk_raw[:, c % 2, i, :], ps[:, c % 2, i * T:(i + 1) * T], ACT.Identity,
                                         bias=cols[:, R_BIN + 2 * c + i:R_BIN + 2 * c + i + 1])
                ins.then_inc(proj_read, 1)

            def gate_sigmoids(b):
                for n in range(4 * b, 4 * b + 4):
                    if n % 4 == 3:
                        act.wait_ge(chunk_used, GATES[b] + 1)
                    else:
                        act.wait_ge(gates_ps, 3 * b + n % 4 + 1)
                    if n == 4:
                        act.wait_ge(state_done, 4)
                    act.activation(g_r[:, n % 4, :], ps[:, 2 + n % 2, 0:T], ACT.Sigmoid, bias=cols[:, R_BRG + n:R_BRG + n + 1])
                    act.activation(g_i[:, n % 4, :], ps[:, 2 + n % 2, T:2 * T], ACT.Sigmoid,
                                   bias=cols[:, R_BIG + n:R_BIG + n + 1]).then_inc(gates_read, 1)

            def gate_powers(b):
                act.wait_ge(decay_done, 1)
                for n in range(4 * b, 4 * b + 4):
                    act.wait_ge(gates_read, n + 1)
                    act.activation(g_a[:, n % 4, :], g_r[:, n % 4, :], ACT.Exp, scale=decay[:, 0, n:n + 1]).then_inc(a_done, 1)
                for n in range(4 * b, 4 * b + 4):
                    act.wait_ge(a_done, n + 1)
                    act.activation(g_r[:, n % 4, :], g_r[:, n % 4, :], ACT.Tanh, scale=decay[:, 1, n:n + 1]).then_inc(th_done, 1)

            def gate_roots(b):
                act.wait_ge(m2_done, 4 * b + 4)
                act.activation(z_gate[:, 0:1024], z_gate[:, 0:1024], ACT.Sqrt).then_inc(mult_done, 1)

            def exps(g):
                act.wait_ge(smax_done, g + 1)
                for h in range(GROUP):
                    for b, sl in ((0, slice(0, P)), (1, slice(P, 3 * P))):
                        act.activation(prob[:, h, sl], prob[:, h, sl], ACT.Exp, bias=smax[:, h, b:b + 1],
                                       scale=HEAD_DIM ** -0.5, accum_out=ssum[:, h, b:b + 1])
                act.activation(snk[:, :, :], snk[:, :, :], ACT.Exp).then_inc(exp_done, 1)

            def prob_t(g):
                for h in range(GROUP):
                    act.wait_ge(prob_t_ps, GROUP * g + h + 1)
                    act.activation(prob[:, h, :], ps[:, 4 + h, 0:3 * P], ACT.Copy).then_inc(prob_t_done, 1)

            def read_ly(n):
                i = n % 2
                j = PROJ.index(LY[n // 2])
                if i == 0:
                    act.wait_ge(chunk_used, LY[n // 2] + 1)
                if n == 0:
                    act.wait_ge(rope_q, 5)
                if n >= 2:
                    act.wait_ge(gelu_done, n - 1)
                src = ps[:, j % 2, i * T:(i + 1) * T]
                act.activation(ly[:, i, :], src, ACT.Identity, bias=bias_in(LY0, n))
                act.activation(ly2[:, i, :], src, ACT.Square, bias=bias_in(LY0, n)).then_inc(ly_in, 1)

            def gelu_sig(n):
                act.wait_ge(z_done, n + 1)
                act.activation(sg[:, n % 2, :], ly2[:, n % 2, :], ACT.Tanh, scale=GELU_B).then_inc(zsig_done, 1)

            def read_gate(n):
                base, m = (GL0, n) if n < KT else (GA0, n - KT)
                chunk = (GL if n < KT else GA)[m // 2]
                i = n % 2
                if i == 0:
                    act.wait_ge(chunk_used, chunk + 1)
                if n >= 2:
                    act.wait_ge(gate_used, n - 1)
                act.activation(gate[:, i, :], ps[:, PROJ.index(chunk) % 2, i * T:(i + 1) * T], ACT.Tanh,
                               bias=half_bias[:, base // P - LY0 // P + m:base // P - LY0 // P + m + 1],
                               scale=0.5).then_inc(gate_in, 1)

            gate_sigmoids(0)
            gate_powers(0)
            for n in (0, 1):
                read_ly(n)
                gelu_sig(n)
            exps(0)
            gate_roots(0)
            read_ly(2)
            prob_t(0)
            gelu_sig(2)
            read_ly(3)
            gelu_sig(3)
            gate_sigmoids(1)
            for n in (4, 5):
                read_ly(n)
                gelu_sig(n)
            exps(1)
            gate_powers(1)
            read_ly(6)
            prob_t(1)
            gelu_sig(6)
            read_ly(7)
            gelu_sig(7)
            act.wait_ge(half_done, 1)
            read_gate(0)
            read_gate(1)
            exps(2)
            gate_roots(1)
            read_gate(2)
            read_gate(3)
            prob_t(2)
            read_gate(4)
            read_gate(5)
            act.wait_ge(state_done, KT)
            load(x1, a["x"][0].rearrange("(t p) d -> p t d", p=P), x_again)
            act.wait_ge(pool_set, 11)
            for q in range(3):
                load(b_out[32 * q:32 * q + 1, :], a["b_out"][0:1, :], x_again)
            act.wait_ge(gelu_done, KT)
            for quad in range(4):
                src = a["b_ada"][0:1, 2 * D:6 * D].rearrange("l (v c n) -> l v c n", v=4, c=4)[:, :, quad, :]
                load(bada_row[32 * quad:32 * quad + 1, :, :], src, late_loaded)
            exps(3)
            read_gate(6)
            read_gate(7)
            prob_t(3)
            for n in range(8, 2 * KT):
                read_gate(n)
            act.wait_ge(merged, KT)
            load(b_e1[0:EXPERTS, :], a["b_e1"][0], moe_loaded)
            act.wait_ge(bias_split, 4)
            for c in range(2):
                load(b_e2[64 * c:64 * c + EXPERTS, :], a["b_e2"][0, :, 512 * c:512 * (c + 1)], moe_loaded)
            act.wait_ge(bc_ps, 1)
            act.activation(g1_bc, ps[:, 6:8, :].rearrange("p a b -> p (a b)"), ACT.Copy).then_inc(bc_done, 1)
            act.wait_ge(bc_ps, 2)
            act.activation(sh2_bc, ps[:, 6:8, :].rearrange("p a b -> p (a b)"), ACT.Copy).then_inc(bc_done, 1)

            act.activation(stats[:, 12:13], eps[:, 0:1], ACT.Sqrt)
            for t in range(TT):
                if t == 0:
                    act.wait_ge(y_ps, 1)
                else:
                    act.wait_ge(chunk_used, WO[-1] + 1)
                act.activation(junk, ps[:, 2 * t:2 * t + 2, :].rearrange("p a b -> p (a b)"), ACT.Square,
                               accum_out=stats[:, t:t + 1]).then_inc(act_step, 1)
                act.wait_ge(act_step, 3 + t)
                act.activation(stats[:, t:t + 1], stats[:, t:t + 1], ACT.Sqrt, bias=eps[:, 0:1], scale=1.0 / D).then_inc(y_sq, 1)
            for t in range(TT):
                act.wait_ge(x1_done, t + 1)
                act.activation(junk, x1[:, t, :], ACT.Square, accum_out=stats[:, 4 + t:5 + t]).then_inc(act_step, 1)
                act.wait_ge(act_step, 5 + t)
                act.activation(stats[:, 4 + t:5 + t], stats[:, 4 + t:5 + t], ACT.Sqrt, bias=eps[:, 0:1],
                               scale=1.0 / D).then_inc(x1_sq, 1)
            for t in range(TT):
                act.wait_ge(h2_t_ps, t + 1)
                act.activation(h2_t[:, 4:8, t * P:(t + 1) * P], ps[:, 2 * t + 1, :].rearrange("p (k t) -> p k t", k=4),
                               ACT.Copy).then_inc(h2_t_act, 1)
            act.wait_ge(top_done, 1)
            for t in range(TT):
                act.activation(soft[:, t, :], logits[:, t, :], ACT.Exp, bias=neg_max[:, t, :]).then_inc(topexp_done, 1)
            act.wait_ge(bc_ps, 4)
            act.activation(g2_bc, ps[:, 6:8, :].rearrange("p a b -> p (a b)"), ACT.Copy).then_inc(bc_done, 1)

            def experts(turn, q, p):
                for r in range(UNROLL):
                    done = turn * UNROLL + r
                    act.wait_ge(g_done, done * 3 + 1)
                    act.activation(s_g, g_c, ACT.Sigmoid, scale=ALPHA).then_inc(sig_done, 1)
                    act.wait_ge(act_t_ps, done * 2 + 1)
                    act.activation(act_t[:, 2:4].rearrange("p a b c -> p (a b c)"), ps[:, 5, 0:T], ACT.Copy).then_inc(act_t_a, 1)
                    act.wait_ge(act_t_ps, done * 2 + 2)
                    act.activation(scat_t[:, :, :], ps[:, 4, 0:T].rearrange("p (t s) -> p t s", t=TT), ACT.Copy).then_inc(scat_t_done, 1)

            more = all_experts(act, experts)

            act.activation(stats[:, 12:13], eps[:, 0:1], ACT.Sqrt)
            for t in range(TT):
                act.wait_ge(combined, more * (TT * EXPERTS) + (TT * EXPERTS + TT + t))
                act.activation(junk, ps[:, 2 * t:2 * t + 2, :].rearrange("p a b -> p (a b)"), ACT.Square,
                               accum_out=stats[:, 8 + t:9 + t]).then_inc(act_step, 1)
                act.wait_ge(act_step, 7 + t)
                act.activation(stats[:, 8 + t:9 + t], stats[:, 8 + t:9 + t], ACT.Sqrt, bias=eps[:, 0:1],
                               scale=1.0 / D).then_inc(y2_sq, 1)
            for t in range(TT):
                act.wait_ge(fin_done, t + 1)
                act.dma_start(out[0, t * P:(t + 1) * P, :], fin[:, t, :]).then_inc(out_stored, 16)
            act.wait_ge(out_stored, 16 * TT)

        @block.gpsimd
        def _(pool):
            pool.memset(gain_row[:, :, :], 1.0).then_inc(gain_set, 1)
            pool.memset(ones[:, :], 1.0).then_inc(pool_set, 1)
            pool.memset(ident[:, :], 0.0).then_inc(pool_set, 1)
            pool.memset(mask[:, :, :], 0.0).then_inc(pool_set, 1)
            pool.wait_ge(pool_set, 3)
            pool.affine_select(out=ident[:, :], in_=ident[:, :], compare_op=ALU.not_equal, fill=1.0, base=0,
                               pattern=[[-1, P]], channel_multiplier=1).then_inc(pool_set, 1)
            pool.affine_select(out=mask[:, 1, :], in_=mask[:, 1, :], compare_op=ALU.is_ge, fill=NEG, base=0,
                               pattern=[[-1, P]], channel_multiplier=1).then_inc(pool_set, 1)
            pool.affine_select(out=mask[:, 0, :], in_=mask[:, 0, :], compare_op=ALU.is_gt, fill=NEG, base=0,
                               pattern=[[1, P]], channel_multiplier=-1).then_inc(pool_set, 1)
            pool.memset(ones_b[:, :], 1.0).then_inc(pool_set, 1)
            pool.wait_ge(pool_set, 7)
            pool.affine_select(out=before[:, :], in_=ones_b[:, :], compare_op=ALU.is_gt, fill=0.0, base=0,
                               pattern=[[1, P]], channel_multiplier=-1).then_inc(pool_set, 1)
            pool.iota(slot_no[:, :, :], pattern=[[0, 2], [1, BLOCK]], base=0, channel_multiplier=0,
                      allow_small_or_imprecise_dtypes=True).then_inc(pool_set, 1)
            pool.iota(expert_no[:, :], pattern=[[1, EXPERTS]], base=0, channel_multiplier=0,
                      allow_small_or_imprecise_dtypes=True).then_inc(pool_set, 1)
            pool.wait_ge(xn_done, TT)
            pool.memset(lx[:, :, 0:CONV - 1], 0.0).then_inc(pad_set, 1)
            for c in range(5):
                pool.wait_ge(swapped, c + 1)
                pool.tensor_tensor(swap, swap, sin_t[:, None, :].broadcast_to([P, 2, T]), ALU.mult).then_inc(times_sin, 1)
            for n in range(KT):
                pool.wait_ge(gates_read, n + 1)
                pool.tensor_tensor(g_i[:, n % 4, :], g_i[:, n % 4, :], xc[:, n, :], ALU.mult).then_inc(ix_done, 1)
            pool.wait_ge(state_done, KT)
            pool.memset(b_out, 0.0).then_inc(pool_set, 1)
            pool.wait_ge(h2_done, TT)
            pool.memset(z_q[:, 1024:1792], 0.0).then_inc(zero_set, 1)
            pool.wait_ge(zero_set, 1)
            pool.wait_ge(moe_loaded, 16 * 3)
            for c in range(2):
                ins = pool.tensor_copy(o_sb[64 * c:64 * c + EXPERTS, :], b_e2[64 * c:64 * c + EXPERTS, :])
            ins.then_inc(o_done, 1)


_INS = ["x", "c", "positions", "w_ada", "b_ada", "g_pre_mix", "g_post_mix", "w_in", "b_in", "sinks", "conv_w", "conv_b",
        "w_rg", "b_rg", "w_ig", "b_ig", "lru_a", "w_out", "b_out", "g_pre_ffn", "g_post_ffn", "w_router", "b_router",
        "w_e1", "b_e1", "w_e2", "b_e2"]


def kernel(**inputs):
    import concourse.bacc as _bacc
    from concourse.bass_utils import run_bass_kernel_spmd as _run

    nc = _bacc.Bacc("TRN2", target_bir_lowering=False, num_devices=1)
    arrays, aps = {}, {}
    for name in _INS:
        arrays[f"in_{name}"] = np.ascontiguousarray(inputs[name])
    freqs = ROPE_THETA ** (-np.arange(0, HEAD_DIM, 2) / HEAD_DIM)
    arrays["in_inv_freq"] = np.tile(freqs.astype(np.float32), P // HALF).reshape(P, 1)
    for name, v in arrays.items():
        aps[name[3:]] = nc.dram_tensor(name, v.shape, mybir.dt.from_np(v.dtype), kind="ExternalInput").ap()
    out = nc.dram_tensor("out_0", (1, T, D), F32, kind="ExternalOutput").ap()
    layer(nc, aps, out)
    r = _run(nc, [arrays], core_ids=[0])
    return r.results[0]["out_0"]
```
